# Optimizing a Trainium2 kernel written in Bass

```python
import jax, jax.numpy as jnp
from jax import lax
import numpy as np

D_MODEL = 1024
BATCH = 1
SEQ = 512
DEPTH = 1

MEM_LEN = 256
EPS = 1e-6

GLA_HEADS = 4
GLA_DV = D_MODEL // (2 * GLA_HEADS)
GLA_DK = GLA_DV // 2
GLA_LOWRANK = 16
GLA_GATE_NORM = 16.0
GLA_CHUNK = 64
CONV_WIDTH = 4
SB_HEADS = 8
SB_DH = D_MODEL // (2 * SB_HEADS)
SB_BLOCK = 128

GLA_QK_W = GLA_HEADS * GLA_DK
GLA_V_W = GLA_HEADS * GLA_DV
SB_W = SB_HEADS * SB_DH
MIX_W = GLA_V_W + SB_W
CONV_W = 2 * GLA_QK_W + GLA_V_W
IN_COLS = CONV_W + GLA_V_W + GLA_LOWRANK + 3 * SB_W

X_HEADS = 4
X_DH = D_MODEL // X_HEADS

PEER_HEADS = 8
PEER_NKEYS = 128
PEER_N = PEER_NKEYS * PEER_NKEYS
PEER_DKEY = 256
PEER_TOPK = 16
PEER_TOKEN_BLOCK = 128

kernel_name = "hybrid_gla_stickbreak_peer_block"

def rms_norm(x, g):
    xf = x.astype(jnp.float32)
    y = xf * lax.rsqrt(jnp.mean(xf * xf, axis=-1, keepdims=True) + EPS)
    return (y * g.astype(jnp.float32)).astype(x.dtype)

def split_heads(a, n_heads):
    b, t, w = a.shape
    return a.reshape(b, t, n_heads, w // n_heads).transpose(0, 2, 1, 3)

def merge_heads(a):
    b, h, t, d = a.shape
    return a.transpose(0, 2, 1, 3).reshape(b, t, h * d)

def causal_short_conv(x, w):
    kw = w.shape[0]
    t = x.shape[1]
    xp = jnp.pad(x, ((0, 0), (kw - 1, 0), (0, 0)))
    y = sum(xp[:, k:k + t] * w[k] for k in range(kw))
    return jax.nn.silu(y)

def gla_chunked(q, k, v, log_decay):
    dtype = v.dtype
    b, h, t, dk = q.shape
    dv = v.shape[-1]
    c = GLA_CHUNK
    n = t // c

    def to_chunks(a):
        return a.astype(jnp.float32).reshape(b, h, n, c, a.shape[-1]).transpose(2, 0, 1, 3, 4)

    qc, kc, vc, gc = map(to_chunks, (q * dk ** -0.5, k, v, log_decay))
    causal = jnp.tril(jnp.ones((c, c), dtype=bool))

    def step(state, inp):
        qi, ki, vi, gi = inp
        cum = jnp.cumsum(gi, axis=2)
        cum_last = cum[:, :, -1, :]
        o_inter = jnp.einsum('bhcd,bhde->bhce', qi * jnp.exp(cum), state)
        diff = cum[:, :, :, None, :] - cum[:, :, None, :, :]
        decay = jnp.exp(jnp.where(causal[:, :, None], diff, -jnp.inf))
        scores = jnp.einsum('bhid,bhjd,bhijd->bhij', qi, ki, decay)
        o_intra = jnp.einsum('bhij,bhje->bhie', scores, vi)
        k_dec = ki * jnp.exp(cum_last[:, :, None, :] - cum)
        new_state = jnp.exp(cum_last)[..., None] * state + jnp.einsum('bhcd,bhce->bhde', k_dec, vi)
        return new_state, o_inter + o_intra

    s0 = jnp.zeros((b, h, dk, dv), jnp.float32)
    _, out = lax.scan(step, s0, (qc, kc, vc, gc))
    return out.transpose(1, 2, 0, 3, 4).reshape(b, h, t, dv).astype(dtype)

def stick_breaking_attention(q, k, v):
    b, h, t, d = q.shape
    scale = d ** -0.5
    outs = []
    for blk in range(t // SB_BLOCK):
        t0 = blk * SB_BLOCK
        t1 = t0 + SB_BLOCK
        qb, kb, vb = q[:, :, t0:t1], k[:, :, :t1], v[:, :, :t1]
        z = jnp.einsum('bhtd,bhsd->bhts', qb, kb).astype(jnp.float32) * scale
        strict = jnp.arange(t1)[None, :] < jnp.arange(t0, t1)[:, None]
        log_beta = jax.nn.log_sigmoid(z)
        log_one_minus = jnp.where(strict, jax.nn.log_sigmoid(-z), 0.0)
        tail = lax.cumsum(log_one_minus, axis=3, reverse=True) - log_one_minus
        weights = jnp.where(strict, jnp.exp(log_beta + tail), 0.0)
        outs.append(jnp.einsum('bhts,bhsd->bhtd', weights.astype(vb.dtype), vb))
    return jnp.concatenate(outs, axis=2)

def memory_cross_attention(hn, mn, w_q, w_kv, w_o):
    b, t, _ = hn.shape
    m = mn.shape[1]
    q = (hn @ w_q).reshape(b, t, X_HEADS, X_DH)
    k, v = jnp.split(mn @ w_kv, 2, axis=-1)
    k = k.reshape(b, m, X_HEADS, X_DH)
    v = v.reshape(b, m, X_HEADS, X_DH)
    s = jnp.einsum('bthd,bmhd->bhtm', q, k).astype(jnp.float32) * X_DH ** -0.5
    p = jax.nn.softmax(s, axis=-1).astype(v.dtype)
    o = jnp.einsum('bhtm,bmhd->bthd', p, v).reshape(b, t, X_HEADS * X_DH)
    return o @ w_o

def peer_ffn(xn, w_q, sub_keys, u, v):
    b, t, d = xn.shape
    q = (xn @ w_q).reshape(b, t, PEER_HEADS, 2, PEER_DKEY // 2)
    s = jnp.einsum('bthpk,hpnk->bthpn', q, sub_keys).astype(jnp.float32)
    top_s, top_i = lax.top_k(s, PEER_TOPK)
    cand_s = top_s[..., 0, :, None] + top_s[..., 1, None, :]
    cand_i = top_i[..., 0, :, None] * PEER_NKEYS + top_i[..., 1, None, :]
    cand_s = cand_s.reshape(b, t, PEER_HEADS, PEER_TOPK * PEER_TOPK)
    cand_i = cand_i.reshape(b, t, PEER_HEADS, PEER_TOPK * PEER_TOPK)
    best_s, best_pos = lax.top_k(cand_s, PEER_TOPK)
    expert_idx = jnp.take_along_axis(cand_i, best_pos, axis=-1)
    gates = jax.nn.softmax(best_s, axis=-1).astype(xn.dtype)

    hk = PEER_HEADS * PEER_TOPK
    n_blk = (b * t) // PEER_TOKEN_BLOCK
    xf = xn.reshape(n_blk, PEER_TOKEN_BLOCK, d)
    idx = expert_idx.reshape(n_blk, PEER_TOKEN_BLOCK, hk)
    gf = gates.reshape(n_blk, PEER_TOKEN_BLOCK, hk)

    def block(args):
        xb, ib, gb = args
        act = jax.nn.gelu(jnp.einsum('td,ted->te', xb, u[ib]))
        return jnp.einsum('te,ted->td', gb * act, v[ib])

    out = lax.map(block, (xf, idx, gf))
    return out.reshape(b, t, d)

def setup_inputs(seed: int = 0) -> dict:
    key = jax.random.key(seed)
    ks = jax.random.split(key, 21)
    f32 = jnp.float32

    def nrm(k, shape, scale):
        return jax.random.normal(k, shape, f32) * scale

    def gain(k, shape):
        return 1.0 + 0.02 * jax.random.normal(k, shape, f32)

    return {
        "x": nrm(ks[0], (BATCH, SEQ, D_MODEL), 1.0),
        "mem": nrm(ks[1], (BATCH, MEM_LEN, D_MODEL), 1.0),
        "mix_norm_g": gain(ks[2], (DEPTH, D_MODEL)),
        "w_in": nrm(ks[3], (DEPTH, D_MODEL, IN_COLS), D_MODEL ** -0.5),
        "gla_conv_w": nrm(ks[4], (DEPTH, CONV_WIDTH, CONV_W), CONV_WIDTH ** -0.5),
        "gla_gate_w": nrm(ks[5], (DEPTH, GLA_LOWRANK, GLA_QK_W), GLA_LOWRANK ** -0.5),
        "gla_gate_b": nrm(ks[6], (DEPTH, GLA_QK_W), 0.1),
        "gla_out_norm_g": gain(ks[7], (DEPTH, GLA_DV)),
        "sb_out_norm_g": gain(ks[8], (DEPTH, SB_W)),
        "w_out": nrm(ks[9], (DEPTH, MIX_W, D_MODEL), MIX_W ** -0.5),
        "xattn_norm_g": gain(ks[10], (DEPTH, D_MODEL)),
        "mem_norm_g": gain(ks[11], (DEPTH, D_MODEL)),
        "w_xq": nrm(ks[12], (DEPTH, D_MODEL, X_HEADS * X_DH), D_MODEL ** -0.5),
        "w_xkv": nrm(ks[13], (DEPTH, D_MODEL, 2 * X_HEADS * X_DH), D_MODEL ** -0.5),
        "w_xo": nrm(ks[14], (DEPTH, X_HEADS * X_DH, D_MODEL), (X_HEADS * X_DH) ** -0.5),
        "ffn_norm_g": gain(ks[15], (DEPTH, D_MODEL)),
        "peer_w_q": nrm(ks[16], (DEPTH, D_MODEL, PEER_HEADS * PEER_DKEY), D_MODEL ** -0.5),
        "peer_sub_keys": nrm(ks[17], (DEPTH, PEER_HEADS, 2, PEER_NKEYS, PEER_DKEY // 2), (PEER_DKEY // 2) ** -0.5),
        "peer_u": nrm(ks[18], (DEPTH, PEER_N, D_MODEL), D_MODEL ** -0.5),
        "peer_v": nrm(ks[19], (DEPTH, PEER_N, D_MODEL), PEER_HEADS ** -0.5),
        "final_norm_g": gain(ks[20], (D_MODEL,)),
    }

def reference(x, mem, mix_norm_g, w_in, gla_conv_w, gla_gate_w, gla_gate_b, gla_out_norm_g,
              sb_out_norm_g, w_out, xattn_norm_g, mem_norm_g, w_xq, w_xkv, w_xo, ffn_norm_g,
              peer_w_q, peer_sub_keys, peer_u, peer_v, final_norm_g):
    h = x
    c1 = CONV_W
    c2 = c1 + GLA_V_W
    c3 = c2 + GLA_LOWRANK
    c4 = c3 + SB_W
    c5 = c4 + SB_W
    for l in range(DEPTH):
        xn = rms_norm(h, mix_norm_g[l])
        proj = xn @ w_in[l]
        gla_qkv, gla_og, gla_low, sb_q, sb_k, sb_v = jnp.split(proj, [c1, c2, c3, c4, c5], axis=-1)

        gla_qkv = causal_short_conv(gla_qkv, gla_conv_w[l])
        g_q, g_k, g_v = jnp.split(gla_qkv, [GLA_QK_W, 2 * GLA_QK_W], axis=-1)
        log_decay = jax.nn.log_sigmoid((gla_low @ gla_gate_w[l] + gla_gate_b[l]).astype(jnp.float32)) / GLA_GATE_NORM
        o_gla = gla_chunked(split_heads(g_q, GLA_HEADS), split_heads(g_k, GLA_HEADS),
                            split_heads(g_v, GLA_HEADS), split_heads(log_decay, GLA_HEADS))
        o_gla = merge_heads(rms_norm(o_gla, gla_out_norm_g[l])) * jax.nn.silu(gla_og)

        o_sb = stick_breaking_attention(split_heads(sb_q, SB_HEADS), split_heads(sb_k, SB_HEADS),
                                        split_heads(sb_v, SB_HEADS))
        o_sb = rms_norm(merge_heads(o_sb), sb_out_norm_g[l])

        h = h + jnp.concatenate([o_gla, o_sb], axis=-1) @ w_out[l]

        h = h + memory_cross_attention(rms_norm(h, xattn_norm_g[l]), rms_norm(mem, mem_norm_g[l]),
                                       w_xq[l], w_xkv[l], w_xo[l])

        h = h + peer_ffn(rms_norm(h, ffn_norm_g[l]), peer_w_q[l], peer_sub_keys[l], peer_u[l], peer_v[l])
    return rms_norm(h, final_norm_g)


_drawn_inputs = setup_inputs


def setup_inputs(seed=0):
    import zlib

    import numpy as np

    out = dict(_drawn_inputs(seed))
    spreads = {}
    factors = {'gla_gate_b': 4.031,
     'gla_out_norm_g': 4.199,
     'sb_out_norm_g': 3.213,
     'xattn_norm_g': 8.0,
     'mem_norm_g': 7.178,
     'ffn_norm_g': 21.274,
     'final_norm_g': 8.721}
    for name, (base, spread) in spreads.items():
        noise = np.random.default_rng([zlib.crc32(name.encode()), seed]).standard_normal(out[name].shape)
        drawn = base * np.exp(spread * noise) if base else spread * noise
        out[name] = __import__('jax').numpy.asarray(drawn.astype(out[name].dtype))
    for name, factor in factors.items():
        out[name] = (out[name] * factor).astype(out[name].dtype)
    return out
```

```python
from contextlib import ExitStack

import numpy as np
import concourse.bass as bass
from concourse import mybir

F32 = mybir.dt.float32
F32R = mybir.dt.float32r
U32 = mybir.dt.uint32
ALU = mybir.AluOpType
ACT = mybir.ActivationFunctionType
AX = mybir.AxisListType

P = 128
D = 1024
DC = D // P
T = 512
TB = T // P
M = 256
MB = M // P
EPS = 1e-6

GH, GDK, GDV, LOWRANK = 4, 64, 128, 16
GATE_NORM = 16.0
CONV = 4
CONV_BLOCKS = (2 * GH * GDK + GH * GDV) // P
SH, SD = 8, 64
XH, XD = 4, 256
PH, NKEYS, TOPK = 8, 128, 16
HP = 2 * PH
SLOTS = PH * TOPK
HALF = T // 2
NEG = -3.0e38

LEVELS = [64, 32, 16, 8, 4, 2, 1]

Q_CONV, Q_OG, Q_SBQ, Q_SBK, Q_SBV, Q_OUT, Q_XQ, Q_XK, Q_XV, Q_XO, Q_PQ = 0, 2, 3, 4, 5, 6, 8, 10, 12, 14, 16
NQUADS = 20
QRING = 2

V_MIX, V_XA, V_MEM, V_FFN, V_CONV, V_GATEB, V_GLAG, V_SBG = 0, 8, 16, 24, 32, 64, 66, 67
NVEC = 71

C_ID, C_ONES, C_TRI, C_IOTA16 = 0, 128, 256, 384
NCONST = 400

SOFF = [0, 512, 896, 1152]
SLEN = [512, 384, 256, 128]
STOT = 1280


class Counts:

    def __init__(self):
        self.full = 0
        self.act = 0
        self.dve = 0
        self.chain = {}


class Groups:

    def __init__(self, counts, plan, banks=8):
        self.banks, self.at, self.value, self.who = banks, {}, [], []
        self.base = counts.full
        for n, (name, who) in enumerate(plan):
            assert name not in self.at
            self.at[name] = n
            if who == "act":
                counts.act += 1
                self.value.append(counts.act)
            else:
                counts.dve += 1
                self.value.append(counts.dve)
            self.who.append(who)
        counts.full += len(plan)

    def bank(self, name):
        return self.at[name] % self.banks

    def full(self, name):
        return self.base + self.at[name] + 1

    def read(self, name):
        n = self.at[name]
        return self.who[n], self.value[n]

    def before(self, name):
        n = self.at[name] - self.banks
        return None if n < 0 else (self.who[n], self.value[n])


def layer(nc, A, out):
    top = ExitStack()

    def sem(name):
        return top.enter_context(nc.semaphore(name))

    def sb(stack, name, shape, dt=F32):
        return stack.enter_context(nc.sbuf_tensor(name, shape, dt))

    psum_full = sem("psum_full")
    act_evac = sem("act_evac")
    dve_evac = sem("dve_evac")
    evac = {"act": act_evac, "dve": dve_evac}
    act_chain, dve_chain, pool_chain = sem("act_chain"), sem("dve_chain"), sem("pool_chain")
    quad_loaded = [sem(f"quad_loaded{s}") for s in range(QRING)]
    small_loaded = sem("small_loaded")
    stored = sem("stored")
    C = Counts()
    loads = [0]
    steps = {"act": 0, "dve": 0, "pool": 0}
    chains = {"act": act_chain, "dve": dve_chain, "pool": pool_chain}

    def link(eng, who, ins):
        steps[who] += 1
        ins.then_inc(chains[who], 1)
        eng.wait_ge(chains[who], steps[who])

    psum = [top.enter_context(nc.psum_tensor(f"bank{b}", [P, 512], F32)) for b in range(8)]
    iota_t = sb(top, "iota", [P, P])
    slot_t = sb(top, "slot_t", [P, 3, T])
    main = ExitStack()
    const = sb(main, "const", [P, NCONST])
    vec = sb(main, "vec", [P, NVEC])
    act_t = sb(main, "act_t", [P, DC, T])
    ident = const[:, C_ID:C_ID + P]
    ones = const[:, C_ONES:C_ONES + P]
    tri = const[:, C_TRI:C_TRI + P]
    iota = iota_t[:]
    iota16 = const[:, C_IOTA16:C_IOTA16 + TOPK]
    h_scratch = nc.dram_tensor("h_scratch", [P, TB, D], F32, kind="Internal").ap()

    xf_scratch = nc.dram_tensor("xf_scratch", [P, 2, DC, HALF], F32, kind="Internal").ap()
    h = sb(main, "h", [P, TB, D])
    ring = sb(main, "ring", [P, QRING * 4, DC, P])
    quad_last = {}

    def load_quad(sp, q):
        if q >= NQUADS:
            return
        if q >= QRING:
            sp.wait_ge(psum_full, quad_last[q - QRING])
        s = q % QRING
        sp.dma_start(ring[:, 4 * s:4 * s + 4], A["w_tiles"][:, 4 * q:4 * q + 4]).then_inc(quad_loaded[s], 16)

    def quad(pe, q):
        pe.wait_ge(quad_loaded[q % QRING], 16 * (q // QRING + 1))
        return 4 * (q % QRING)

    def prefetch(sp, a, b):
        for q in range(a, b):
            load_quad(sp, q + QRING)

    def opened(pe, g, name):
        old = g.before(name)
        if old:
            pe.wait_ge(evac[old[0]], old[1])
        return psum[g.bank(name)]

    def wait_read(eng, g, name):
        who, value = g.read(name)
        eng.wait_ge(evac[who], value)

    with nc.Block() as block:
        @block.sync
        def _(sp):
            sp.dma_start(h[:], A["x"]).then_inc(small_loaded, 16)
            sp.dma_start(const[:], A["const"]).then_inc(small_loaded, 16)
            sp.dma_start(iota_t[:], A["iota"]).then_inc(small_loaded, 16)
            sp.dma_start(vec[:], A["vec"]).then_inc(small_loaded, 16)
            for q in range(QRING):
                load_quad(sp, q)
            sp.wait_ge(small_loaded, 64)
    loads[0] = 64

    def norm_transpose(name, src, nt, width, gain_at, dst, chunk0=0):
        nc_chunks = width // P
        stack = ExitStack()
        sq = sb(stack, name + "_sq", [P, width])
        stat = sb(stack, name + "_stat", [P, 5, nt])
        xs = sb(stack, name + "_xs", [P, nt, width])
        a_sum, a_sqrt, d_scaled = sem(name + "_sum"), sem(name + "_sqrt"), sem(name + "_scaled")
        plan = [((t, c), "dve") for t in range(nt) for c in range(0, nc_chunks, 4)]
        g = Groups(C, plan)
        with nc.Block() as block:
            @block.scalar
            def _(act):
                for t in range(nt):
                    nc.scalar.activation(sq[:], src[:, t, :], ACT.Square,
                                         accum_out=stat[:, 0, t:t + 1]).then_inc(a_sum, 1)
                    act.wait_ge(a_sum, t + 1)
                act.wait_ge(a_sum, nt + 1)
                nc.scalar.activation(stat[:, 2, :], stat[:, 1, :], ACT.Sqrt).then_inc(a_sqrt, 1)

            @block.vector
            def _(dve):
                dve.wait_ge(a_sum, nt)
                nc.vector.tensor_scalar(stat[:, 1, :], stat[:, 0, :], 1.0 / width, EPS, ALU.mult,
                                        ALU.add).then_inc(a_sum, 1)
                dve.wait_ge(a_sqrt, 1)
                link(dve, "dve", nc.vector.reciprocal(stat[:, 2, :], stat[:, 2, :]))
                link(dve, "dve", nc.vector.tensor_tensor(stat[:, 3, :], stat[:, 2, :], stat[:, 2, :], ALU.mult))
                link(dve, "dve", nc.vector.tensor_tensor(stat[:, 3, :], stat[:, 3, :], stat[:, 1, :], ALU.mult))
                link(dve, "dve", nc.vector.tensor_scalar(stat[:, 3, :], stat[:, 3, :], -0.5, 1.5, ALU.mult, ALU.add))
                link(dve, "dve", nc.vector.tensor_tensor(stat[:, 4, :], stat[:, 3, :], stat[:, 2, :], ALU.mult))

                def scale(t):
                    nc.vector.tensor_scalar(xs[:, t, :], src[:, t, :], stat[:, 4, t:t + 1], None,
                                            ALU.mult).then_inc(d_scaled, 1)
                scale(0)
                for t in range(nt):
                    if t + 1 < nt:
                        scale(t + 1)
                    for c in range(0, nc_chunks, 4):
                        dve.wait_ge(psum_full, g.full((t, c)))
                        gain = vec[:, gain_at + c:gain_at + c + 4].unsqueeze(2).to_broadcast([P, 4, P])
                        nc.vector.tensor_tensor(
                            dst[:, chunk0 + c:chunk0 + c + 4, t * P:(t + 1) * P],
                            psum[g.bank((t, c))][:].rearrange("p (c t) -> p c t", c=4), gain,
                            ALU.mult).then_inc(dve_evac, 1)

            @block.tensor
            def _(pe):
                for t in range(nt):
                    pe.wait_ge(d_scaled, t + 1)
                    for c in range(0, nc_chunks, 4):
                        bank = opened(pe, g, (t, c))
                        for k in range(4):
                            last = nc.tensor.transpose(bank[:, k * P:(k + 1) * P],
                                                       xs[:, t, (c + k) * P:(c + k + 1) * P], ident)
                        last.then_inc(psum_full, 1)
        stack.close()

    def projected(pe, g, name, cols, rhs, n):
        bank = opened(pe, g, name)
        for c in range(DC):
            last = nc.tensor.matmul(bank[:, 0:n], ring[:, cols, c, :], rhs(c), start=(c == 0), stop=(c == DC - 1))
        last.then_inc(psum_full, 1)

    def projected_natural(pe, g, name, slot, src, t):
        bank = opened(pe, g, name)
        for c in range(DC):
            last = nc.tensor.matmul(bank[:], src[:, c, t * P:(t + 1) * P], ring[:, slot:slot + 4, c, :],
                                    start=(c == 0), stop=(c == DC - 1))
        last.then_inc(psum_full, 1)

    norm_transpose("nx", h, TB, D, V_MIX, act_t)

    mixer = ExitStack()
    qkv = sb(mixer, "qkv", [P, CONV_BLOCKS, T])
    zg = sb(mixer, "zg", [P, 2, T])
    og = sb(mixer, "og", [P, TB, GH * GDV])
    s_q = sb(mixer, "s_q", [P, SH // 2, T])
    s_k = sb(mixer, "s_k", [P, SH // 2, T])
    s_v = sb(mixer, "s_v", [P, TB, SH * SD])
    stage = ExitStack()
    w_low = sb(stage, "w_low", [P, DC, LOWRANK])
    gate_w = sb(stage, "gate_w", [LOWRANK, 2 * P])
    low = sb(stage, "low", [LOWRANK, T])
    conv = sb(stage, "conv", [P, 2, T])
    conv_done, conv_silu = sem("conv_done"), sem("conv_silu")
    plan = [("low", "act"), ("gate0", "act"), ("gate1", "act")]
    plan = [(("conv", n), "dve") for n in range(CONV_BLOCKS)] + plan
    plan += [(("og", t), "act") for t in range(TB)]
    plan += [(("sq", n), "act") for n in range(4)] + [(("sk", n), "dve") for n in range(4)]
    plan += [(("sv", t), "dve") for t in range(TB)]
    g = Groups(C, plan)
    for q in range(2):
        quad_last[Q_CONV + q] = g.full(("conv", 4 * q + 3))
    quad_last[Q_OG], quad_last[Q_SBQ] = g.full(("og", 3)), g.full(("sq", 3))
    quad_last[Q_SBK], quad_last[Q_SBV] = g.full(("sk", 3)), g.full(("sv", 3))
    with nc.Block() as block:
        @block.sync
        def _(sp):
            sp.dma_start(w_low[:], A["w_low"]).then_inc(small_loaded, 16)
            sp.dma_start(gate_w[:], A["gate_w"]).then_inc(small_loaded, 16)
            prefetch(sp, Q_CONV, Q_OUT)

        @block.tensor
        def _(pe):
            for q in range(2):
                s = quad(pe, Q_CONV + q)
                for n in range(4):
                    projected(pe, g, ("conv", 4 * q + n), s + n, lambda c: act_t[:, c, :], T)
            pe.wait_ge(small_loaded, loads[0] + 32)
            bank = opened(pe, g, "low")
            for c in range(DC):
                last = nc.tensor.matmul(bank[0:LOWRANK, :], w_low[:, c, :], act_t[:, c, :],
                                        start=(c == 0), stop=(c == DC - 1))
            last.then_inc(psum_full, 1)
            wait_read(pe, g, "low")
            for n in range(2):
                bank = opened(pe, g, f"gate{n}")
                nc.tensor.matmul(bank[:], gate_w[:, n * P:(n + 1) * P], low[:], start=True,
                                 stop=True).then_inc(psum_full, 1)
            s = quad(pe, Q_OG)
            for t in range(TB):
                projected_natural(pe, g, ("og", t), s, act_t, t)
            for q, name in ((Q_SBQ, "sq"), (Q_SBK, "sk")):
                s = quad(pe, q)
                for n in range(4):
                    projected(pe, g, (name, n), s + n, lambda c: act_t[:, c, :], T)
            s = quad(pe, Q_SBV)
            for t in range(TB):
                projected_natural(pe, g, ("sv", t), s, act_t, t)

        @block.vector
        def _(dve):
            for n in range(CONV_BLOCKS):
                w = lambda k: vec[:, V_CONV + n * CONV + k:V_CONV + n * CONV + k + 1]
                y, x = conv[:, n % 2, :], psum[g.bank(("conv", n))]
                if n >= 2:
                    dve.wait_ge(conv_silu, n - 1)
                dve.wait_ge(psum_full, g.full(("conv", n)))
                link(dve, "dve", nc.vector.tensor_scalar(y, x[:], w(CONV - 1), None, ALU.mult))
                for back in range(1, CONV - 1):
                    link(dve, "dve", nc.vector.scalar_tensor_tensor(
                        out=y[:, back:], in0=x[:, 0:T - back], scalar=w(CONV - 1 - back), in1=y[:, back:],
                        op0=ALU.mult, op1=ALU.add))
                back = CONV - 1
                nc.vector.scalar_tensor_tensor(out=y[:, back:], in0=x[:, 0:T - back], scalar=w(0), in1=y[:, back:],
                                               op0=ALU.mult, op1=ALU.add).then_inc(dve_evac, 1)
            for n in range(4):
                dve.wait_ge(psum_full, g.full(("sk", n)))
                nc.vector.tensor_copy(s_k[:, n, :], psum[g.bank(("sk", n))][:]).then_inc(dve_evac, 1)
            for t in range(TB):
                dve.wait_ge(psum_full, g.full(("sv", t)))
                nc.vector.tensor_copy(s_v[:, t, :], psum[g.bank(("sv", t))][:]).then_inc(dve_evac, 1)

        @block.scalar
        def _(act):
            for n in range(CONV_BLOCKS):
                wait_read(act, g, ("conv", n))
                nc.scalar.activation(qkv[:, n, :], conv[:, n % 2, :], ACT.Silu).then_inc(conv_silu, 1)
            act.wait_ge(psum_full, g.full("low"))
            nc.scalar.activation(low[:], psum[g.bank("low")][0:LOWRANK, :], ACT.Identity).then_inc(act_evac, 1)
            for n in range(2):
                act.wait_ge(psum_full, g.full(f"gate{n}"))
                nc.scalar.activation(zg[:, n, :], psum[g.bank(f"gate{n}")][:], ACT.Identity,
                                     bias=vec[:, V_GATEB + n:V_GATEB + n + 1]).then_inc(act_evac, 1)
            for t in range(TB):
                act.wait_ge(psum_full, g.full(("og", t)))
                nc.scalar.activation(og[:, t, :], psum[g.bank(("og", t))][:], ACT.Silu).then_inc(act_evac, 1)
            for n in range(4):
                act.wait_ge(psum_full, g.full(("sq", n)))
                nc.scalar.activation(s_q[:, n, :], psum[g.bank(("sq", n))][:], ACT.Identity,
                                     scale=float(SD) ** -0.5).then_inc(act_evac, 1)
    loads[0] += 32
    stage.close()

    stage = ExitStack()
    masks = sb(stage, "masks", [P, len(LEVELS) + 1, P], U32)
    cum = sb(stage, "cum", [P, 2, TB, P])
    lv_e = sb(stage, "lv_e", [P, 2, 2 * T])
    lv_q = sb(stage, "lv_q", [P, 2, 2, T])
    lv_k = sb(stage, "lv_k", [P, 2, 2, T])
    q_s = sb(stage, "q_s", [P, 2, T])
    q_in = sb(stage, "q_in", [P, 2, T])
    k_dec = sb(stage, "k_dec", [P, 2, T])
    k_nat = sb(stage, "k_nat", [P, 2, TB, P])
    dec = sb(stage, "dec", [P, 2, TB])
    v_nat = sb(stage, "v_nat", [P, TB, GH * GDV])
    scores = sb(stage, "scores", [P, GH, TB, P])
    state = sb(stage, "state", [P, 2, 2, GDV])
    o_gla = sb(stage, "o_gla", [P, TB, GH * GDV])
    gst = sb(stage, "gst", [P, 5, TB * GH])
    tmp = lv_e[:].rearrange("p a b -> p (a b)")
    NL = len(LEVELS)
    names = ["gl_mask", "gl_abs", "gl_ln", "gl_cum", "gl_diff", "gl_exp", "gl_fac", "gl_qin", "gl_kdiff",
             "gl_kexp", "gl_kdec", "gl_sq", "gl_var", "gl_sqrt", "gl_on", "gl_clear", "gl_qs", "gl_decay", "gl_scored"]
    S = {n: sem(n) for n in names}
    plan = [(("vt", x), "act") for x in range(GH)]
    plan += [(("lv", 0, x), "dve") for x in range(GH)]
    plan += [(("kt", x), "act") for x in range(2)]
    plan += [(("lv", l, x), "dve") for l in range(1, NL + 1) for x in range(GH)]
    for t in range(TB):
        plan += [(("o", t, y), "act") for y in range(2)]
        if t < TB - 1:
            plan += [(("st", t), "dve")]
    plan += [(("gt", x), "act") for x in range(GH)]
    g = Groups(C, plan)
    with nc.Block() as block:
        @block.sync
        def _(sp):
            sp.dma_start(masks[:], A["masks"]).then_inc(small_loaded, 16)

        @block.scalar
        def _(act):
            z = zg[:].rearrange("p a b -> p (a b)")
            z2 = lv_q[:, 0].rearrange("p a b -> p (a b)")
            link(act, "act", nc.scalar.activation(z2, z, ACT.Abs))
            link(act, "act", nc.scalar.activation(z2, z2, ACT.Exp, scale=-1.0))
            nc.scalar.activation(z2, z2, ACT.Ln, bias=1.0).then_inc(S["gl_ln"], 1)
            act.wait_ge(S["gl_cum"], 1)
            cf = cum[:].rearrange("p a b c -> p (a b c)")
            nc.scalar.activation(tmp[:, 0:2 * T], cf, ACT.Exp).then_inc(S["gl_exp"], 1)
            nc.scalar.activation(dec[:], cum[:, :, :, P - 1], ACT.Exp).then_inc(S["gl_decay"], 1)
            act.wait_ge(S["gl_kdiff"], 1)
            nc.scalar.activation(tmp[:, 2 * T:4 * T], tmp[:, 2 * T:4 * T], ACT.Exp, scale=-1.0).then_inc(S["gl_kexp"], 1)
            for x in range(GH):
                act.wait_ge(psum_full, g.full(("vt", x)))
                nc.scalar.activation(v_nat[:, :, x * GDV:(x + 1) * GDV],
                                     psum[g.bank(("vt", x))][:].rearrange("p (t d) -> p t d", t=TB),
                                     ACT.Identity).then_inc(act_evac, 1)
            for x in range(2):
                act.wait_ge(psum_full, g.full(("kt", x)))
                nc.scalar.activation(k_nat[:, x], psum[g.bank(("kt", x))][:].rearrange("p (t d) -> p t d", t=TB),
                                     ACT.Identity).then_inc(act_evac, 1)
            for l in range(NL):
                act.wait_ge(S["gl_diff"], l + 1)
                nc.scalar.activation(lv_e[:, l % 2], lv_e[:, l % 2], ACT.Exp).then_inc(S["gl_exp"], 1)
            for t in range(TB):
                for y in range(2):
                    act.wait_ge(psum_full, g.full(("o", t, y)))
                    nc.scalar.activation(o_gla[:, t, :].rearrange("p (x y d) -> p x y d", y=2, d=GDV)[:, :, y, :],
                                         psum[g.bank(("o", t, y))][:, 0:2 * GDV].rearrange("p (x d) -> p x d", x=2),
                                         ACT.Identity).then_inc(act_evac, 1)
            wait_read(act, g, ("o", TB - 1, 1))
            act.wait_ge(S["gl_fac"], 2 * NL)
            nc.scalar.activation(tmp[:, 0:4 * T], o_gla[:].rearrange("p a b -> p (a b)"),
                                 ACT.Square).then_inc(S["gl_sq"], 1)
            act.wait_ge(S["gl_var"], 1)
            nc.scalar.activation(gst[:, 2, :], gst[:, 1, :], ACT.Sqrt).then_inc(S["gl_sqrt"], 1)
            for x in range(GH):
                act.wait_ge(psum_full, g.full(("gt", x)))
                nc.scalar.activation(act_t[:, x, :], psum[g.bank(("gt", x))][:], ACT.Identity,
                                     scale=vec[:, V_GLAG:V_GLAG + 1]).then_inc(act_evac, 1)

        @block.vector
        def _(dve):
            link(dve, "dve", nc.vector.memset(lv_k[:], 0.0))
            nc.vector.memset(lv_q[:, 1], 0.0)
            nc.vector.memset(scores[:], 0.0).then_inc(S["gl_clear"], 1)
            nc.vector.tensor_scalar(q_s[:], qkv[:, 0:2, :], float(GDK) ** -0.5, None, ALU.mult).then_inc(S["gl_qs"], 1)
            dve.wait_ge(S["gl_ln"], 1)
            zf = zg[:].rearrange("p a b -> p (a b)")
            z2 = lv_q[:, 0].rearrange("p a b -> p (a b)")
            link(dve, "dve", nc.vector.scalar_tensor_tensor(out=zf, in0=zf, scalar=0.0, in1=z2,
                                                            op0=ALU.min, op1=ALU.subtract))
            link(dve, "dve", nc.vector.tensor_scalar(zf, zf, 1.0 / GATE_NORM, None, ALU.mult))
            nc.vector.memset(lv_q[:, 0], 0.0)
            for x in range(2):
                for t in range(TB):
                    last = nc.vector.tensor_tensor_scan(cum[:, x, t, :], ones, zg[:, x, t * P:(t + 1) * P], 0.0,
                                                        ALU.mult, ALU.add)
            last.then_inc(S["gl_cum"], 1)
            dve.wait_ge(S["gl_cum"], 1)
            cb = cum[:].rearrange("p a b c -> p (a b) c")
            nc.vector.tensor_tensor(tmp[:, 2 * T:4 * T].rearrange("p (a c) -> p a c", c=P), cb,
                                    cb[:, :, P - 1:P].to_broadcast([P, 2 * TB, P]),
                                    ALU.subtract).then_inc(S["gl_kdiff"], 1)
            qf = lambda a: a.rearrange("p a b -> p (a b)")
            dve.wait_ge(S["gl_exp"], 1)
            dve.wait_ge(S["gl_qs"], 1)
            nc.vector.tensor_tensor(qf(q_in[:]), qf(q_s[:]), tmp[:, 0:2 * T], ALU.mult).then_inc(S["gl_qin"], 1)
            dve.wait_ge(S["gl_kexp"], 1)
            nc.vector.tensor_tensor(qf(k_dec[:]), qf(qkv[:, 2:4, :]), tmp[:, 2 * T:4 * T],
                                    ALU.mult).then_inc(S["gl_kdec"], 1)
            dve.wait_ge(S["gl_kdec"], 1)
            dve.wait_ge(S["gl_qin"], 1)
            dve.wait_ge(small_loaded, loads[0] + 16)

            def halves(a, half):
                return a.rearrange("p (n b) -> p n b", b=2 * half)

            def diff(l):
                half = LEVELS[l]
                n = 2 * T // (2 * half)
                c = halves(cum[:].rearrange("p a b c -> p (a b c)"), half)
                e = halves(lv_e[:, l % 2], half)
                edge = c[:, :, half - 1:half].to_broadcast([P, n, half])
                nc.vector.tensor_tensor(e[:, :, half:], c[:, :, half:], edge, ALU.subtract)
                nc.vector.tensor_tensor(e[:, :, 0:half], edge, c[:, :, 0:half], ALU.subtract).then_inc(S["gl_diff"], 1)

            def factors(l):
                half = LEVELS[l]
                e = halves(lv_e[:, l % 2], half)
                if l >= 2:
                    dve.wait_ge(psum_full, g.full(("lv", l - 1, GH - 1)))
                dve.wait_ge(S["gl_exp"], l + 2)
                nc.vector.tensor_tensor(halves(qf(lv_q[:, l % 2]), half)[:, :, half:],
                                        halves(qf(q_s[:]), half)[:, :, half:], e[:, :, half:],
                                        ALU.mult).then_inc(S["gl_fac"], 1)
                nc.vector.tensor_tensor(halves(qf(lv_k[:, l % 2]), half)[:, :, 0:half],
                                        halves(qf(qkv[:, 2:4, :]), half)[:, :, 0:half], e[:, :, 0:half],
                                        ALU.mult).then_inc(S["gl_fac"], 1)
                dve.wait_ge(S["gl_fac"], 2 * l + 2)

            def keep(l):
                for x in range(GH):
                    dve.wait_ge(psum_full, g.full(("lv", l, x)))
                    nc.vector.copy_predicated(
                        scores[:, x], masks[:, l, :].unsqueeze(1).to_broadcast([P, TB, P]),
                        psum[g.bank(("lv", l, x))][:].rearrange("p (t c) -> p t c", t=TB)).then_inc(dve_evac, 1)
                dve.wait_ge(dve_evac, g.read(("lv", l, GH - 1))[1])

            diff(0)
            for l in range(NL):
                if l + 1 < NL:
                    diff(l + 1)
                factors(l)
                keep(l)
            keep(NL)
            nc.vector.engine_nop().then_inc(S["gl_scored"], 1)
            dve.wait_ge(S["gl_decay"], 1)
            for t in range(TB - 1):
                dve.wait_ge(psum_full, g.full(("st", t)))
                b = psum[g.bank(("st", t))]
                for x in range(2):
                    for y in range(2):
                        r = slice(GDK * y, GDK * y + GDK)
                        new = state[r, t % 2, x, :]
                        add = b[r, 2 * x * GDV + y * GDV:2 * x * GDV + (y + 1) * GDV]
                        if t == 0:
                            last = nc.vector.tensor_copy(new, add)
                        else:
                            last = nc.vector.scalar_tensor_tensor(out=new, in0=state[r, (t - 1) % 2, x, :],
                                                                  scalar=dec[r, x, t:t + 1], in1=add,
                                                                  op0=ALU.mult, op1=ALU.add)
                last.then_inc(dve_evac, 1)
                dve.wait_ge(dve_evac, g.read(("st", t))[1])
            dve.wait_ge(S["gl_sq"], 1)
            link(dve, "dve", nc.vector.reduce_sum(gst[:, 0, :], tmp[:, 0:4 * T].rearrange("p (n d) -> p n d", d=GDV),
                                                  axis=AX.X))
            nc.vector.tensor_scalar(gst[:, 1, :], gst[:, 0, :], 1.0 / GDV, EPS, ALU.mult, ALU.add).then_inc(S["gl_var"], 1)
            dve.wait_ge(S["gl_sqrt"], 1)
            link(dve, "dve", nc.vector.reciprocal(gst[:, 2, :], gst[:, 2, :]))
            link(dve, "dve", nc.vector.tensor_tensor(gst[:, 3, :], gst[:, 2, :], gst[:, 2, :], ALU.mult))
            link(dve, "dve", nc.vector.tensor_tensor(gst[:, 3, :], gst[:, 3, :], gst[:, 1, :], ALU.mult))
            link(dve, "dve", nc.vector.tensor_scalar(gst[:, 3, :], gst[:, 3, :], -0.5, 1.5, ALU.mult, ALU.add))
            link(dve, "dve", nc.vector.tensor_tensor(gst[:, 4, :], gst[:, 3, :], gst[:, 2, :], ALU.mult))
            of = o_gla[:].rearrange("p t (x d) -> p (t x) d", d=GDV)
            link(dve, "dve", nc.vector.tensor_tensor(of, of, gst[:, 4, :].unsqueeze(2).to_broadcast([P, TB * GH, GDV]),
                                                     ALU.mult))
            nc.vector.tensor_tensor(o_gla[:], o_gla[:], og[:], ALU.mult).then_inc(S["gl_on"], 1)

        @block.tensor
        def _(pe):
            for x in range(GH):
                bank = opened(pe, g, ("vt", x))
                for t in range(TB):
                    last = nc.tensor.transpose(bank[:, t * P:(t + 1) * P], qkv[:, 4 + x, t * P:(t + 1) * P], ident)
                last.then_inc(psum_full, 1)

            def level(l, q, k):
                for x in range(GH):
                    bank = opened(pe, g, ("lv", l, x))
                    r = slice(GDK * (x % 2), GDK * (x % 2) + GDK)
                    for t in range(TB):
                        c = slice(t * P, (t + 1) * P)
                        last = nc.tensor.matmul(bank[:, c], k[r, x // 2, c], q[r, x // 2, c], start=True, stop=True)
                    last.then_inc(psum_full, 1)
            pe.wait_ge(S["gl_qs"], 1)
            level(0, q_s, qkv[:, 2:4, :])
            pe.wait_ge(S["gl_kdec"], 1)
            for x in range(2):
                bank = opened(pe, g, ("kt", x))
                for t in range(TB):
                    last = nc.tensor.transpose(bank[:, t * P:(t + 1) * P], k_dec[:, x, t * P:(t + 1) * P], ident)
                last.then_inc(psum_full, 1)
            pe.wait_ge(S["gl_clear"], 1)
            for l in range(NL):
                pe.wait_ge(S["gl_fac"], 2 * l + 2)
                level(l + 1, lv_q[:, l % 2], lv_k[:, l % 2])
            pe.wait_ge(S["gl_scored"], 1)
            pe.wait_ge(S["gl_qin"], 1)
            wait_read(pe, g, ("kt", 1))
            wait_read(pe, g, ("vt", GH - 1))
            for t in range(TB):
                if t:
                    wait_read(pe, g, ("st", t - 1))
                for y in range(2):
                    bank = opened(pe, g, ("o", t, y))
                    r = slice(GDK * y, GDK * y + GDK)
                    for x in (y, y + 2):
                        o = bank[:, (x // 2) * GDV:(x // 2 + 1) * GDV]
                        last = nc.tensor.matmul(o, scores[:, x, t, :], v_nat[:, t, x * GDV:(x + 1) * GDV],
                                                start=True, stop=(t == 0))
                        if t:
                            last = nc.tensor.matmul(o, q_in[r, x // 2, t * P:(t + 1) * P],
                                                    state[r, (t - 1) % 2, x // 2, :], start=False, stop=True)
                    last.then_inc(psum_full, 1)
                if t < TB - 1:
                    bank = opened(pe, g, ("st", t))
                    for x in range(2):
                        last = nc.tensor.matmul(bank[:, 2 * x * GDV:2 * (x + 1) * GDV], k_nat[:, x, t, :],
                                                v_nat[:, t, 2 * x * GDV:2 * (x + 1) * GDV], start=True, stop=True)
                    last.then_inc(psum_full, 1)
            pe.wait_ge(S["gl_on"], 1)
            for x in range(GH):
                bank = opened(pe, g, ("gt", x))
                for t in range(TB):
                    last = nc.tensor.transpose(bank[:, t * P:(t + 1) * P], o_gla[:, t, x * GDV:(x + 1) * GDV], ident)
                last.then_inc(psum_full, 1)
    loads[0] += 16
    stage.close()

    stage = ExitStack()
    zb = sb(stage, "zb", [P, 3, STOT])
    sp_ = sb(stage, "sp", [P, 2, STOT])
    wb = sb(stage, "wb", [P, 2, STOT])
    o_sb = sb(stage, "o_sb", [P, TB, SH * SD])
    s_names = ["sb_ln", "sb_sp", "sb_spm", "sb_arg", "sb_w", "sb_wm"]
    S = {n: sem(n) for n in s_names}
    plan = []
    for i in range(SH + 2):
        if i < SH:
            plan += [(("z", i, s), "act") for s in range(TB)]
        if 1 <= i <= SH:
            plan += [(("c", i - 1, s), "dve") for s in range(TB)]
        if i >= 2:
            plan += [(("pv", i - 2), "act")]
    g = Groups(C, plan)
    with nc.Block() as block:
        @block.tensor
        def _(pe):
            for i in range(SH + 2):
                if i < SH:
                    x, r = i // 2, slice(SD * (i % 2), SD * (i % 2) + SD)
                    for s in range(TB):
                        bank = opened(pe, g, ("z", i, s))
                        nc.tensor.matmul(bank[:, 0:SLEN[s]], s_k[r, x, s * P:(s + 1) * P], s_q[r, x, s * P:T],
                                         start=True, stop=True).then_inc(psum_full, 1)
                if 1 <= i <= SH:
                    n = i - 1
                    pe.wait_ge(S["sb_spm"], n + 1)
                    for s in range(TB):
                        bank = opened(pe, g, ("c", n, s))
                        for s2 in range(s, TB):
                            last = nc.tensor.matmul(bank[:, (s2 - s) * P:SLEN[s]], tri if s2 == s else ones,
                                                    sp_[:, n % 2, SOFF[s2]:SOFF[s2] + SLEN[s2]],
                                                    start=(s2 == s), stop=(s2 == TB - 1))
                        last.then_inc(psum_full, 1)
                if i >= 2:
                    n = i - 2
                    pe.wait_ge(S["sb_wm"], n + 1)
                    bank = opened(pe, g, ("pv", n))
                    for t in range(TB):
                        for s in range(t + 1):
                            at = SOFF[s] + (t - s) * P
                            last = nc.tensor.matmul(bank[:, t * SD:(t + 1) * SD], wb[:, n % 2, at:at + P],
                                                    s_v[:, s, n * SD:(n + 1) * SD], start=(s == 0), stop=(s == t))
                    last.then_inc(psum_full, 1)

        @block.scalar
        def _(act):
            for i in range(SH + 2):
                if i < SH:
                    if i >= 3:
                        act.wait_ge(S["sb_arg"], i - 2)
                    for s in range(TB):
                        act.wait_ge(psum_full, g.full(("z", i, s)))
                        nc.scalar.activation(zb[:, i % 3, SOFF[s]:SOFF[s] + SLEN[s]],
                                             psum[g.bank(("z", i, s))][:, 0:SLEN[s]],
                                             ACT.Identity).then_inc(act_evac, 1)
                    wait_read(act, g, ("z", i, TB - 1))
                    if i >= 2:
                        act.wait_ge(psum_full, g.full(("c", i - 2, TB - 1)))
                    t = sp_[:, i % 2, :]
                    link(act, "act", nc.scalar.activation(t, zb[:, i % 3, :], ACT.Abs))
                    link(act, "act", nc.scalar.activation(t, t, ACT.Exp, scale=-1.0))
                    nc.scalar.activation(t, t, ACT.Ln, bias=1.0).then_inc(S["sb_ln"], 1)
                if 1 <= i <= SH:
                    n = i - 1
                    act.wait_ge(S["sb_arg"], n + 1)
                    nc.scalar.activation(wb[:, n % 2, :], wb[:, n % 2, :], ACT.Exp).then_inc(S["sb_w"], 1)
                if i >= 2:
                    n = i - 2
                    act.wait_ge(psum_full, g.full(("pv", n)))
                    nc.scalar.activation(o_sb[:, :, n * SD:(n + 1) * SD],
                                         psum[g.bank(("pv", n))][:, 0:TB * SD].rearrange("p (t d) -> p t d", t=TB),
                                         ACT.Identity).then_inc(act_evac, 1)

        @block.vector
        def _(dve):
            for i in range(SH + 1):
                if i < SH:
                    dve.wait_ge(S["sb_ln"], i + 1)
                    nc.vector.scalar_tensor_tensor(out=sp_[:, i % 2, :], in0=zb[:, i % 3, :], scalar=0.0,
                                                   in1=sp_[:, i % 2, :], op0=ALU.max,
                                                   op1=ALU.add).then_inc(S["sb_sp"], 1)
                if i >= 1:
                    n = i - 1
                    if n >= 2:
                        dve.wait_ge(psum_full, g.full(("pv", n - 2)))
                    for s in range(TB):
                        o = slice(SOFF[s], SOFF[s] + SLEN[s])
                        dve.wait_ge(psum_full, g.full(("c", n, s)))
                        nc.vector.tensor_tensor(wb[:, n % 2, o], zb[:, n % 3, o],
                                                psum[g.bank(("c", n, s))][:, 0:SLEN[s]],
                                                ALU.subtract).then_inc(dve_evac, 1)
                    dve.wait_ge(dve_evac, g.read(("c", n, TB - 1))[1])
                    nc.vector.engine_nop().then_inc(S["sb_arg"], 1)

        @block.gpsimd
        def _(pool):
            def strict(buf, done):
                for s in range(TB):
                    piece = buf[:, SOFF[s]:SOFF[s] + P]
                    last = nc.gpsimd.affine_select(out=piece, in_=piece, compare_op=ALU.is_gt, fill=0.0, base=0,
                                                   pattern=[[1, P]], channel_multiplier=-1)
                last.then_inc(done, 1)
            for i in range(SH + 1):
                if i < SH:
                    pool.wait_ge(S["sb_sp"], i + 1)
                    strict(sp_[:, i % 2, :], S["sb_spm"])
                if i >= 1:
                    pool.wait_ge(S["sb_w"], i)
                    strict(wb[:, (i - 1) % 2, :], S["sb_wm"])
    norm_transpose("nsb", o_sb, TB, SH * SD, V_SBG, act_t, GH * GDV // P)
    stage.close()
    mixer.close()

    def add_projection(name, q0):
        plan = [((half, t), "dve") for half in range(2) for t in range(TB)]
        g = Groups(C, plan)
        for half in range(2):
            quad_last[q0 + half] = g.full((half, TB - 1))
        with nc.Block() as block:
            @block.sync
            def _(sp):
                prefetch(sp, q0, q0 + 2)

            @block.tensor
            def _(pe):
                for half in range(2):
                    s = quad(pe, q0 + half)
                    for t in range(TB):
                        projected_natural(pe, g, (half, t), s, act_t, t)

            @block.vector
            def _(dve):
                for half in range(2):
                    for t in range(TB):
                        dve.wait_ge(psum_full, g.full((half, t)))
                        o = h[:, t, 512 * half:512 * half + 512]
                        nc.vector.tensor_tensor(o, o, psum[g.bank((half, t))][:], ALU.add).then_inc(dve_evac, 1)

    add_projection("wout", Q_OUT)

    xa = ExitStack()
    xk = sb(xa, "xk", [P, DC, M])
    xv = sb(xa, "xv", [P, MB, D])
    xq = sb(xa, "xq", [P, DC, T])
    stage = ExitStack()
    mem = sb(stage, "mem", [P, MB, D])
    mem_t = sb(stage, "mem_t", [P, DC, M])
    with nc.Block() as block:
        @block.sync
        def _(sp):
            sp.dma_start(mem[:], A["mem"]).then_inc(small_loaded, 16)
            sp.wait_ge(small_loaded, loads[0] + 16)
    loads[0] += 16
    norm_transpose("nmem", mem, MB, D, V_MEM, mem_t)
    norm_transpose("nxa", h, TB, D, V_XA, act_t)
    plan = [(("q", n), "act") for n in range(DC)] + [(("k", n), "dve") for n in range(DC)]
    plan += [(("v", half, t), "dve") for half in range(2) for t in range(MB)]
    g = Groups(C, plan)
    for q in range(2):
        quad_last[Q_XQ + q] = g.full(("q", 4 * q + 3))
        quad_last[Q_XK + q] = g.full(("k", 4 * q + 3))
        quad_last[Q_XV + q] = g.full(("v", q, MB - 1))
    with nc.Block() as block:
        @block.sync
        def _(sp):
            prefetch(sp, Q_XQ, Q_XO)

        @block.tensor
        def _(pe):
            for q in range(2):
                s = quad(pe, Q_XQ + q)
                for n in range(4):
                    projected(pe, g, ("q", 4 * q + n), s + n, lambda c: act_t[:, c, :], T)
            for q in range(2):
                s = quad(pe, Q_XK + q)
                for n in range(4):
                    projected(pe, g, ("k", 4 * q + n), s + n, lambda c: mem_t[:, c, :], M)
            for q in range(2):
                s = quad(pe, Q_XV + q)
                for t in range(MB):
                    projected_natural(pe, g, ("v", q, t), s, mem_t, t)

        @block.scalar
        def _(act):
            for n in range(DC):
                act.wait_ge(psum_full, g.full(("q", n)))
                nc.scalar.activation(xq[:, n, :], psum[g.bank(("q", n))][:], ACT.Identity).then_inc(act_evac, 1)

        @block.vector
        def _(dve):
            for n in range(DC):
                dve.wait_ge(psum_full, g.full(("k", n)))
                nc.vector.tensor_copy(xk[:, n, :], psum[g.bank(("k", n))][:, 0:M]).then_inc(dve_evac, 1)
            for half in range(2):
                for t in range(MB):
                    dve.wait_ge(psum_full, g.full(("v", half, t)))
                    nc.vector.tensor_copy(xv[:, t, 512 * half:512 * half + 512],
                                          psum[g.bank(("v", half, t))][:]).then_inc(dve_evac, 1)
    stage.close()
    stage = ExitStack()
    prob = sb(stage, "prob", [P, 2, TB, M])
    prob_t = sb(stage, "prob_t", [P, 2, MB, T])
    xst = sb(stage, "xst", [P, XH, 4, TB])
    x_max, x_exp, x_norm = sem("x_max"), sem("x_exp"), sem("x_norm")
    XSCALE = float(XD) ** -0.5
    plan = []
    for i in range(XH + 1):
        if i < XH:
            plan += [(("s", i, u), "act") for u in range(TB // 2)]
        if i >= 1:
            plan += [(("p", i - 1, m), "act") for m in range(MB)]
            plan += [(("o", i - 1, c), "dve") for c in range(2)]
    g = Groups(C, plan)
    with nc.Block() as block:
        @block.tensor
        def _(pe):
            for i in range(XH + 1):
                if i < XH:
                    for u in range(TB // 2):
                        bank = opened(pe, g, ("s", i, u))
                        for v in range(2):
                            t = 2 * u + v
                            for c in range(2):
                                last = nc.tensor.matmul(bank[:, v * M:(v + 1) * M],
                                                        xq[:, 2 * i + c, t * P:(t + 1) * P], xk[:, 2 * i + c, :],
                                                        start=(c == 0), stop=(c == 1))
                        last.then_inc(psum_full, 1)
                if i >= 1:
                    n = i - 1
                    pe.wait_ge(x_norm, n + 1)
                    for m in range(MB):
                        bank = opened(pe, g, ("p", n, m))
                        for t in range(TB):
                            last = nc.tensor.transpose(bank[:, t * P:(t + 1) * P],
                                                       prob[:, n % 2, t, m * P:(m + 1) * P], ident)
                        last.then_inc(psum_full, 1)
                    wait_read(pe, g, ("p", n, MB - 1))
                    for c in range(2):
                        bank = opened(pe, g, ("o", n, c))
                        f = (2 * n + c) * P
                        for m in range(MB):
                            last = nc.tensor.matmul(bank[:], xv[:, m, f:f + P], prob_t[:, n % 2, m, :],
                                                    start=(m == 0), stop=(m == MB - 1))
                        last.then_inc(psum_full, 1)

        @block.scalar
        def _(act):
            for i in range(XH + 1):
                if i < XH:
                    if i >= 2:
                        act.wait_ge(psum_full, g.full(("p", i - 2, MB - 1)))
                    act.wait_ge(x_max, i + 1)
                    for t in range(TB):
                        b = psum[g.bank(("s", i, t // 2))]
                        ins = nc.scalar.activation(prob[:, i % 2, t, :], b[:, (t % 2) * M:(t % 2 + 1) * M], ACT.Exp,
                                                   bias=xst[:, i, 1, t:t + 1], scale=XSCALE,
                                                   accum_out=xst[:, i, 2, t:t + 1])
                        if t % 2:
                            ins.then_inc(act_evac, 1)
                if i >= 1:
                    for m in range(MB):
                        act.wait_ge(psum_full, g.full(("p", i - 1, m)))
                        nc.scalar.activation(prob_t[:, (i - 1) % 2, m, :], psum[g.bank(("p", i - 1, m))][:],
                                             ACT.Identity).then_inc(act_evac, 1)

        @block.vector
        def _(dve):
            for i in range(XH + 1):
                if i < XH:
                    for u in range(2):
                        dve.wait_ge(psum_full, g.full(("s", i, u)))
                        ins = nc.vector.reduce_max(xst[:, i, 0, 2 * u:2 * u + 2],
                                                   psum[g.bank(("s", i, u))][:].rearrange("p (t m) -> p t m", t=2),
                                                   axis=AX.X)
                    link(dve, "dve", ins)
                    nc.vector.tensor_scalar(xst[:, i, 1, :], xst[:, i, 0, :], -XSCALE, None, ALU.mult).then_inc(x_max, 1)
                    wait_read(dve, g, ("s", i, 1))
                    link(dve, "dve", nc.vector.reciprocal(xst[:, i, 3, :], xst[:, i, 2, :]))
                    nc.vector.tensor_tensor(prob[:, i % 2], prob[:, i % 2],
                                            xst[:, i, 3, :].unsqueeze(2).to_broadcast([P, TB, M]),
                                            ALU.mult).then_inc(x_norm, 1)
                if i >= 1:
                    for c in range(2):
                        dve.wait_ge(psum_full, g.full(("o", i - 1, c)))
                        nc.vector.tensor_copy(act_t[:, 2 * (i - 1) + c, :],
                                              psum[g.bank(("o", i - 1, c))][:]).then_inc(dve_evac, 1)
    stage.close()
    xa.close()
    add_projection("xo", Q_XO)

    norm_transpose("nffn", h, TB, D, V_FFN, act_t)
    route = ExitStack()
    top_v = sb(route, "top_v", [P, TB, HP, TOPK])
    top_i = sb(route, "top_i", [P, TB, HP, TOPK], U32)
    stage = ExitStack()
    keys = sb(stage, "keys", [P, HP, NKEYS])
    pq = sb(stage, "pq", [P, 2, T])
    ps = sb(stage, "ps", [P, 2, TB, NKEYS])
    pw = sb(stage, "pw", [P, TB, NKEYS])
    r_top = sem("r_top")
    plan = []
    for i in range(HP + 1):
        if i < HP:
            plan += [(("q", i), "act")]
        if i >= 1:
            plan += [(("s", i - 1), "act")]
    g = Groups(C, plan)
    for q in range(4):
        quad_last[Q_PQ + q] = g.full(("q", 4 * q + 3))
    with nc.Block() as block:
        @block.sync
        def _(sp):
            sp.dma_start(keys[:], A["keys"]).then_inc(small_loaded, 16)
            sp.dma_start(h_scratch, h[:]).then_inc(stored, 16)
            for half in range(2):
                sp.dma_start(xf_scratch[:, half], act_t[:, :, half * HALF:(half + 1) * HALF]).then_inc(stored, 16)
            prefetch(sp, Q_PQ, NQUADS - QRING)
            sp.wait_ge(stored, 48)

        @block.tensor
        def _(pe):
            for i in range(HP + 1):
                if i < HP:
                    s = quad(pe, Q_PQ + i // 4)
                    projected(pe, g, ("q", i), s + i % 4, lambda c: act_t[:, c, :], T)
                if i >= 1:
                    if i == 1:
                        pe.wait_ge(small_loaded, loads[0] + 16)
                    wait_read(pe, g, ("q", i - 1))
                    bank = opened(pe, g, ("s", i - 1))
                    for t in range(TB):
                        last = nc.tensor.matmul(bank[:, t * P:(t + 1) * P], pq[:, (i - 1) % 2, t * P:(t + 1) * P],
                                                keys[:, i - 1, :], start=True, stop=True)
                    last.then_inc(psum_full, 1)

        @block.scalar
        def _(act):
            for i in range(HP + 1):
                if i < HP:
                    act.wait_ge(psum_full, g.full(("q", i)))
                    if i >= 2:
                        act.wait_ge(psum_full, g.full(("s", i - 2)))
                    nc.scalar.activation(pq[:, i % 2, :], psum[g.bank(("q", i))][:], ACT.Identity).then_inc(act_evac, 1)
                if i >= 1:
                    act.wait_ge(psum_full, g.full(("s", i - 1)))
                    if i >= 3:
                        act.wait_ge(r_top, i - 2)
                    nc.scalar.activation(ps[:, (i - 1) % 2], psum[g.bank(("s", i - 1))][:].rearrange(
                        "p (t n) -> p t n", t=TB), ACT.Identity).then_inc(act_evac, 1)

        @block.vector
        def _(dve):
            for i in range(HP):
                wait_read(dve, g, ("s", i))
                for t in range(TB):
                    ins = nc.vector.max(top_v[:, t, i, 0:8], ps[:, i % 2, t, :])
                link(dve, "dve", ins)
                for t in range(TB):
                    nc.vector.max_index(top_i[:, t, i, 0:8], top_v[:, t, i, 0:8], ps[:, i % 2, t, :])
                    ins = nc.vector.match_replace(pw[:, t, :], top_v[:, t, i, 0:8], ps[:, i % 2, t, :], NEG)
                link(dve, "dve", ins)
                for t in range(TB):
                    ins = nc.vector.max(top_v[:, t, i, 8:16], pw[:, t, :])
                link(dve, "dve", ins)
                for t in range(TB):
                    ins = nc.vector.max_index(top_i[:, t, i, 8:16], top_v[:, t, i, 8:16], pw[:, t, :])
                ins.then_inc(r_top, 1)
                dve.wait_ge(r_top, i + 1)
    loads[0] += 16
    stage.close()

    stage = ExitStack()
    NC = TOPK * TOPK
    cand = sb(stage, "cand", [P, PH, NC])
    cw = sb(stage, "cw", [P, PH, NC])
    best = sb(stage, "best", [P, PH, TOPK])
    pos = sb(stage, "pos", [P, PH, TOPK], U32)
    posx = sb(stage, "posx", [P, 2, SLOTS], U32)
    posf = sb(stage, "posf", [P, 2, SLOTS])
    idxf = sb(stage, "idxf", [P, HP, TOPK])
    triple = sb(stage, "triple", [P, 2, 3, SLOTS])
    gs = sb(stage, "gs", [P, 2, PH])
    r_diff, r_exp, r_triple = sem("r_diff"), sem("r_exp"), sem("r_triple")
    g = Groups(C, [(t, "act") for t in range(TB)])
    with nc.Block() as block:
        @block.vector
        def _(dve):
            for t in range(TB):
                if t >= 2:
                    dve.wait_ge(psum_full, g.full(t - 2))
                tv = top_v[:, t].rearrange("p (x s) k -> p x s k", s=2)
                c4 = cand[:].rearrange("p x (a b) -> p x a b", b=TOPK)
                link(dve, "dve", nc.vector.tensor_tensor(
                    c4, tv[:, :, 0, :].unsqueeze(3).to_broadcast([P, PH, TOPK, TOPK]),
                    tv[:, :, 1, :].unsqueeze(2).to_broadcast([P, PH, TOPK, TOPK]), ALU.add))
                for x in range(PH):
                    ins = nc.vector.max(best[:, x, 0:8], cand[:, x, :])
                link(dve, "dve", ins)
                for x in range(PH):
                    nc.vector.max_index(pos[:, x, 0:8], best[:, x, 0:8], cand[:, x, :])
                    ins = nc.vector.match_replace(cw[:, x, :], best[:, x, 0:8], cand[:, x, :], NEG)
                link(dve, "dve", ins)
                for x in range(PH):
                    ins = nc.vector.max(best[:, x, 8:16], cw[:, x, :])
                link(dve, "dve", ins)
                for x in range(PH):
                    ins = nc.vector.max_index(pos[:, x, 8:16], best[:, x, 8:16], cw[:, x, :])
                link(dve, "dve", ins)
                gate = triple[:, t % 2, 2, :].rearrange("p (x k) -> p x k", k=TOPK)
                nc.vector.tensor_tensor(gate, best[:], best[:, :, 0:1].to_broadcast([P, PH, TOPK]),
                                        ALU.subtract).then_inc(r_diff, 1)
                pf = pos[:].rearrange("p x k -> p (x k)")
                nc.vector.tensor_scalar(posx[:, 0, :], pf, 4, None, ALU.logical_shift_right)
                link(dve, "dve", nc.vector.tensor_scalar(posx[:, 1, :], pf, TOPK - 1, None, ALU.bitwise_and))
                nc.vector.tensor_copy(idxf[:], top_i[:, t])
                link(dve, "dve", nc.vector.tensor_copy(posf[:], posx[:]))
                for s in range(2):
                    pick = cand[:].rearrange("p x (k a) -> p x k a", a=TOPK)
                    rank = posf[:, s, :].rearrange("p (x k) -> p x k", k=TOPK).unsqueeze(3)
                    idx = idxf[:].rearrange("p (x s) a -> p x s a", s=2)[:, :, s, :].unsqueeze(2)
                    link(dve, "dve", nc.vector.tensor_tensor(
                        pick.rearrange("p x k a -> p (x k) a"),
                        posf[:, s, :].unsqueeze(2).to_broadcast([P, SLOTS, TOPK]),
                        iota16.unsqueeze(1).to_broadcast([P, SLOTS, TOPK]), ALU.is_equal))
                    link(dve, "dve", nc.vector.tensor_tensor(pick, pick, idx.to_broadcast([P, PH, TOPK, TOPK]),
                                                             ALU.mult))
                    link(dve, "dve", nc.vector.reduce_sum(triple[:, t % 2, s, :],
                                                          pick.rearrange("p x k a -> p (x k) a"), axis=AX.X))
                dve.wait_ge(r_exp, t + 1)
                link(dve, "dve", nc.vector.reduce_sum(gs[:, 0, :], gate, axis=AX.X))
                link(dve, "dve", nc.vector.reciprocal(gs[:, 1, :], gs[:, 0, :]))
                nc.vector.tensor_tensor(gate, gate, gs[:, 1, :].unsqueeze(2).to_broadcast([P, PH, TOPK]),
                                        ALU.mult).then_inc(r_triple, 1)
                dve.wait_ge(r_triple, t + 1)

        @block.scalar
        def _(act):
            for t in range(TB):
                act.wait_ge(r_diff, t + 1)
                gate = triple[:, t % 2, 2, :]
                nc.scalar.activation(gate, gate, ACT.Exp).then_inc(r_exp, 1)
                act.wait_ge(psum_full, g.full(t))
                nc.scalar.activation(slot_t[:, :, t * P:(t + 1) * P],
                                     psum[g.bank(t)][:, 0:3 * P].rearrange("p (s t) -> p s t", s=3),
                                     ACT.Identity).then_inc(act_evac, 1)

        @block.tensor
        def _(pe):
            for t in range(TB):
                pe.wait_ge(r_triple, t + 1)
                bank = opened(pe, g, t)
                for s in range(3):
                    last = nc.tensor.transpose(bank[:, s * P:(s + 1) * P], triple[:, t % 2, s, :], ident)
                last.then_inc(psum_full, 1)
    stage.close()
    route.close()
    main.close()

    peer = ExitStack()
    NB = 4
    NT, HOT = 8, 4
    G = sb(peer, "gates", [P, NKEYS, HALF])
    raw = sb(peer, "raw", [P, 4, D])
    xs_hi = sb(peer, "xs_hi", [P, DC, HALF], F32R)
    xs_lo = sb(peer, "xs_lo", [P, DC, HALF], F32R)
    u_hi = sb(peer, "u_hi", [P, 2, DC, P], F32R)
    u_lo = sb(peer, "u_lo", [P, 2, DC, P], F32R)
    v_hi = sb(peer, "v_hi", [P, 2, D], F32R)
    v_lo = sb(peer, "v_lo", [P, 2, D], F32R)
    u_loaded = [sem(f"u_loaded{k}") for k in range(2)]
    v_loaded = [sem(f"v_loaded{k}") for k in range(2)]
    hot_ready, hot_used, g_read = sem("hot_ready"), sem("hot_used"), sem("g_read")
    u_hi_done, u_lo_done, v_hi_done, v_lo_done = (sem(x) for x in ("u_hi_done", "u_lo_done", "v_hi_done", "v_lo_done"))
    u_done, v_done, gelu_done, w_mult, w_hi_done, w_ready, y_read = (
        sem(x) for x in ("u_done", "v_done", "gelu_done", "w_mult", "w_hi_done", "w_ready", "y_read"))
    x_loaded, x_hi_done, x_lo_done = sem("x_loaded"), sem("x_hi_done"), sem("x_lo_done")
    f_h, f_g, f_ss, f_sq = sem("f_h"), sem("f_g"), sem("f_ss"), sem("f_sq")
    BODIES = NKEYS // NB
    TBODIES = HALF // NT
    for half in range(2):
        t0 = half * HALF
        x_raw = raw[:, 0:2].rearrange("p s (c t) -> p (s c) t", t=HALF)
        stage = ExitStack()
        hot = sb(stage, f"hot{half}", [P, HOT, 2, P])
        with nc.Block() as block:
            @block.sync
            def _(sp):
                sp.dma_start(x_raw, xf_scratch[:, half]).then_inc(x_loaded, 16)

            @block.vector
            def _(dve):
                def body(i, first):
                    for k in range(NT):
                        if not (first and k < HOT):
                            dve.wait_ge(hot_used, i * NT + (half * HALF + k + 1 - HOT))
                        col = lambda s: slot_t[:, s, bass.ds(i * NT + (t0 + k), 1)]
                        nc.vector.tensor_scalar(hot[:, k % HOT, 0, :], iota, col(0), None, ALU.is_equal)
                        nc.vector.tensor_scalar(hot[:, k % HOT, 1, :], iota, col(1), col(2), ALU.is_equal,
                                                ALU.mult).then_inc(hot_ready, 1)
                body(0, half == 0)
                with dve.Fori(1, TBODIES) as i:
                    body(i, False)
                dve.wait_ge(x_hi_done, half + 1)
                nc.vector.tensor_tensor(xs_lo[:], x_raw, xs_hi[:].bitcast(F32), ALU.subtract).then_inc(x_lo_done, 1)

            @block.tensor
            def _(pe):
                def body(i, first):
                    for k in range(NT):
                        if k % 4 == 0 and not first:
                            pe.wait_ge(g_read, i * 2 + (2 * half * TBODIES + k // 4 - 1))
                        pe.wait_ge(hot_ready, i * NT + (half * HALF + k + 1))
                        nc.tensor.matmul(psum[k // 4][:, k % 4 * P:(k % 4 + 1) * P], hot[:, k % HOT, 0, :],
                                         hot[:, k % HOT, 1, :], start=True, stop=True).then_inc(hot_used, 1)
                body(0, half == 0)
                with pe.Fori(1, TBODIES) as i:
                    body(i, False)

            @block.scalar
            def _(act):
                act.wait_ge(x_loaded, 16 * (half + 1))
                nc.scalar.activation(xs_hi[:], x_raw, ACT.Identity).then_inc(x_hi_done, 1)

                def body(i):
                    for b in range(2):
                        act.wait_ge(hot_used, i * NT + (half * HALF + 4 * b + 4))
                        nc.scalar.activation(G[:, :, bass.ds(i * NT + 4 * b, 4)],
                                             psum[b][:].rearrange("p (t j) -> p j t", t=4),
                                             ACT.Identity).then_inc(g_read, 1)
                body(0)
                with act.Fori(1, TBODIES) as i:
                    body(i)
        stage.close()
        stage = ExitStack()
        gel = sb(stage, f"gel{half}", [P, 2, HALF])
        w_hi = sb(stage, f"w_hi{half}", [P, 2, HALF], F32R)
        w_lo = sb(stage, f"w_lo{half}", [P, 2, HALF], F32R)
        wf = gel
        base = half * NKEYS
        u_raw = lambda n: raw[:, n % 2].rearrange("p (c i) -> p c i", i=P)
        v_raw = lambda n: raw[:, 2 + n % 2]
        with nc.Block() as block:
            @block.sync
            def _(sp):
                def load_u(i, k, first):
                    if not first:
                        sp.wait_ge(u_lo_done, i * NB + (base + k - 1))
                    sp.dma_start(u_raw(k), A["u_tiles"][bass.ds(i * NB + k, 1)].rearrange("o p c i -> (o p) c i")
                                 ).then_inc(u_loaded[k % 2], 16)

                def load_v(i, k, first):
                    if not first:
                        sp.wait_ge(v_lo_done, i * NB + (base + k - 1))
                    sp.dma_start(v_raw(k), A["v"][:, bass.ds(i * NB + k, 1), :].rearrange("i o d -> i (o d)")
                                 ).then_inc(v_loaded[k % 2], 16)
                for k in range(NB):
                    load_u(0, k, half == 0 and k < 2)
                    load_v(0, k, half == 0 and k < 2)
                with sp.Fori(1, BODIES) as i:
                    for k in range(NB):
                        load_u(i, k, False)
                        load_v(i, k, False)

            @block.tensor
            def _(pe):
                def up(i, k, first=False):
                    pe.wait_ge(u_lo_done, i * NB + (base + k + 1))
                    if not first:
                        pe.wait_ge(gelu_done, i * NB + (base + k - 1))
                    bank = psum[k % 2][:, 0:HALF]
                    for c in range(DC):
                        nc.tensor.matmul(bank, u_lo[:, k % 2, c, :], xs_hi[:, c, :], start=(c == 0), stop=False)
                        nc.tensor.matmul(bank, u_hi[:, k % 2, c, :], xs_lo[:, c, :], start=False, stop=False)
                        last = nc.tensor.matmul(bank, u_hi[:, k % 2, c, :], xs_hi[:, c, :], start=False,
                                                stop=(c == DC - 1))
                    last.then_inc(u_done, 1)

                def down(i, k, start=False, stop=False):
                    pe.wait_ge(v_lo_done, i * NB + (base + k + 1))
                    pe.wait_ge(w_ready, i * NB + (base + k + 1))
                    for t in range(2):
                        for d in range(2):
                            y = psum[4 + 2 * t + d][:]
                            tk, f = slice(t * P, (t + 1) * P), slice(512 * d, 512 * d + 512)
                            nc.tensor.matmul(y, w_lo[:, k % 2, tk], v_hi[:, k % 2, f], start=start, stop=False)
                            nc.tensor.matmul(y, w_hi[:, k % 2, tk], v_lo[:, k % 2, f], start=False, stop=False)
                            last = nc.tensor.matmul(y, w_hi[:, k % 2, tk], v_hi[:, k % 2, f], start=False, stop=stop)
                    last.then_inc(v_done, 1)
                pe.wait_ge(x_lo_done, half + 1)
                up(0, 0, half == 0)
                for k in range(NB):
                    up(0, k + 1, half == 0 and k == 0)
                    down(0, k, start=(k == 0))
                with pe.Fori(1, BODIES - 1) as i:
                    for k in range(NB):
                        up(i, k + 1)
                        down(i, k)
                for k in range(NB):
                    if k < NB - 1:
                        up(BODIES - 1, k + 1)
                    down(BODIES - 1, k, stop=(k == NB - 1))

            @block.scalar
            def _(act):
                def u_part(i, k, first=False):
                    act.wait_ge(u_loaded[k % 2], i * (NB // 2 * 16) + 16 * (base // 2 + k // 2 + 1))
                    if not first:
                        act.wait_ge(u_done, i * NB + (base + k - 1))
                    nc.scalar.activation(u_hi[:, k % 2], u_raw(k), ACT.Identity).then_inc(u_hi_done, 1)

                def v_part(i, k, first=False):
                    act.wait_ge(v_loaded[k % 2], i * (NB // 2 * 16) + 16 * (base // 2 + k // 2 + 1))
                    if not first:
                        act.wait_ge(v_done, i * NB + (base + k - 1))
                    nc.scalar.activation(v_hi[:, k % 2], v_raw(k), ACT.Identity).then_inc(v_hi_done, 1)

                def gelu(i, k, first=False):
                    act.wait_ge(u_done, i * NB + (base + k + 1))
                    if not first:
                        act.wait_ge(w_ready, i * NB + (base + k - 1))
                    nc.scalar.activation(gel[:, k % 2, :], psum[k % 2][:, 0:HALF],
                                         ACT.Gelu_apprx_tanh).then_inc(gelu_done, 1)
                u_part(0, 0, half == 0)
                u_part(0, 1, half == 0)
                v_part(0, 0, half == 0)
                for k in range(NB):
                    gelu(0, k, half == 0 and k < 2)
                    u_part(0, k + 2)
                    v_part(0, k + 1, half == 0 and k == 0)
                with act.Fori(1, BODIES - 1) as i:
                    for k in range(NB):
                        gelu(i, k)
                        u_part(i, k + 2)
                        v_part(i, k + 1)
                for k in range(NB):
                    gelu(BODIES - 1, k)
                    if k + 2 < NB:
                        u_part(BODIES - 1, k + 2)
                    if k + 1 < NB:
                        v_part(BODIES - 1, k + 1)

            @block.vector
            def _(dve):
                def u_part(i, k):
                    dve.wait_ge(u_hi_done, i * NB + (base + k + 1))
                    nc.vector.tensor_tensor(u_lo[:, k % 2], u_raw(k), u_hi[:, k % 2].bitcast(F32),
                                            ALU.subtract).then_inc(u_lo_done, 1)

                def v_part(i, k):
                    dve.wait_ge(v_hi_done, i * NB + (base + k + 1))
                    nc.vector.tensor_tensor(v_lo[:, k % 2], v_raw(k), v_hi[:, k % 2].bitcast(F32),
                                            ALU.subtract).then_inc(v_lo_done, 1)

                def weights(i, k, first=False):
                    n = lambda d: i * NB + (base + k + 1 - d)
                    dve.wait_ge(gelu_done, n(0))
                    if not first:
                        dve.wait_ge(v_done, n(2))
                    nc.vector.tensor_tensor(wf[:, k % 2, :], gel[:, k % 2, :], G[:, bass.ds(i * NB + k, 1), :].
                                            rearrange("p o t -> p (o t)"), ALU.mult).then_inc(w_mult, 1)
                    dve.wait_ge(w_mult, n(0))
                    nc.vector.tensor_copy(w_hi[:, k % 2, :], wf[:, k % 2, :]).then_inc(w_hi_done, 1)
                    dve.wait_ge(w_hi_done, n(0))
                    nc.vector.tensor_tensor(w_lo[:, k % 2, :], wf[:, k % 2, :], w_hi[:, k % 2, :].bitcast(F32),
                                            ALU.subtract).then_inc(w_ready, 1)
                u_part(0, 0)
                u_part(0, 1)
                v_part(0, 0)
                for k in range(NB):
                    weights(0, k, half == 0 and k < 2)
                    u_part(0, k + 2)
                    v_part(0, k + 1)
                with dve.Fori(1, BODIES - 1) as i:
                    for k in range(NB):
                        weights(i, k)
                        u_part(i, k + 2)
                        v_part(i, k + 1)
                for k in range(NB):
                    weights(BODIES - 1, k)
                    if k + 2 < NB:
                        u_part(BODIES - 1, k + 2)
                    if k + 1 < NB:
                        v_part(BODIES - 1, k + 1)
        hh, sq, gf = raw[:, 0:2], raw[:, 2], raw[:, 3]
        st = gel[:, 0, 0:10].rearrange("p (a b) -> p a b", b=2)
        with nc.Block() as block:
            @block.sync
            def _(sp):
                sp.dma_start(hh, h_scratch[:, 2 * half:2 * half + 2, :]).then_inc(f_h, 16)
                sp.dma_start(gf, A["final_g"].partition_broadcast(P)).then_inc(f_g, 16)
                sp.wait_ge(f_sq, 2 * half + 2)
                sp.dma_start(out[:, 2 * half:2 * half + 2, :], hh).then_inc(stored, 16)
                sp.wait_ge(stored, 16 * (half + 4))

            @block.vector
            def _(dve):
                dve.wait_ge(f_h, 16 * (half + 1))
                for t in range(2):
                    for d in range(2):
                        o = hh[:, t, 512 * d:512 * d + 512]
                        ins = nc.vector.tensor_tensor(o, o, psum[4 + 2 * t + d][:], ALU.add)
                ins.then_inc(y_read, 1)
                dve.wait_ge(f_ss, 4 * half + 2)
                nc.vector.tensor_scalar(st[:, 1, :], st[:, 0, :], 1.0 / D, EPS, ALU.mult, ALU.add).then_inc(f_ss, 1)
                dve.wait_ge(f_ss, 4 * half + 4)
                link(dve, "dve", nc.vector.reciprocal(st[:, 2, :], st[:, 2, :]))
                link(dve, "dve", nc.vector.tensor_tensor(st[:, 3, :], st[:, 2, :], st[:, 2, :], ALU.mult))
                link(dve, "dve", nc.vector.tensor_tensor(st[:, 3, :], st[:, 3, :], st[:, 1, :], ALU.mult))
                link(dve, "dve", nc.vector.tensor_scalar(st[:, 3, :], st[:, 3, :], -0.5, 1.5, ALU.mult, ALU.add))
                link(dve, "dve", nc.vector.tensor_tensor(st[:, 4, :], st[:, 3, :], st[:, 2, :], ALU.mult))
                dve.wait_ge(f_g, 16 * (half + 1))
                for t in range(2):
                    nc.vector.scalar_tensor_tensor(out=hh[:, t, :], in0=hh[:, t, :], scalar=st[:, 4, t:t + 1], in1=gf,
                                                   op0=ALU.mult, op1=ALU.mult).then_inc(f_sq, 1)

            @block.scalar
            def _(act):
                act.wait_ge(y_read, half + 1)
                for t in range(2):
                    nc.scalar.activation(sq, hh[:, t, :], ACT.Square, accum_out=st[:, 0, t:t + 1]).then_inc(f_ss, 1)
                    act.wait_ge(f_ss, 4 * half + t + 1)
                act.wait_ge(f_ss, 4 * half + 3)
                nc.scalar.activation(st[:, 2, :], st[:, 1, :], ACT.Sqrt).then_inc(f_ss, 1)
        stage.close()
    peer.close()
    top.close()


def _lay_out(a):
    f = {k: np.asarray(v) for k, v in a.items()}
    for k in f:
        if k not in ("x", "mem", "final_norm_g"):
            f[k] = f[k][0]
    w_in = f["w_in"]
    c1 = 2 * GH * GDK + GH * GDV
    c3 = c1 + GH * GDV
    dense = np.concatenate([w_in[:, :c3], w_in[:, c3 + LOWRANK:], f["w_out"], f["w_xq"], f["w_xkv"], f["w_xo"],
                            f["peer_w_q"]], axis=1)
    cols = lambda v: v.reshape(-1, P).T
    conv = f["gla_conv_w"].reshape(CONV, CONV_BLOCKS, P).transpose(2, 1, 0).reshape(P, -1)
    vec = np.concatenate([cols(f["mix_norm_g"]), cols(f["xattn_norm_g"]), cols(f["mem_norm_g"]),
                          cols(f["ffn_norm_g"]), conv, cols(f["gla_gate_b"]), cols(f["gla_out_norm_g"]),
                          cols(f["sb_out_norm_g"])], axis=1)
    r = np.arange(P)
    const = np.zeros((P, NCONST), np.float32)
    const[:, C_ID:C_ID + P] = np.eye(P)
    const[:, C_ONES:C_ONES + P] = 1
    const[:, C_TRI:C_TRI + P] = r[:, None] >= r[None, :]
    const[:, C_IOTA16:C_IOTA16 + TOPK] = np.arange(TOPK)[None, :]
    masks = [np.eye(P, dtype=bool)]
    key, query = r[:, None], r[None, :]
    for b in LEVELS:
        masks.append((key // (2 * b) == query // (2 * b)) & (key % (2 * b) < b) & (query % (2 * b) >= b))
    out = {
        "x": f["x"].reshape(TB, P, D).transpose(1, 0, 2),
        "mem": f["mem"].reshape(MB, P, D).transpose(1, 0, 2),
        "w_tiles": dense.reshape(DC, P, 4 * NQUADS, P).transpose(1, 2, 0, 3),
        "w_low": w_in[:, c3:c3 + LOWRANK].reshape(DC, P, LOWRANK).transpose(1, 0, 2),
        "gate_w": f["gla_gate_w"],
        "vec": vec,
        "const": const,
        "iota": np.broadcast_to(r.astype(np.float32), (P, P)),
        "masks": np.stack(masks, axis=1).astype(np.uint32),
        "keys": f["peer_sub_keys"].reshape(HP, NKEYS, P).transpose(2, 0, 1),
        "u_tiles": f["peer_u"].reshape(NKEYS, NKEYS, DC, P).transpose(1, 3, 2, 0),
        "v": f["peer_v"].reshape(NKEYS, NKEYS, D),
        "final_g": f["final_norm_g"],
    }
    return {k: np.ascontiguousarray(v) for k, v in out.items()}


def kernel(**inputs):
    import concourse.bacc as bacc
    from concourse.bass_utils import run_bass_kernel_spmd

    arrays = _lay_out(inputs)
    nc = bacc.Bacc("TRN2", target_bir_lowering=False, num_devices=1)
    A = {k: nc.dram_tensor("in_" + k, v.shape, mybir.dt.from_np(v.dtype), kind="ExternalInput").ap()
         for k, v in arrays.items()}
    out = nc.dram_tensor("out_0", [P, TB, D], F32, kind="ExternalOutput").ap()
    layer(nc, A, out)
    r = run_bass_kernel_spmd(nc, [{"in_" + k: v for k, v in arrays.items()}], core_ids=[0])
    return r.results[0]["out_0"].transpose(1, 0, 2).reshape(1, T, D)
```

```python
from contextlib import ExitStack

import numpy as np
import concourse.bass as bass
from concourse import mybir

F32 = mybir.dt.float32
F32R = mybir.dt.float32r
U32 = mybir.dt.uint32
ALU = mybir.AluOpType
ACT = mybir.ActivationFunctionType
AX = mybir.AxisListType

P = 128
D = 1024
DC = D // P
T = 512
TB = T // P
M = 256
MB = M // P
EPS = 1e-6

GH, GDK, GDV, LOWRANK = 4, 64, 128, 16
GATE_NORM = 16.0
CONV = 4
CONV_BLOCKS = (2 * GH * GDK + GH * GDV) // P
SH, SD = 8, 64
XH, XD = 4, 256
PH, NKEYS, TOPK = 8, 128, 16
HP = 2 * PH
SLOTS = PH * TOPK
HALF = T // 2
NEG = -3.0e38

LEVELS = [64, 32, 16, 8, 4, 2, 1]

Q_CONV, Q_OG, Q_SBQ, Q_SBK, Q_SBV, Q_OUT, Q_XK, Q_XV, Q_XQ, Q_XO, Q_PQ = 0, 2, 3, 4, 5, 6, 8, 10, 12, 14, 16
NQUADS = 20
NTILES = 4 * NQUADS
RAW, SPLIT = 4, 8

V_MIX, V_XA, V_MEM, V_FFN, V_CONV, V_GATEB, V_GLAG, V_SBG = 0, 8, 16, 24, 32, 64, 66, 67
NVEC = 71

C_ID, C_ONES, C_TRI, C_IOTA16 = 0, 128, 256, 384
NCONST = 400

SOFF = [0, 512, 896, 1152]
SLEN = [512, 384, 256, 128]
STOT = 1280


class Counts:

    def __init__(self):
        self.full = 0
        self.act = 0
        self.dve = 0
        self.chain = {}


class Groups:

    def __init__(self, counts, plan, banks=8):
        self.banks, self.at, self.value, self.who = banks, {}, [], []
        self.base = counts.full
        for n, (name, who) in enumerate(plan):
            assert name not in self.at
            self.at[name] = n
            if who == "act":
                counts.act += 1
                self.value.append(counts.act)
            else:
                counts.dve += 1
                self.value.append(counts.dve)
            self.who.append(who)
        counts.full += len(plan)

    def bank(self, name):
        return self.at[name] % self.banks

    def full(self, name):
        return self.base + self.at[name] + 1

    def read(self, name):
        n = self.at[name]
        return self.who[n], self.value[n]

    def before(self, name):
        n = self.at[name] - self.banks
        return None if n < 0 else (self.who[n], self.value[n])


def layer(nc, A, out):
    top = ExitStack()

    def sem(name):
        return top.enter_context(nc.semaphore(name))

    def sb(stack, name, shape, dt=F32):
        return stack.enter_context(nc.sbuf_tensor(name, shape, dt))

    psum_full = sem("psum_full")
    act_evac = sem("act_evac")
    dve_evac = sem("dve_evac")
    evac = {"act": act_evac, "dve": dve_evac}
    act_chain, dve_chain, pool_chain = sem("act_chain"), sem("dve_chain"), sem("pool_chain")
    tile_loaded = [sem(f"tile_loaded{s}") for s in range(RAW)]
    w_hi_done, w_split = sem("w_tile_hi"), sem("w_tile_split")
    small_loaded = sem("small_loaded")
    stored = sem("stored")
    C = Counts()
    loads = [0]
    steps = {"act": 0, "dve": 0, "pool": 0}
    chains = {"act": act_chain, "dve": dve_chain, "pool": pool_chain}

    def link(eng, who, ins):
        steps[who] += 1
        ins.then_inc(chains[who], 1)
        eng.wait_ge(chains[who], steps[who])

    psum = [top.enter_context(nc.psum_tensor(f"bank{b}", [P, 512], F32)) for b in range(8)]
    iota_t = sb(top, "iota", [P, P])
    slot_t = sb(top, "slot_t", [P, 3, T])
    main = ExitStack()
    const = sb(main, "const", [P, NCONST])
    vec = sb(main, "vec", [P, NVEC])
    act_t = sb(main, "act_t", [P, DC, T])
    ident = const[:, C_ID:C_ID + P]
    ones = const[:, C_ONES:C_ONES + P]
    tri = const[:, C_TRI:C_TRI + P]
    iota = iota_t[:]
    iota16 = const[:, C_IOTA16:C_IOTA16 + TOPK]
    h_scratch = nc.dram_tensor("h_scratch", [P, TB, D], F32, kind="Internal").ap()

    xf_scratch = nc.dram_tensor("xf_scratch", [P, 2, DC, HALF], F32, kind="Internal").ap()
    h = sb(main, "h", [P, TB, D])
    w_raw = sb(main, "w_raw", [P, RAW, DC, P])
    tile_last = {}

    def load_tile(sp, n):
        if n >= NTILES:
            return
        if n >= RAW:
            sp.wait_ge(w_split, n - RAW + 1)
        sp.dma_start(w_raw[:, n % RAW], A["w_tiles"][:, n]).then_inc(tile_loaded[n % RAW], 16)

    def load_tiles(sp, a, b):
        for n in range(a, b):
            load_tile(sp, n + RAW)

    def tile_hi(act, w, n, first):
        act.wait_ge(tile_loaded[n % RAW], 16 * (n // RAW + 1))
        if n - SPLIT >= first:
            act.wait_ge(psum_full, tile_last[n - SPLIT])
        nc.scalar.activation(w[0][:, n % SPLIT], w_raw[:, n % RAW], ACT.Identity).then_inc(w_hi_done, 1)

    def tile_lo(queue, w, n, engine=nc.vector):
        queue.wait_ge(w_hi_done, n + 1)
        engine.tensor_tensor(w[1][:, n % SPLIT], w_raw[:, n % RAW], w[0][:, n % SPLIT].bitcast(F32),
                                ALU.subtract).then_inc(w_split, 1)

    def pair(stack, name, shape):
        return sb(stack, name + "_hi", shape, F32R), sb(stack, name + "_lo", shape, F32R)

    def opened(pe, g, name):
        old = g.before(name)
        if old:
            pe.wait_ge(evac[old[0]], old[1])
        return psum[g.bank(name)]

    def wait_read(eng, g, name):
        who, value = g.read(name)
        eng.wait_ge(evac[who], value)

    x_block = [sem(f"x_block{t}") for t in range(TB)]
    ssq = sb(main, "ssq", [P, TB])

    with nc.Block() as block:
        @block.sync
        def _(sp):
            for t in range(TB):
                sp.dma_start(h[:, t], A["x"][:, t]).then_inc(x_block[t], 16)
            sp.dma_start(const[:], A["const"]).then_inc(small_loaded, 16)
            sp.dma_start(iota_t[:], A["iota"]).then_inc(small_loaded, 16)
            sp.dma_start(vec[:], A["vec"]).then_inc(small_loaded, 16)
            for n in range(RAW):
                load_tile(sp, n)
            sp.wait_ge(small_loaded, 48)
    loads[0] = 48

    def norm_transpose(name, src, nt, width, gain_at, dst, chunk0=0, parts=None, summed=None, loaded=None):
        nc_chunks = width // P
        stack = ExitStack()
        sq = sb(stack, name + "_sq", [P, width])
        stat = sb(stack, name + "_stat", [P, 5, nt])
        xs = sb(stack, name + "_xs", [P, nt, width])
        total = stat[:, 0, :] if summed is None else summed
        a_sum, a_sqrt, d_scaled = sem(name + "_sum"), sem(name + "_sqrt"), sem(name + "_scaled")
        a_hi, d_lo = sem(name + "_hi_done"), sem(name + "_lo_done")
        plan = [((t, c), "dve") for t in range(nt) for c in range(0, nc_chunks, 4)]
        g = Groups(C, plan)
        sums = nt if summed is None else 0
        with nc.Block() as block:
            @block.scalar
            def _(act):
                if summed is None:
                    for t in range(nt):
                        if loaded:
                            act.wait_ge(loaded[t], 16)
                        if t:
                            act.wait_ge(a_sum, t)
                        nc.scalar.activation(sq[:], src[:, t, :], ACT.Square,
                                             accum_out=stat[:, 0, t:t + 1]).then_inc(a_sum, 1)
                act.wait_ge(a_sum, sums + 1)
                nc.scalar.activation(stat[:, 2, :], stat[:, 1, :], ACT.Sqrt).then_inc(a_sqrt, 1)
                if parts:
                    for t in range(nt):
                        wait_read(act, g, (t, nc_chunks - 4))
                        cols = slice(t * P, (t + 1) * P)
                        nc.scalar.activation(parts[0][:, :, cols], dst[:, :, cols], ACT.Identity).then_inc(a_hi, 1)

            @block.vector
            def _(dve):
                if sums:
                    dve.wait_ge(a_sum, sums)
                nc.vector.tensor_scalar(stat[:, 1, :], total, 1.0 / width, EPS, ALU.mult,
                                        ALU.add).then_inc(a_sum, 1)
                dve.wait_ge(a_sqrt, 1)
                link(dve, "dve", nc.vector.reciprocal(stat[:, 2, :], stat[:, 2, :]))
                link(dve, "dve", nc.vector.tensor_tensor(stat[:, 3, :], stat[:, 2, :], stat[:, 2, :], ALU.mult))
                link(dve, "dve", nc.vector.tensor_tensor(stat[:, 3, :], stat[:, 3, :], stat[:, 1, :], ALU.mult))
                link(dve, "dve", nc.vector.tensor_scalar(stat[:, 3, :], stat[:, 3, :], -0.5, 1.5, ALU.mult, ALU.add))
                link(dve, "dve", nc.vector.tensor_tensor(stat[:, 4, :], stat[:, 3, :], stat[:, 2, :], ALU.mult))

                def scale(t):
                    nc.vector.tensor_scalar(xs[:, t, :], src[:, t, :], stat[:, 4, t:t + 1], None,
                                            ALU.mult).then_inc(d_scaled, 1)
                def low_part(t):
                    cols = slice(t * P, (t + 1) * P)
                    dve.wait_ge(a_hi, t + 1)
                    nc.vector.tensor_tensor(parts[1][:, :, cols], dst[:, :, cols], parts[0][:, :, cols].bitcast(F32),
                                            ALU.subtract).then_inc(d_lo, 1)
                scale(0)
                for t in range(nt):
                    if t + 1 < nt:
                        scale(t + 1)
                    for c in range(0, nc_chunks, 4):
                        dve.wait_ge(psum_full, g.full((t, c)))
                        gain = vec[:, gain_at + c:gain_at + c + 4].unsqueeze(2).to_broadcast([P, 4, P])
                        nc.vector.tensor_tensor(
                            dst[:, chunk0 + c:chunk0 + c + 4, t * P:(t + 1) * P],
                            psum[g.bank((t, c))][:].rearrange("p (c t) -> p c t", c=4), gain,
                            ALU.mult).then_inc(dve_evac, 1)
                    if parts and t >= 1:
                        low_part(t - 1)
                if parts:
                    low_part(nt - 1)

            @block.tensor
            def _(pe):
                for t in range(nt):
                    pe.wait_ge(d_scaled, t + 1)
                    for c in range(0, nc_chunks, 4):
                        bank = opened(pe, g, (t, c))
                        for k in range(4):
                            last = nc.tensor.transpose(bank[:, k * P:(k + 1) * P],
                                                       xs[:, t, (c + k) * P:(c + k + 1) * P], ident)
                        last.then_inc(psum_full, 1)
        stack.close()

    def three(bank, lhs, rhs, start, stop):
        nc.tensor.matmul(bank, lhs(1), rhs(0), start=start, stop=False)
        nc.tensor.matmul(bank, lhs(0), rhs(1), start=False, stop=False)
        return nc.tensor.matmul(bank, lhs(0), rhs(0), start=False, stop=stop)

    def projected(pe, g, name, w, tile, x, n):
        bank = opened(pe, g, name)
        pe.wait_ge(w_split, tile + 1)
        for c in range(DC):
            last = three(bank[:, 0:n], lambda s: w[s][:, tile % SPLIT, c, :], lambda s: x[s][:, c, :], c == 0, c == DC - 1)
        last.then_inc(psum_full, 1)

    def projected_natural(pe, g, name, w, q, x, t):
        bank = opened(pe, g, name)
        pe.wait_ge(w_split, 4 * q + 4)
        e = 4 * q % SPLIT
        for c in range(DC):
            last = three(bank[:], lambda s: x[s][:, c, t * P:(t + 1) * P], lambda s: w[s][:, e:e + 4, c, :],
                         c == 0, c == DC - 1)
        last.then_inc(psum_full, 1)

    dense = ExitStack()
    zg = sb(dense, "zg", [P, 2, T])
    og = sb(dense, "og", [P, TB, GH * GDV])
    s_q = sb(dense, "s_q", [P, SH // 2, T])
    s_k = sb(dense, "s_k", [P, SH // 2, T])
    s_v = sb(dense, "s_v", [P, TB, SH * SD])
    mixer = dense
    stage = ExitStack()
    x2 = pair(stage, "xn", [P, DC, T])
    norm_transpose("nx", h, TB, D, V_MIX, act_t, parts=x2, loaded=x_block)
    w = pair(stage, "w_in", [P, SPLIT, DC, P])

    qkv = act_t
    w_low = sb(stage, "w_low", [P, DC, LOWRANK])
    gate_w = sb(stage, "gate_w", [LOWRANK, 2 * P])
    low = sb(stage, "low", [LOWRANK, T])
    conv = sb(stage, "conv", [P, 2, T])
    conv_done, conv_silu = sem("conv_done"), sem("conv_silu")
    plan = [("low", "act")] + [(("conv", n), "dve") for n in range(4)] + [("gate0", "act"), ("gate1", "act")]
    plan += [(("conv", n), "dve") for n in range(4, CONV_BLOCKS)]
    plan += [(("og", t), "act") for t in range(TB)]
    plan += [(("sq", n), "act") for n in range(4)] + [(("sk", n), "dve") for n in range(4)]
    plan += [(("sv", t), "dve") for t in range(TB)]
    g = Groups(C, plan)
    for n in range(4):
        for q in range(2):
            tile_last[4 * (Q_CONV + q) + n] = g.full(("conv", 4 * q + n))
        for q, name in ((Q_OG, ("og", 3)), (Q_SBQ, ("sq", n)), (Q_SBK, ("sk", n)), (Q_SBV, ("sv", 3))):
            tile_last[4 * q + n] = g.full(name)
    with nc.Block() as block:
        @block.sync
        def _(sp):
            sp.dma_start(w_low[:], A["w_low"]).then_inc(small_loaded, 16)
            sp.dma_start(gate_w[:], A["gate_w"]).then_inc(small_loaded, 16)
            load_tiles(sp, 0, 4 * Q_OUT)

        @block.tensor
        def _(pe):
            pe.wait_ge(small_loaded, loads[0] + 32)
            bank = opened(pe, g, "low")
            for c in range(DC):
                last = nc.tensor.matmul(bank[0:LOWRANK, :], w_low[:, c, :], act_t[:, c, :],
                                        start=(c == 0), stop=(c == DC - 1))
            last.then_inc(psum_full, 1)
            for n in range(4):
                projected(pe, g, ("conv", n), w, n, x2, T)
            wait_read(pe, g, "low")
            for n in range(2):
                bank = opened(pe, g, f"gate{n}")
                nc.tensor.matmul(bank[:], gate_w[:, n * P:(n + 1) * P], low[:], start=True,
                                 stop=True).then_inc(psum_full, 1)
            for n in range(4, CONV_BLOCKS):
                projected(pe, g, ("conv", n), w, n, x2, T)
            for t in range(TB):
                projected_natural(pe, g, ("og", t), w, Q_OG, x2, t)
            for q, name in ((Q_SBQ, "sq"), (Q_SBK, "sk")):
                for n in range(4):
                    projected(pe, g, (name, n), w, 4 * q + n, x2, T)
            for t in range(TB):
                projected_natural(pe, g, ("sv", t), w, Q_SBV, x2, t)

        @block.vector
        def _(dve):
            for n in range(SPLIT):
                tile_lo(dve, w, n)
            for n in range(CONV_BLOCKS):
                tap = lambda k: vec[:, V_CONV + n * CONV + k:V_CONV + n * CONV + k + 1]
                y, x = conv[:, n % 2, :], psum[g.bank(("conv", n))]
                if n >= 2:
                    dve.wait_ge(conv_silu, n - 1)
                dve.wait_ge(psum_full, g.full(("conv", n)))
                link(dve, "dve", nc.vector.tensor_scalar(y, x[:], tap(CONV - 1), None, ALU.mult))
                for back in range(1, CONV - 1):
                    link(dve, "dve", nc.vector.scalar_tensor_tensor(
                        out=y[:, back:], in0=x[:, 0:T - back], scalar=tap(CONV - 1 - back), in1=y[:, back:],
                        op0=ALU.mult, op1=ALU.add))
                back = CONV - 1
                nc.vector.scalar_tensor_tensor(out=y[:, back:], in0=x[:, 0:T - back], scalar=tap(0), in1=y[:, back:],
                                               op0=ALU.mult, op1=ALU.add).then_inc(dve_evac, 1)
                tile_lo(dve, w, n + SPLIT)
            for n in range(4 * Q_SBK, 4 * Q_OUT):
                tile_lo(dve, w, n)
            for n in range(4):
                dve.wait_ge(psum_full, g.full(("sk", n)))
                nc.vector.tensor_copy(s_k[:, n, :], psum[g.bank(("sk", n))][:]).then_inc(dve_evac, 1)
            for t in range(TB):
                dve.wait_ge(psum_full, g.full(("sv", t)))
                nc.vector.tensor_copy(s_v[:, t, :], psum[g.bank(("sv", t))][:]).then_inc(dve_evac, 1)

        @block.scalar
        def _(act):
            for n in range(SPLIT):
                tile_hi(act, w, n, 0)
            act.wait_ge(psum_full, g.full("low"))
            nc.scalar.activation(low[:], psum[g.bank("low")][0:LOWRANK, :], ACT.Identity).then_inc(act_evac, 1)
            for n in range(CONV_BLOCKS):
                if n == 4:
                    for m in range(2):
                        act.wait_ge(psum_full, g.full(f"gate{m}"))
                        nc.scalar.activation(zg[:, m, :], psum[g.bank(f"gate{m}")][:], ACT.Identity,
                                             bias=vec[:, V_GATEB + m:V_GATEB + m + 1]).then_inc(act_evac, 1)
                wait_read(act, g, ("conv", n))
                nc.scalar.activation(qkv[:, n, :], conv[:, n % 2, :], ACT.Silu).then_inc(conv_silu, 1)
                tile_hi(act, w, n + SPLIT, 0)
            for t in range(TB):
                act.wait_ge(psum_full, g.full(("og", t)))
                nc.scalar.activation(og[:, t, :], psum[g.bank(("og", t))][:], ACT.Silu).then_inc(act_evac, 1)
            for n in range(4 * Q_SBK, 4 * Q_SBV):
                tile_hi(act, w, n, 0)
            for n in range(4):
                act.wait_ge(psum_full, g.full(("sq", n)))
                nc.scalar.activation(s_q[:, n, :], psum[g.bank(("sq", n))][:], ACT.Identity,
                                     scale=float(SD) ** -0.5).then_inc(act_evac, 1)
                tile_hi(act, w, 4 * Q_SBV + n, 0)
    loads[0] += 32
    stage.close()

    stage = ExitStack()
    masks = sb(stage, "masks", [P, len(LEVELS) + 1, P], U32)
    cum = sb(stage, "cum", [P, 2, TB, P])
    lv_e = sb(stage, "lv_e", [P, 2, 2 * T])
    lv_q = sb(stage, "lv_q", [P, 2, 2, T])
    lv_k = sb(stage, "lv_k", [P, 2, 2, T])
    q_s = sb(stage, "q_s", [P, 2, T])
    q_in = sb(stage, "q_in", [P, 2, T])
    k_dec = sb(stage, "k_dec", [P, 2, T])
    k_nat = sb(stage, "k_nat", [P, 2, TB, P])
    dec = sb(stage, "dec", [P, 2, TB])
    v_nat = sb(stage, "v_nat", [P, TB, GH * GDV])
    scores = sb(stage, "scores", [P, GH, TB, P])
    state = sb(stage, "state", [P, 2, 2, GDV])
    o_gla = sb(stage, "o_gla", [P, TB, GH * GDV])
    gst = sb(stage, "gst", [P, 5, TB * GH])
    tmp = lv_e[:].rearrange("p a b -> p (a b)")
    NL = len(LEVELS)
    names = ["gl_mask", "gl_abs", "gl_ln", "gl_cum", "gl_diff", "gl_exp", "gl_fac", "gl_qin", "gl_kdiff",
             "gl_kexp", "gl_kdec", "gl_sq", "gl_var", "gl_sqrt", "gl_on", "gl_clear", "gl_qs", "gl_decay", "gl_scored"]
    S = {n: sem(n) for n in names}
    plan = [(("vt", x), "act") for x in range(GH)]
    plan += [(("lv", 0, x), "dve") for x in range(GH)]
    plan += [(("kt", x), "act") for x in range(2)]
    plan += [(("lv", l, x), "dve") for l in range(1, NL + 1) for x in range(GH)]
    for t in range(TB):
        plan += [(("o", t, y), "act") for y in range(2)]
        if t < TB - 1:
            plan += [(("st", t), "dve")]
    plan += [(("gt", x), "act") for x in range(GH)]
    g = Groups(C, plan)
    with nc.Block() as block:
        @block.sync
        def _(sp):
            sp.dma_start(masks[:], A["masks"]).then_inc(small_loaded, 16)

        @block.scalar
        def _(act):
            z = zg[:].rearrange("p a b -> p (a b)")
            z2 = lv_q[:, 0].rearrange("p a b -> p (a b)")
            link(act, "act", nc.scalar.activation(z2, z, ACT.Abs))
            link(act, "act", nc.scalar.activation(z2, z2, ACT.Exp, scale=-1.0))
            nc.scalar.activation(z2, z2, ACT.Ln, bias=1.0).then_inc(S["gl_ln"], 1)
            act.wait_ge(S["gl_cum"], 1)
            cf = cum[:].rearrange("p a b c -> p (a b c)")
            nc.scalar.activation(tmp[:, 0:2 * T], cf, ACT.Exp).then_inc(S["gl_exp"], 1)
            nc.scalar.activation(dec[:], cum[:, :, :, P - 1], ACT.Exp).then_inc(S["gl_decay"], 1)
            act.wait_ge(S["gl_kdiff"], 1)
            nc.scalar.activation(tmp[:, 2 * T:4 * T], tmp[:, 2 * T:4 * T], ACT.Exp, scale=-1.0).then_inc(S["gl_kexp"], 1)
            for x in range(GH):
                act.wait_ge(psum_full, g.full(("vt", x)))
                nc.scalar.activation(v_nat[:, :, x * GDV:(x + 1) * GDV],
                                     psum[g.bank(("vt", x))][:].rearrange("p (t d) -> p t d", t=TB),
                                     ACT.Identity).then_inc(act_evac, 1)
            for x in range(2):
                act.wait_ge(psum_full, g.full(("kt", x)))
                nc.scalar.activation(k_nat[:, x], psum[g.bank(("kt", x))][:].rearrange("p (t d) -> p t d", t=TB),
                                     ACT.Identity).then_inc(act_evac, 1)
            for l in range(NL):
                act.wait_ge(S["gl_diff"], l + 1)
                nc.scalar.activation(lv_e[:, l % 2], lv_e[:, l % 2], ACT.Exp).then_inc(S["gl_exp"], 1)
            for t in range(TB):
                for y in range(2):
                    act.wait_ge(psum_full, g.full(("o", t, y)))
                    nc.scalar.activation(o_gla[:, t, :].rearrange("p (x y d) -> p x y d", y=2, d=GDV)[:, :, y, :],
                                         psum[g.bank(("o", t, y))][:, 0:2 * GDV].rearrange("p (x d) -> p x d", x=2),
                                         ACT.Identity).then_inc(act_evac, 1)
            wait_read(act, g, ("o", TB - 1, 1))
            act.wait_ge(S["gl_fac"], 2 * NL)
            nc.scalar.activation(tmp[:, 0:4 * T], o_gla[:].rearrange("p a b -> p (a b)"),
                                 ACT.Square).then_inc(S["gl_sq"], 1)
            act.wait_ge(S["gl_var"], 1)
            nc.scalar.activation(gst[:, 2, :], gst[:, 1, :], ACT.Sqrt).then_inc(S["gl_sqrt"], 1)
            for x in range(GH):
                act.wait_ge(psum_full, g.full(("gt", x)))
                nc.scalar.activation(act_t[:, x, :], psum[g.bank(("gt", x))][:], ACT.Identity,
                                     scale=vec[:, V_GLAG:V_GLAG + 1]).then_inc(act_evac, 1)

        @block.vector
        def _(dve):
            link(dve, "dve", nc.vector.memset(lv_k[:], 0.0))
            nc.vector.memset(lv_q[:, 1], 0.0)
            nc.vector.memset(scores[:], 0.0).then_inc(S["gl_clear"], 1)
            nc.vector.tensor_scalar(q_s[:], qkv[:, 0:2, :], float(GDK) ** -0.5, None, ALU.mult).then_inc(S["gl_qs"], 1)
            dve.wait_ge(S["gl_ln"], 1)
            zf = zg[:].rearrange("p a b -> p (a b)")
            z2 = lv_q[:, 0].rearrange("p a b -> p (a b)")
            link(dve, "dve", nc.vector.scalar_tensor_tensor(out=zf, in0=zf, scalar=0.0, in1=z2,
                                                            op0=ALU.min, op1=ALU.subtract))
            link(dve, "dve", nc.vector.tensor_scalar(zf, zf, 1.0 / GATE_NORM, None, ALU.mult))
            nc.vector.memset(lv_q[:, 0], 0.0)
            for x in range(2):
                for t in range(TB):
                    last = nc.vector.tensor_tensor_scan(cum[:, x, t, :], ones, zg[:, x, t * P:(t + 1) * P], 0.0,
                                                        ALU.mult, ALU.add)
            last.then_inc(S["gl_cum"], 1)
            dve.wait_ge(S["gl_cum"], 1)
            cb = cum[:].rearrange("p a b c -> p (a b) c")
            nc.vector.tensor_tensor(tmp[:, 2 * T:4 * T].rearrange("p (a c) -> p a c", c=P), cb,
                                    cb[:, :, P - 1:P].to_broadcast([P, 2 * TB, P]),
                                    ALU.subtract).then_inc(S["gl_kdiff"], 1)
            qf = lambda a: a.rearrange("p a b -> p (a b)")
            dve.wait_ge(S["gl_exp"], 1)
            dve.wait_ge(S["gl_qs"], 1)
            nc.vector.tensor_tensor(qf(q_in[:]), qf(q_s[:]), tmp[:, 0:2 * T], ALU.mult).then_inc(S["gl_qin"], 1)
            dve.wait_ge(S["gl_kexp"], 1)
            nc.vector.tensor_tensor(qf(k_dec[:]), qf(qkv[:, 2:4, :]), tmp[:, 2 * T:4 * T],
                                    ALU.mult).then_inc(S["gl_kdec"], 1)
            dve.wait_ge(S["gl_kdec"], 1)
            dve.wait_ge(S["gl_qin"], 1)
            dve.wait_ge(small_loaded, loads[0] + 16)

            def halves(a, half):
                return a.rearrange("p (n b) -> p n b", b=2 * half)

            def diff(l):
                half = LEVELS[l]
                n = 2 * T // (2 * half)
                c = halves(cum[:].rearrange("p a b c -> p (a b c)"), half)
                e = halves(lv_e[:, l % 2], half)
                edge = c[:, :, half - 1:half].to_broadcast([P, n, half])
                nc.vector.tensor_tensor(e[:, :, half:], c[:, :, half:], edge, ALU.subtract)
                nc.vector.tensor_tensor(e[:, :, 0:half], edge, c[:, :, 0:half], ALU.subtract).then_inc(S["gl_diff"], 1)

            def factors(l):
                half = LEVELS[l]
                e = halves(lv_e[:, l % 2], half)
                if l >= 2:
                    dve.wait_ge(psum_full, g.full(("lv", l - 1, GH - 1)))
                dve.wait_ge(S["gl_exp"], l + 2)
                nc.vector.tensor_tensor(halves(qf(lv_q[:, l % 2]), half)[:, :, half:],
                                        halves(qf(q_s[:]), half)[:, :, half:], e[:, :, half:],
                                        ALU.mult).then_inc(S["gl_fac"], 1)
                nc.vector.tensor_tensor(halves(qf(lv_k[:, l % 2]), half)[:, :, 0:half],
                                        halves(qf(qkv[:, 2:4, :]), half)[:, :, 0:half], e[:, :, 0:half],
                                        ALU.mult).then_inc(S["gl_fac"], 1)
                dve.wait_ge(S["gl_fac"], 2 * l + 2)

            def keep(l):
                for x in range(GH):
                    dve.wait_ge(psum_full, g.full(("lv", l, x)))
                    nc.vector.copy_predicated(
                        scores[:, x], masks[:, l, :].unsqueeze(1).to_broadcast([P, TB, P]),
                        psum[g.bank(("lv", l, x))][:].rearrange("p (t c) -> p t c", t=TB)).then_inc(dve_evac, 1)
                dve.wait_ge(dve_evac, g.read(("lv", l, GH - 1))[1])

            diff(0)
            for l in range(NL):
                if l + 1 < NL:
                    diff(l + 1)
                factors(l)
                keep(l)
            keep(NL)
            nc.vector.engine_nop().then_inc(S["gl_scored"], 1)
            dve.wait_ge(S["gl_decay"], 1)
            for t in range(TB - 1):
                dve.wait_ge(psum_full, g.full(("st", t)))
                b = psum[g.bank(("st", t))]
                for x in range(2):
                    for y in range(2):
                        r = slice(GDK * y, GDK * y + GDK)
                        new = state[r, t % 2, x, :]
                        add = b[r, 2 * x * GDV + y * GDV:2 * x * GDV + (y + 1) * GDV]
                        if t == 0:
                            last = nc.vector.tensor_copy(new, add)
                        else:
                            last = nc.vector.scalar_tensor_tensor(out=new, in0=state[r, (t - 1) % 2, x, :],
                                                                  scalar=dec[r, x, t:t + 1], in1=add,
                                                                  op0=ALU.mult, op1=ALU.add)
                last.then_inc(dve_evac, 1)
                dve.wait_ge(dve_evac, g.read(("st", t))[1])
            dve.wait_ge(S["gl_sq"], 1)
            link(dve, "dve", nc.vector.reduce_sum(gst[:, 0, :], tmp[:, 0:4 * T].rearrange("p (n d) -> p n d", d=GDV),
                                                  axis=AX.X))
            nc.vector.tensor_scalar(gst[:, 1, :], gst[:, 0, :], 1.0 / GDV, EPS, ALU.mult, ALU.add).then_inc(S["gl_var"], 1)
            dve.wait_ge(S["gl_sqrt"], 1)
            link(dve, "dve", nc.vector.reciprocal(gst[:, 2, :], gst[:, 2, :]))
            link(dve, "dve", nc.vector.tensor_tensor(gst[:, 3, :], gst[:, 2, :], gst[:, 2, :], ALU.mult))
            link(dve, "dve", nc.vector.tensor_tensor(gst[:, 3, :], gst[:, 3, :], gst[:, 1, :], ALU.mult))
            link(dve, "dve", nc.vector.tensor_scalar(gst[:, 3, :], gst[:, 3, :], -0.5, 1.5, ALU.mult, ALU.add))
            link(dve, "dve", nc.vector.tensor_tensor(gst[:, 4, :], gst[:, 3, :], gst[:, 2, :], ALU.mult))
            of = o_gla[:].rearrange("p t (x d) -> p (t x) d", d=GDV)
            link(dve, "dve", nc.vector.tensor_tensor(of, of, gst[:, 4, :].unsqueeze(2).to_broadcast([P, TB * GH, GDV]),
                                                     ALU.mult))
            nc.vector.tensor_tensor(o_gla[:], o_gla[:], og[:], ALU.mult).then_inc(S["gl_on"], 1)

        @block.tensor
        def _(pe):
            for x in range(GH):
                bank = opened(pe, g, ("vt", x))
                for t in range(TB):
                    last = nc.tensor.transpose(bank[:, t * P:(t + 1) * P], qkv[:, 4 + x, t * P:(t + 1) * P], ident)
                last.then_inc(psum_full, 1)

            def level(l, q, k):
                for x in range(GH):
                    bank = opened(pe, g, ("lv", l, x))
                    r = slice(GDK * (x % 2), GDK * (x % 2) + GDK)
                    for t in range(TB):
                        c = slice(t * P, (t + 1) * P)
                        last = nc.tensor.matmul(bank[:, c], k[r, x // 2, c], q[r, x // 2, c], start=True, stop=True)
                    last.then_inc(psum_full, 1)
            pe.wait_ge(S["gl_qs"], 1)
            level(0, q_s, qkv[:, 2:4, :])
            pe.wait_ge(S["gl_kdec"], 1)
            for x in range(2):
                bank = opened(pe, g, ("kt", x))
                for t in range(TB):
                    last = nc.tensor.transpose(bank[:, t * P:(t + 1) * P], k_dec[:, x, t * P:(t + 1) * P], ident)
                last.then_inc(psum_full, 1)
            pe.wait_ge(S["gl_clear"], 1)
            for l in range(NL):
                pe.wait_ge(S["gl_fac"], 2 * l + 2)
                level(l + 1, lv_q[:, l % 2], lv_k[:, l % 2])
            pe.wait_ge(S["gl_scored"], 1)
            pe.wait_ge(S["gl_qin"], 1)
            wait_read(pe, g, ("kt", 1))
            wait_read(pe, g, ("vt", GH - 1))
            for t in range(TB):
                if t:
                    wait_read(pe, g, ("st", t - 1))
                for y in range(2):
                    bank = opened(pe, g, ("o", t, y))
                    r = slice(GDK * y, GDK * y + GDK)
                    for x in (y, y + 2):
                        o = bank[:, (x // 2) * GDV:(x // 2 + 1) * GDV]
                        last = nc.tensor.matmul(o, scores[:, x, t, :], v_nat[:, t, x * GDV:(x + 1) * GDV],
                                                start=True, stop=(t == 0))
                        if t:
                            last = nc.tensor.matmul(o, q_in[r, x // 2, t * P:(t + 1) * P],
                                                    state[r, (t - 1) % 2, x // 2, :], start=False, stop=True)
                    last.then_inc(psum_full, 1)
                if t < TB - 1:
                    bank = opened(pe, g, ("st", t))
                    for x in range(2):
                        last = nc.tensor.matmul(bank[:, 2 * x * GDV:2 * (x + 1) * GDV], k_nat[:, x, t, :],
                                                v_nat[:, t, 2 * x * GDV:2 * (x + 1) * GDV], start=True, stop=True)
                    last.then_inc(psum_full, 1)
            pe.wait_ge(S["gl_on"], 1)
            for x in range(GH):
                bank = opened(pe, g, ("gt", x))
                for t in range(TB):
                    last = nc.tensor.transpose(bank[:, t * P:(t + 1) * P], o_gla[:, t, x * GDV:(x + 1) * GDV], ident)
                last.then_inc(psum_full, 1)
    loads[0] += 16
    stage.close()

    stage = ExitStack()
    ZR, PR, WR, LC, LP = 4, 3, 2, 2, 3
    zb = sb(stage, "zb", [P, ZR, STOT])
    sp_ = sb(stage, "sp", [P, PR, STOT])
    wb = sb(stage, "wb", [P, WR, STOT])
    o_sb = sb(stage, "o_sb", [P, TB, SH * SD])
    s_names = ["sb_ln", "sb_sp", "sb_spm", "sb_arg", "sb_w", "sb_wm"]
    S = {n: sem(n) for n in s_names}
    plan = []
    for i in range(SH + LP):
        if i < SH:
            plan += [(("z", i, s), "dve") for s in range(TB)]
        if LC <= i < SH + LC:
            plan += [(("c", i - LC, s), "dve") for s in range(TB)]
        if i >= LP:
            plan += [(("pv", i - LP), "act")]
    g = Groups(C, plan)
    with nc.Block() as block:
        @block.tensor
        def _(pe):
            for i in range(SH + LP):
                if i < SH:
                    x, r = i // 2, slice(SD * (i % 2), SD * (i % 2) + SD)
                    for s in range(TB):
                        bank = opened(pe, g, ("z", i, s))
                        nc.tensor.matmul(bank[:, 0:SLEN[s]], s_k[r, x, s * P:(s + 1) * P], s_q[r, x, s * P:T],
                                         start=True, stop=True).then_inc(psum_full, 1)
                if LC <= i < SH + LC:
                    n = i - LC
                    pe.wait_ge(S["sb_spm"], n + 1)
                    for s in range(TB):
                        bank = opened(pe, g, ("c", n, s))
                        for s2 in range(s, TB):
                            last = nc.tensor.matmul(bank[:, (s2 - s) * P:SLEN[s]], tri if s2 == s else ones,
                                                    sp_[:, n % PR, SOFF[s2]:SOFF[s2] + SLEN[s2]],
                                                    start=(s2 == s), stop=(s2 == TB - 1))
                        last.then_inc(psum_full, 1)
                if i >= LP:
                    n = i - LP
                    pe.wait_ge(S["sb_wm"], n + 1)
                    bank = opened(pe, g, ("pv", n))
                    for t in range(TB):
                        for s in range(t + 1):
                            at = SOFF[s] + (t - s) * P
                            last = nc.tensor.matmul(bank[:, t * SD:(t + 1) * SD], wb[:, n % WR, at:at + P],
                                                    s_v[:, s, n * SD:(n + 1) * SD], start=(s == 0), stop=(s == t))
                    last.then_inc(psum_full, 1)

        @block.scalar
        def _(act):
            for i in range(SH + LP):
                if i < SH:
                    wait_read(act, g, ("z", i, TB - 1))
                    if i >= PR:
                        act.wait_ge(psum_full, g.full(("c", i - PR, TB - 1)))
                    t = sp_[:, i % PR, :]
                    link(act, "act", nc.scalar.activation(t, zb[:, i % ZR, :], ACT.Abs))
                    link(act, "act", nc.scalar.activation(t, t, ACT.Exp, scale=-1.0))
                    nc.scalar.activation(t, t, ACT.Ln, bias=1.0).then_inc(S["sb_ln"], 1)
                if LC <= i < SH + LC:
                    n = i - LC
                    act.wait_ge(S["sb_arg"], n + 1)
                    nc.scalar.activation(wb[:, n % WR, :], wb[:, n % WR, :], ACT.Exp).then_inc(S["sb_w"], 1)
                if i >= LP:
                    n = i - LP
                    act.wait_ge(psum_full, g.full(("pv", n)))
                    nc.scalar.activation(o_sb[:, :, n * SD:(n + 1) * SD],
                                         psum[g.bank(("pv", n))][:, 0:TB * SD].rearrange("p (t d) -> p t d", t=TB),
                                         ACT.Identity).then_inc(act_evac, 1)

        @block.vector
        def _(dve):
            for i in range(SH + LC):
                if i < SH:
                    for s in range(TB):
                        dve.wait_ge(psum_full, g.full(("z", i, s)))
                        nc.vector.tensor_copy(zb[:, i % ZR, SOFF[s]:SOFF[s] + SLEN[s]],
                                              psum[g.bank(("z", i, s))][:, 0:SLEN[s]]).then_inc(dve_evac, 1)
                if i >= LC:
                    n = i - LC
                    if n >= WR:
                        dve.wait_ge(psum_full, g.full(("pv", n - WR)))
                    for s in range(TB):
                        o = slice(SOFF[s], SOFF[s] + SLEN[s])
                        dve.wait_ge(psum_full, g.full(("c", n, s)))
                        nc.vector.tensor_tensor(wb[:, n % WR, o], zb[:, n % ZR, o],
                                                psum[g.bank(("c", n, s))][:, 0:SLEN[s]],
                                                ALU.subtract).then_inc(dve_evac, 1)
                    dve.wait_ge(dve_evac, g.read(("c", n, TB - 1))[1])
                    nc.vector.engine_nop().then_inc(S["sb_arg"], 1)
                if i < SH:
                    dve.wait_ge(S["sb_ln"], i + 1)
                    nc.vector.scalar_tensor_tensor(out=sp_[:, i % PR, :], in0=zb[:, i % ZR, :], scalar=0.0,
                                                   in1=sp_[:, i % PR, :], op0=ALU.max,
                                                   op1=ALU.add).then_inc(S["sb_sp"], 1)

        @block.gpsimd
        def _(pool):
            def strict(buf, done):
                for s in range(TB):
                    piece = buf[:, SOFF[s]:SOFF[s] + P]
                    last = nc.gpsimd.affine_select(out=piece, in_=piece, compare_op=ALU.is_gt, fill=0.0, base=0,
                                                   pattern=[[1, P]], channel_multiplier=-1)
                last.then_inc(done, 1)
            for i in range(SH + LC):
                if i >= LC:
                    pool.wait_ge(S["sb_w"], i - LC + 1)
                    strict(wb[:, (i - LC) % WR, :], S["sb_wm"])
                if i < SH:
                    pool.wait_ge(S["sb_sp"], i + 1)
                    strict(sp_[:, i % PR, :], S["sb_spm"])
    norm_transpose("nsb", o_sb, TB, SH * SD, V_SBG, act_t, GH * GDV // P)
    stage.close()
    mixer.close()

    def add_projection(name, q0):
        stage = ExitStack()
        x = pair(stage, name + "_x", [P, DC, T])
        w = pair(stage, name + "_w", [P, SPLIT, DC, P])
        x_hi_done, x_split = sem(name + "_x_hi"), sem(name + "_x_split")
        squares, squared = sb(stage, name + "_sq", [P, D]), sem(name + "_squared")
        g = Groups(C, [((t, half), "dve") for t in range(TB) for half in range(2)])
        for n in range(8):
            tile_last[4 * q0 + n] = g.full((TB - 1, n // 4))
        with nc.Block() as block:
            @block.sync
            def _(sp):
                load_tiles(sp, 4 * q0, 4 * q0 + 8)

            @block.tensor
            def _(pe):
                for t in range(TB):
                    pe.wait_ge(x_split, t + 1)
                    for half in range(2):
                        projected_natural(pe, g, (t, half), w, q0 + half, x, t)

            @block.scalar
            def _(act):
                for t in range(TB):
                    cols = slice(t * P, (t + 1) * P)
                    nc.scalar.activation(x[0][:, :, cols], act_t[:, :, cols], ACT.Identity).then_inc(x_hi_done, 1)
                    if t < 2:
                        for n in range(4 * t, 4 * t + 4):
                            tile_hi(act, w, 4 * q0 + n, 4 * q0)
                for t in range(TB):
                    wait_read(act, g, (t, 1))
                    if t:
                        act.wait_ge(squared, t)
                    nc.scalar.activation(squares[:], h[:, t, :], ACT.Square, accum_out=ssq[:, t:t + 1]).then_inc(squared, 1)

            @block.vector
            def _(dve):
                for t in range(TB):
                    cols = slice(t * P, (t + 1) * P)
                    dve.wait_ge(x_hi_done, t + 1)
                    nc.vector.tensor_tensor(x[1][:, :, cols], act_t[:, :, cols], x[0][:, :, cols].bitcast(F32),
                                            ALU.subtract).then_inc(x_split, 1)
                    if t < 2:
                        for n in range(4 * t, 4 * t + 4):
                            tile_lo(dve, w, 4 * q0 + n)
                for t in range(TB):
                    for half in range(2):
                        dve.wait_ge(psum_full, g.full((t, half)))
                        o = h[:, t, 512 * half:512 * half + 512]
                        nc.vector.tensor_tensor(o, o, psum[g.bank((t, half))][:], ALU.add).then_inc(dve_evac, 1)
        stage.close()

    add_projection("wout", Q_OUT)

    xa = ExitStack()
    xk = sb(xa, "xk", [P, DC, M])
    xv = sb(xa, "xv", [P, MB, D])
    xq = sb(xa, "xq", [P, DC, T])
    stage = ExitStack()
    mem = sb(stage, "mem", [P, MB, D])
    mem_t = sb(stage, "mem_t", [P, DC, M])
    m2 = pair(stage, "mem", [P, DC, M])
    w = pair(stage, "w_xkv", [P, SPLIT, DC, P])
    with nc.Block() as block:
        @block.sync
        def _(sp):
            sp.dma_start(mem[:], A["mem"]).then_inc(small_loaded, 16)
            sp.wait_ge(small_loaded, loads[0] + 16)
    loads[0] += 16
    norm_transpose("nmem", mem, MB, D, V_MEM, mem_t, parts=m2)
    plan = [(("k", n), "dve") for n in range(DC)]
    plan += [(("v", half, t), "dve") for half in range(2) for t in range(MB)]
    g = Groups(C, plan)
    for n in range(8):
        tile_last[4 * Q_XK + n] = g.full(("k", n))
        tile_last[4 * Q_XV + n] = g.full(("v", n // 4, MB - 1))
    with nc.Block() as block:
        @block.sync
        def _(sp):
            load_tiles(sp, 4 * Q_XK, 4 * Q_XQ)

        @block.tensor
        def _(pe):
            for n in range(DC):
                projected(pe, g, ("k", n), w, 4 * Q_XK + n, m2, M)
            for q in range(2):
                for t in range(MB):
                    projected_natural(pe, g, ("v", q, t), w, Q_XV + q, m2, t)

        @block.scalar
        def _(act):
            for n in range(4 * Q_XK, 4 * Q_XQ):
                tile_hi(act, w, n, 4 * Q_XK)

        @block.vector
        def _(dve):
            for n in range(SPLIT):
                tile_lo(dve, w, 4 * Q_XK + n)
            for n in range(DC):
                dve.wait_ge(psum_full, g.full(("k", n)))
                nc.vector.tensor_copy(xk[:, n, :], psum[g.bank(("k", n))][:, 0:M]).then_inc(dve_evac, 1)
                tile_lo(dve, w, 4 * Q_XV + n)
            for half in range(2):
                for t in range(MB):
                    dve.wait_ge(psum_full, g.full(("v", half, t)))
                    nc.vector.tensor_copy(xv[:, t, 512 * half:512 * half + 512],
                                          psum[g.bank(("v", half, t))][:]).then_inc(dve_evac, 1)
    stage.close()
    stage = ExitStack()
    x2 = pair(stage, "xh", [P, DC, T])
    norm_transpose("nxa", h, TB, D, V_XA, act_t, parts=x2, summed=ssq[:])
    w = pair(stage, "w_xq", [P, SPLIT, DC, P])
    g = Groups(C, [(n, "act") for n in range(DC)])
    for n in range(8):
        tile_last[4 * Q_XQ + n] = g.full(n)
    with nc.Block() as block:
        @block.sync
        def _(sp):
            load_tiles(sp, 4 * Q_XQ, 4 * Q_XO)

        @block.tensor
        def _(pe):
            for n in range(DC):
                projected(pe, g, n, w, 4 * Q_XQ + n, x2, T)

        @block.vector
        def _(dve):
            for n in range(4 * Q_XQ, 4 * Q_XO):
                tile_lo(dve, w, n)

        @block.scalar
        def _(act):
            for n in range(4 * Q_XQ, 4 * Q_XO):
                tile_hi(act, w, n, 4 * Q_XQ)
            for n in range(DC):
                act.wait_ge(psum_full, g.full(n))
                nc.scalar.activation(xq[:, n, :], psum[g.bank(n)][:], ACT.Identity).then_inc(act_evac, 1)
    stage.close()
    stage = ExitStack()
    prob = sb(stage, "prob", [P, 2, TB, M])
    prob_t = sb(stage, "prob_t", [P, 2, MB, T])
    xst = sb(stage, "xst", [P, XH, 4, TB])
    x_max, x_exp, x_norm = sem("x_max"), sem("x_exp"), sem("x_norm")
    XSCALE = float(XD) ** -0.5
    plan = []
    for i in range(XH + 1):
        if i < XH:
            plan += [(("s", i, u), "act") for u in range(TB // 2)]
        if i >= 1:
            plan += [(("p", i - 1, m), "act") for m in range(MB)]
            plan += [(("o", i - 1, c), "dve") for c in range(2)]
    g = Groups(C, plan)
    with nc.Block() as block:
        @block.tensor
        def _(pe):
            for i in range(XH + 1):
                if i < XH:
                    for u in range(TB // 2):
                        bank = opened(pe, g, ("s", i, u))
                        for v in range(2):
                            t = 2 * u + v
                            for c in range(2):
                                last = nc.tensor.matmul(bank[:, v * M:(v + 1) * M],
                                                        xq[:, 2 * i + c, t * P:(t + 1) * P], xk[:, 2 * i + c, :],
                                                        start=(c == 0), stop=(c == 1))
                        last.then_inc(psum_full, 1)
                if i >= 1:
                    n = i - 1
                    pe.wait_ge(x_norm, n + 1)
                    for m in range(MB):
                        bank = opened(pe, g, ("p", n, m))
                        for t in range(TB):
                            last = nc.tensor.transpose(bank[:, t * P:(t + 1) * P],
                                                       prob[:, n % 2, t, m * P:(m + 1) * P], ident)
                        last.then_inc(psum_full, 1)
                    wait_read(pe, g, ("p", n, MB - 1))
                    for c in range(2):
                        bank = opened(pe, g, ("o", n, c))
                        f = (2 * n + c) * P
                        for m in range(MB):
                            last = nc.tensor.matmul(bank[:], xv[:, m, f:f + P], prob_t[:, n % 2, m, :],
                                                    start=(m == 0), stop=(m == MB - 1))
                        last.then_inc(psum_full, 1)

        @block.scalar
        def _(act):
            for i in range(XH + 1):
                if i < XH:
                    if i >= 2:
                        act.wait_ge(psum_full, g.full(("p", i - 2, MB - 1)))
                    act.wait_ge(x_max, i + 1)
                    for t in range(TB):
                        b = psum[g.bank(("s", i, t // 2))]
                        ins = nc.scalar.activation(prob[:, i % 2, t, :], b[:, (t % 2) * M:(t % 2 + 1) * M], ACT.Exp,
                                                   bias=xst[:, i, 1, t:t + 1], scale=XSCALE,
                                                   accum_out=xst[:, i, 2, t:t + 1])
                        if t % 2:
                            ins.then_inc(act_evac, 1)
                if i >= 1:
                    for m in range(MB):
                        act.wait_ge(psum_full, g.full(("p", i - 1, m)))
                        nc.scalar.activation(prob_t[:, (i - 1) % 2, m, :], psum[g.bank(("p", i - 1, m))][:],
                                             ACT.Identity).then_inc(act_evac, 1)

        @block.vector
        def _(dve):
            for i in range(XH + 1):
                if i < XH:
                    for u in range(2):
                        dve.wait_ge(psum_full, g.full(("s", i, u)))
                        ins = nc.vector.reduce_max(xst[:, i, 0, 2 * u:2 * u + 2],
                                                   psum[g.bank(("s", i, u))][:].rearrange("p (t m) -> p t m", t=2),
                                                   axis=AX.X)
                    link(dve, "dve", ins)
                    nc.vector.tensor_scalar(xst[:, i, 1, :], xst[:, i, 0, :], -XSCALE, None, ALU.mult).then_inc(x_max, 1)
                    wait_read(dve, g, ("s", i, 1))
                    link(dve, "dve", nc.vector.reciprocal(xst[:, i, 3, :], xst[:, i, 2, :]))
                    nc.vector.tensor_tensor(prob[:, i % 2], prob[:, i % 2],
                                            xst[:, i, 3, :].unsqueeze(2).to_broadcast([P, TB, M]),
                                            ALU.mult).then_inc(x_norm, 1)
                if i >= 1:
                    for c in range(2):
                        dve.wait_ge(psum_full, g.full(("o", i - 1, c)))
                        nc.vector.tensor_copy(act_t[:, 2 * (i - 1) + c, :],
                                              psum[g.bank(("o", i - 1, c))][:]).then_inc(dve_evac, 1)
    stage.close()
    xa.close()
    add_projection("xo", Q_XO)

    stage = ExitStack()
    x2 = pair(stage, "xf", [P, DC, T])
    norm_transpose("nffn", h, TB, D, V_FFN, act_t, parts=x2, summed=ssq[:])
    w = pair(stage, "w_pq", [P, SPLIT, DC, P])
    ROWS, RW = 10, 8
    AHEAD = 4
    NC = ROWS * RW
    HS = TB * TOPK
    keys = sb(stage, "keys", [P, HP, NKEYS])
    pq = sb(stage, "pq", [P, 2, T])
    ps = sb(stage, "ps", [P, 4, TB, NKEYS])
    pw = sb(stage, "pw", [P, 2, TB, NKEYS])
    top_v = sb(stage, "top_v", [P, 4, TB, TOPK])
    top_i = sb(stage, "top_i", [P, 4, TB, TOPK], U32)
    cand = sb(stage, "cand", [P, TB, NC])
    cw = sb(stage, "cw", [P, TB, NC])
    best = sb(stage, "best", [P, TB, TOPK])
    pos = sb(stage, "pos", [P, TB, TOPK], U32)
    posx = sb(stage, "posx", [P, 2, HS], U32)
    posf = sb(stage, "posf", [P, 2, HS])
    extra = sb(stage, "extra", [P, 3, HS])
    rank = sb(stage, "rank", [P, 2, HS])
    idxf = sb(stage, "idxf", [P, 2, TB, TOPK])
    picked = sb(stage, "picked", [P, 2, HS, TOPK])
    triple = sb(stage, "triple", [P, TB, 3, SLOTS])
    gs = sb(stage, "gs", [P, 2, TB * PH])
    r_top, r_diff, r_exp, r_triple = (sem(x) for x in ("r_top", "r_diff", "r_exp", "r_triple"))
    plan = []
    for i in range(HP + 1):
        if i < HP:
            plan += [(("q", i), "act")]
        if i >= 1:
            plan += [(("s", i - 1), "act")]
    plan += [(("t", t), "act") for t in range(TB)]
    g = Groups(C, plan)
    for n in range(HP):
        tile_last[4 * Q_PQ + n] = g.full(("q", n))
    with nc.Block() as block:
        @block.sync
        def _(sp):
            sp.dma_start(keys[:], A["keys"]).then_inc(small_loaded, 16)
            load_tiles(sp, 4 * Q_PQ, 4 * Q_PQ + 2 * SPLIT)
            sp.dma_start(h_scratch, h[:]).then_inc(stored, 16)
            for half in range(2):
                sp.dma_start(xf_scratch[:, half], act_t[:, :, half * HALF:(half + 1) * HALF]).then_inc(stored, 16)
            load_tiles(sp, 4 * Q_PQ + 2 * SPLIT, NTILES)
            sp.wait_ge(stored, 48)

        @block.tensor
        def _(pe):
            for i in range(HP + 1):
                if i < HP:
                    projected(pe, g, ("q", i), w, 4 * Q_PQ + i, x2, T)
                if i >= 1:
                    if i == 1:
                        pe.wait_ge(small_loaded, loads[0] + 16)
                    wait_read(pe, g, ("q", i - 1))
                    bank = opened(pe, g, ("s", i - 1))
                    for t in range(TB):
                        last = nc.tensor.matmul(bank[:, t * P:(t + 1) * P], pq[:, (i - 1) % 2, t * P:(t + 1) * P],
                                                keys[:, i - 1, :], start=True, stop=True)
                    last.then_inc(psum_full, 1)
            pe.wait_ge(r_triple, 1)
            for t in range(TB):
                bank = opened(pe, g, ("t", t))
                for s in range(3):
                    last = nc.tensor.transpose(bank[:, s * P:(s + 1) * P], triple[:, t, s, :], ident)
                last.then_inc(psum_full, 1)

        @block.gpsimd
        def _(pool):
            pool.wait_ge(w_split, 4 * Q_PQ + AHEAD)
            for n in range(AHEAD, HP):
                tile_lo(pool, w, 4 * Q_PQ + n, nc.gpsimd)

        @block.scalar
        def _(act):
            for n in range(AHEAD):
                tile_hi(act, w, 4 * Q_PQ + n, 4 * Q_PQ)
            for i in range(HP + 1):
                if i < HP:
                    act.wait_ge(psum_full, g.full(("q", i)))
                    if i >= 2:
                        act.wait_ge(psum_full, g.full(("s", i - 2)))
                    nc.scalar.activation(pq[:, i % 2, :], psum[g.bank(("q", i))][:], ACT.Identity).then_inc(act_evac, 1)
                    if i + AHEAD < HP:
                        tile_hi(act, w, 4 * Q_PQ + i + AHEAD, 4 * Q_PQ)
                if i >= 1:
                    act.wait_ge(psum_full, g.full(("s", i - 1)))
                    if i >= 5:
                        act.wait_ge(r_top, i - 4)
                    nc.scalar.activation(ps[:, (i - 1) % 4], psum[g.bank(("s", i - 1))][:].rearrange(
                        "p (t n) -> p t n", t=TB), ACT.Identity).then_inc(act_evac, 1)
            act.wait_ge(r_diff, PH)
            nc.scalar.activation(triple[:, :, 2, :], triple[:, :, 2, :], ACT.Exp).then_inc(r_exp, 1)
            for t in range(TB):
                act.wait_ge(psum_full, g.full(("t", t)))
                nc.scalar.activation(slot_t[:, :, t * P:(t + 1) * P],
                                     psum[g.bank(("t", t))][:, 0:3 * P].rearrange("p (s t) -> p s t", s=3),
                                     ACT.Identity).then_inc(act_evac, 1)

        @block.vector
        def _(dve):
            def lockstep(*chains):
                chains = list(chains)
                while chains:
                    last = None
                    for chain in list(chains):
                        ins = next(chain, None)
                        if ins is None:
                            chains.remove(chain)
                        else:
                            last = ins
                    if last is not None:
                        link(dve, "dve", last)

            def one_after_another(*chains):
                for chain in chains:
                    yield from chain

            def top(i):
                wait_read(dve, g, ("s", i))
                v, n, p, q = top_v[:, i % 4], top_i[:, i % 4], ps[:, i % 4], pw[:, i % 2]
                for t in range(TB):
                    ins = nc.vector.max(v[:, t, 0:8], p[:, t, :])
                yield ins
                for t in range(TB):
                    nc.vector.max_index(n[:, t, 0:8], v[:, t, 0:8], p[:, t, :])
                    ins = nc.vector.match_replace(q[:, t, :], v[:, t, 0:8], p[:, t, :], NEG)
                yield ins
                for t in range(TB):
                    ins = nc.vector.max(v[:, t, 8:16], q[:, t, :])
                nc.vector.engine_nop().then_inc(r_top, 1)
                yield ins
                for t in range(TB):
                    ins = nc.vector.max_index(n[:, t, 8:16], v[:, t, 8:16], q[:, t, :])
                yield ins

            def combine(x):
                r = 2 * (x % 2)
                va, vb, index = top_v[:, r], top_v[:, r + 1], top_i[:, r:r + 2]
                c4 = cand[:].rearrange("p t (r c) -> p t r c", c=RW)
                nc.vector.tensor_copy(idxf[:], index)
                nc.vector.tensor_tensor(cand[:, :, 0:2 * RW], va[:, :, 0:1].to_broadcast([P, TB, 2 * RW]), vb, ALU.add)
                nc.vector.tensor_tensor(c4[:, :, 2:9, :], va[:, :, 1:8].unsqueeze(3).to_broadcast([P, TB, 7, RW]),
                                        vb[:, :, 0:RW].unsqueeze(2).to_broadcast([P, TB, 7, RW]), ALU.add)
                yield nc.vector.tensor_tensor(c4[:, :, 9, :], va[:, :, 8:16],
                                              vb[:, :, 0:1].to_broadcast([P, TB, RW]), ALU.add)
                for t in range(TB):
                    ins = nc.vector.max(best[:, t, 0:8], cand[:, t, :])
                yield ins
                for t in range(TB):
                    nc.vector.max_index(pos[:, t, 0:8], best[:, t, 0:8], cand[:, t, :])
                    ins = nc.vector.match_replace(cw[:, t, :], best[:, t, 0:8], cand[:, t, :], NEG)
                yield ins
                for t in range(TB):
                    ins = nc.vector.max(best[:, t, 8:16], cw[:, t, :])
                yield ins
                for t in range(TB):
                    ins = nc.vector.max_index(pos[:, t, 8:16], best[:, t, 8:16], cw[:, t, :])
                yield ins
                nc.vector.tensor_tensor(triple[:, :, 2, x * TOPK:(x + 1) * TOPK], best[:],
                                        best[:, :, 0:1].to_broadcast([P, TB, TOPK]), ALU.subtract).then_inc(r_diff, 1)
                pf = pos[:].rearrange("p t k -> p (t k)")
                nc.vector.tensor_scalar(posx[:, 0, :], pf, 3, None, ALU.logical_shift_right)
                yield nc.vector.tensor_scalar(posx[:, 1, :], pf, RW - 1, None, ALU.bitwise_and)
                yield nc.vector.tensor_copy(posf[:], posx[:])
                row, col = posf[:, 0, :], posf[:, 1, :]
                end, shift, moved = extra[:, 0, :], extra[:, 1, :], extra[:, 2, :]
                a, b = rank[:, 0, :], rank[:, 1, :]
                nc.vector.tensor_scalar(end, row, float(ROWS - 1), None, ALU.is_equal)
                nc.vector.tensor_scalar(shift, row, 1.0, float(RW), ALU.is_equal, ALU.mult)
                yield nc.vector.tensor_scalar(a, row, -1.0, 0.0, ALU.add, ALU.max)
                yield nc.vector.tensor_tensor(moved, end, col, ALU.mult)
                nc.vector.tensor_tensor(a, a, moved, ALU.add)
                yield nc.vector.tensor_tensor(b, col, moved, ALU.subtract)
                yield nc.vector.tensor_tensor(b, b, shift, ALU.add)
                yield nc.vector.tensor_tensor(
                    picked[:], rank[:].unsqueeze(3).to_broadcast([P, 2, HS, TOPK]),
                    iota16.unsqueeze(1).unsqueeze(1).to_broadcast([P, 2, HS, TOPK]), ALU.is_equal)
                pick = picked[:].rearrange("p s (t k) a -> p (s t) k a", k=TOPK)
                yield nc.vector.tensor_tensor(
                    pick, pick, idxf[:].rearrange("p s t a -> p (s t) a").unsqueeze(2).to_broadcast(
                        [P, 2 * TB, TOPK, TOPK]), ALU.mult)
                for s in range(2):
                    ins = nc.vector.reduce_sum(triple[:, :, s, x * TOPK:(x + 1) * TOPK],
                                               picked[:, s].rearrange("p (t k) a -> p t k a", k=TOPK), axis=AX.X)
                yield ins

            for n in range(AHEAD):
                tile_lo(dve, w, 4 * Q_PQ + n)
            lockstep(one_after_another(top(0), top(1)))
            for x in range(1, PH):
                lockstep(combine(x - 1), one_after_another(top(2 * x), top(2 * x + 1)))
            lockstep(combine(PH - 1))
            dve.wait_ge(r_exp, 1)
            gate = triple[:, :, 2, :].rearrange("p t (x k) -> p t x k", k=TOPK)
            gs4 = lambda n: gs[:, n, :].rearrange("p (t x) -> p t x", x=PH)
            link(dve, "dve", nc.vector.reduce_sum(gs4(0), gate, axis=AX.X))
            link(dve, "dve", nc.vector.reciprocal(gs[:, 1, :], gs[:, 0, :]))
            nc.vector.tensor_tensor(gate, gate, gs4(1).unsqueeze(3).to_broadcast([P, TB, PH, TOPK]),
                                    ALU.mult).then_inc(r_triple, 1)
    loads[0] += 16
    stage.close()
    main.close()

    peer = ExitStack()
    NB = 4
    NT, HOT = 8, 4
    G = sb(peer, "gates", [P, NKEYS, HALF])
    raw = sb(peer, "raw", [P, 4, D])
    xs_hi = sb(peer, "xs_hi", [P, DC, HALF], F32R)
    xs_lo = sb(peer, "xs_lo", [P, DC, HALF], F32R)
    u_hi = sb(peer, "u_hi", [P, 2, DC, P], F32R)
    u_lo = sb(peer, "u_lo", [P, 2, DC, P], F32R)
    v_hi = sb(peer, "v_hi", [P, 2, D], F32R)
    v_lo = sb(peer, "v_lo", [P, 2, D], F32R)
    u_loaded = [sem(f"u_loaded{k}") for k in range(2)]
    v_loaded = [sem(f"v_loaded{k}") for k in range(2)]
    hot_ready, hot_used, g_read = sem("hot_ready"), sem("hot_used"), sem("g_read")
    u_hi_done, u_lo_done, v_hi_done, v_lo_done = (sem(x) for x in ("u_hi_done", "u_lo_done", "v_hi_done", "v_lo_done"))
    u_done, v_done, gelu_done, w_mult, w_hi_done, w_ready, y_read = (
        sem(x) for x in ("u_done", "v_done", "gelu_done", "w_mult", "w_hi_done", "w_ready", "y_read"))
    x_loaded, x_hi_done, x_lo_done = sem("x_loaded"), sem("x_hi_done"), sem("x_lo_done")
    f_h, f_g, f_ss, f_sq = sem("f_h"), sem("f_g"), sem("f_ss"), sem("f_sq")
    BODIES = NKEYS // NB
    TBODIES = HALF // NT
    for half in range(2):
        t0 = half * HALF
        x_raw = raw[:, 0:2].rearrange("p s (c t) -> p (s c) t", t=HALF)
        stage = ExitStack()
        hot = sb(stage, f"hot{half}", [P, HOT, 2, P])
        with nc.Block() as block:
            @block.sync
            def _(sp):
                sp.dma_start(x_raw, xf_scratch[:, half]).then_inc(x_loaded, 16)

            @block.vector
            def _(dve):
                def body(i, first):
                    for k in range(NT):
                        if not (first and k < HOT):
                            dve.wait_ge(hot_used, i * NT + (half * HALF + k + 1 - HOT))
                        col = lambda s: slot_t[:, s, bass.ds(i * NT + (t0 + k), 1)]
                        nc.vector.tensor_scalar(hot[:, k % HOT, 0, :], iota, col(0), None, ALU.is_equal)
                        nc.vector.tensor_scalar(hot[:, k % HOT, 1, :], iota, col(1), col(2), ALU.is_equal,
                                                ALU.mult).then_inc(hot_ready, 1)
                body(0, half == 0)
                with dve.Fori(1, TBODIES) as i:
                    body(i, False)
                dve.wait_ge(x_hi_done, half + 1)
                nc.vector.tensor_tensor(xs_lo[:], x_raw, xs_hi[:].bitcast(F32), ALU.subtract).then_inc(x_lo_done, 1)

            @block.tensor
            def _(pe):
                def body(i, first):
                    for k in range(NT):
                        if k % 4 == 0 and not first:
                            pe.wait_ge(g_read, i * 2 + (2 * half * TBODIES + k // 4 - 1))
                        pe.wait_ge(hot_ready, i * NT + (half * HALF + k + 1))
                        nc.tensor.matmul(psum[k // 4][:, k % 4 * P:(k % 4 + 1) * P], hot[:, k % HOT, 0, :],
                                         hot[:, k % HOT, 1, :], start=True, stop=True).then_inc(hot_used, 1)
                body(0, half == 0)
                with pe.Fori(1, TBODIES) as i:
                    body(i, False)

            @block.scalar
            def _(act):
                act.wait_ge(x_loaded, 16 * (half + 1))
                nc.scalar.activation(xs_hi[:], x_raw, ACT.Identity).then_inc(x_hi_done, 1)

                def body(i):
                    for b in range(2):
                        act.wait_ge(hot_used, i * NT + (half * HALF + 4 * b + 4))
                        nc.scalar.activation(G[:, :, bass.ds(i * NT + 4 * b, 4)],
                                             psum[b][:].rearrange("p (t j) -> p j t", t=4),
                                             ACT.Identity).then_inc(g_read, 1)
                body(0)
                with act.Fori(1, TBODIES) as i:
                    body(i)
        stage.close()
        stage = ExitStack()
        gel = sb(stage, f"gel{half}", [P, 2, HALF])
        w_hi = sb(stage, f"w_hi{half}", [P, 2, HALF], F32R)
        w_lo = sb(stage, f"w_lo{half}", [P, 2, HALF], F32R)
        wf = gel
        base = half * NKEYS
        u_raw = lambda n: raw[:, n % 2].rearrange("p (c i) -> p c i", i=P)
        v_raw = lambda n: raw[:, 2 + n % 2]
        with nc.Block() as block:
            @block.sync
            def _(sp):
                def load_u(i, k, first):
                    if not first:
                        sp.wait_ge(u_lo_done, i * NB + (base + k - 1))
                    sp.dma_start(u_raw(k), A["u_tiles"][bass.ds(i * NB + k, 1)].rearrange("o p c i -> (o p) c i")
                                 ).then_inc(u_loaded[k % 2], 16)

                def load_v(i, k, first):
                    if not first:
                        sp.wait_ge(v_lo_done, i * NB + (base + k - 1))
                    sp.dma_start(v_raw(k), A["v"][:, bass.ds(i * NB + k, 1), :].rearrange("i o d -> i (o d)")
                                 ).then_inc(v_loaded[k % 2], 16)
                for k in range(NB):
                    load_u(0, k, half == 0 and k < 2)
                    load_v(0, k, half == 0 and k < 2)
                with sp.Fori(1, BODIES) as i:
                    for k in range(NB):
                        load_u(i, k, False)
                        load_v(i, k, False)

            @block.tensor
            def _(pe):
                def up(i, k, first=False):
                    pe.wait_ge(u_lo_done, i * NB + (base + k + 1))
                    if not first:
                        pe.wait_ge(gelu_done, i * NB + (base + k - 1))
                    bank = psum[k % 2][:, 0:HALF]
                    for c in range(DC):
                        nc.tensor.matmul(bank, u_lo[:, k % 2, c, :], xs_hi[:, c, :], start=(c == 0), stop=False)
                        nc.tensor.matmul(bank, u_hi[:, k % 2, c, :], xs_lo[:, c, :], start=False, stop=False)
                        last = nc.tensor.matmul(bank, u_hi[:, k % 2, c, :], xs_hi[:, c, :], start=False,
                                                stop=(c == DC - 1))
                    last.then_inc(u_done, 1)

                def down(i, k, start=False, stop=False):
                    pe.wait_ge(v_lo_done, i * NB + (base + k + 1))
                    pe.wait_ge(w_ready, i * NB + (base + k + 1))
                    for t in range(2):
                        for d in range(2):
                            y = psum[4 + 2 * t + d][:]
                            tk, f = slice(t * P, (t + 1) * P), slice(512 * d, 512 * d + 512)
                            nc.tensor.matmul(y, w_lo[:, k % 2, tk], v_hi[:, k % 2, f], start=start, stop=False)
                            nc.tensor.matmul(y, w_hi[:, k % 2, tk], v_lo[:, k % 2, f], start=False, stop=False)
                            last = nc.tensor.matmul(y, w_hi[:, k % 2, tk], v_hi[:, k % 2, f], start=False, stop=stop)
                    last.then_inc(v_done, 1)
                pe.wait_ge(x_lo_done, half + 1)
                up(0, 0, half == 0)
                for k in range(NB):
                    up(0, k + 1, half == 0 and k == 0)
                    down(0, k, start=(k == 0))
                with pe.Fori(1, BODIES - 1) as i:
                    for k in range(NB):
                        up(i, k + 1)
                        down(i, k)
                for k in range(NB):
                    if k < NB - 1:
                        up(BODIES - 1, k + 1)
                    down(BODIES - 1, k, stop=(k == NB - 1))

            @block.scalar
            def _(act):
                def u_part(i, k, first=False):
                    act.wait_ge(u_loaded[k % 2], i * (NB // 2 * 16) + 16 * (base // 2 + k // 2 + 1))
                    if not first:
                        act.wait_ge(u_done, i * NB + (base + k - 1))
                    nc.scalar.activation(u_hi[:, k % 2], u_raw(k), ACT.Identity).then_inc(u_hi_done, 1)

                def v_part(i, k, first=False):
                    act.wait_ge(v_loaded[k % 2], i * (NB // 2 * 16) + 16 * (base // 2 + k // 2 + 1))
                    if not first:
                        act.wait_ge(v_done, i * NB + (base + k - 1))
                    nc.scalar.activation(v_hi[:, k % 2], v_raw(k), ACT.Identity).then_inc(v_hi_done, 1)

                def gelu(i, k, first=False):
                    act.wait_ge(u_done, i * NB + (base + k + 1))
                    if not first:
                        act.wait_ge(w_ready, i * NB + (base + k - 1))
                    nc.scalar.activation(gel[:, k % 2, :], psum[k % 2][:, 0:HALF],
                                         ACT.Gelu_apprx_tanh).then_inc(gelu_done, 1)
                u_part(0, 0, half == 0)
                u_part(0, 1, half == 0)
                v_part(0, 0, half == 0)
                for k in range(NB):
                    gelu(0, k, half == 0 and k < 2)
                    u_part(0, k + 2)
                    v_part(0, k + 1, half == 0 and k == 0)
                with act.Fori(1, BODIES - 1) as i:
                    for k in range(NB):
                        gelu(i, k)
                        u_part(i, k + 2)
                        v_part(i, k + 1)
                for k in range(NB):
                    gelu(BODIES - 1, k)
                    if k + 2 < NB:
                        u_part(BODIES - 1, k + 2)
                    if k + 1 < NB:
                        v_part(BODIES - 1, k + 1)

            @block.vector
            def _(dve):
                def u_part(i, k):
                    dve.wait_ge(u_hi_done, i * NB + (base + k + 1))
                    nc.vector.tensor_tensor(u_lo[:, k % 2], u_raw(k), u_hi[:, k % 2].bitcast(F32),
                                            ALU.subtract).then_inc(u_lo_done, 1)

                def v_part(i, k):
                    dve.wait_ge(v_hi_done, i * NB + (base + k + 1))
                    nc.vector.tensor_tensor(v_lo[:, k % 2], v_raw(k), v_hi[:, k % 2].bitcast(F32),
                                            ALU.subtract).then_inc(v_lo_done, 1)

                def weights(i, k, first=False):
                    n = lambda d: i * NB + (base + k + 1 - d)
                    dve.wait_ge(gelu_done, n(0))
                    if not first:
                        dve.wait_ge(v_done, n(2))
                    nc.vector.tensor_tensor(wf[:, k % 2, :], gel[:, k % 2, :], G[:, bass.ds(i * NB + k, 1), :].
                                            rearrange("p o t -> p (o t)"), ALU.mult).then_inc(w_mult, 1)
                    dve.wait_ge(w_mult, n(0))
                    nc.vector.tensor_copy(w_hi[:, k % 2, :], wf[:, k % 2, :]).then_inc(w_hi_done, 1)
                    dve.wait_ge(w_hi_done, n(0))
                    nc.vector.tensor_tensor(w_lo[:, k % 2, :], wf[:, k % 2, :], w_hi[:, k % 2, :].bitcast(F32),
                                            ALU.subtract).then_inc(w_ready, 1)
                u_part(0, 0)
                u_part(0, 1)
                v_part(0, 0)
                for k in range(NB):
                    weights(0, k, half == 0 and k < 2)
                    u_part(0, k + 2)
                    v_part(0, k + 1)
                with dve.Fori(1, BODIES - 1) as i:
                    for k in range(NB):
                        weights(i, k)
                        u_part(i, k + 2)
                        v_part(i, k + 1)
                for k in range(NB):
                    weights(BODIES - 1, k)
                    if k + 2 < NB:
                        u_part(BODIES - 1, k + 2)
                    if k + 1 < NB:
                        v_part(BODIES - 1, k + 1)
        hh, sq, gf = raw[:, 0:2], raw[:, 2], raw[:, 3]
        st = gel[:, 0, 0:10].rearrange("p (a b) -> p a b", b=2)
        with nc.Block() as block:
            @block.sync
            def _(sp):
                sp.dma_start(hh, h_scratch[:, 2 * half:2 * half + 2, :]).then_inc(f_h, 16)
                sp.dma_start(gf, A["final_g"].partition_broadcast(P)).then_inc(f_g, 16)
                sp.wait_ge(f_sq, 2 * half + 2)
                sp.dma_start(out[:, 2 * half:2 * half + 2, :], hh).then_inc(stored, 16)
                sp.wait_ge(stored, 16 * (half + 4))

            @block.vector
            def _(dve):
                dve.wait_ge(f_h, 16 * (half + 1))
                for t in range(2):
                    for d in range(2):
                        o = hh[:, t, 512 * d:512 * d + 512]
                        ins = nc.vector.tensor_tensor(o, o, psum[4 + 2 * t + d][:], ALU.add)
                ins.then_inc(y_read, 1)
                dve.wait_ge(f_ss, 4 * half + 2)
                nc.vector.tensor_scalar(st[:, 1, :], st[:, 0, :], 1.0 / D, EPS, ALU.mult, ALU.add).then_inc(f_ss, 1)
                dve.wait_ge(f_ss, 4 * half + 4)
                link(dve, "dve", nc.vector.reciprocal(st[:, 2, :], st[:, 2, :]))
                link(dve, "dve", nc.vector.tensor_tensor(st[:, 3, :], st[:, 2, :], st[:, 2, :], ALU.mult))
                link(dve, "dve", nc.vector.tensor_tensor(st[:, 3, :], st[:, 3, :], st[:, 1, :], ALU.mult))
                link(dve, "dve", nc.vector.tensor_scalar(st[:, 3, :], st[:, 3, :], -0.5, 1.5, ALU.mult, ALU.add))
                link(dve, "dve", nc.vector.tensor_tensor(st[:, 4, :], st[:, 3, :], st[:, 2, :], ALU.mult))
                dve.wait_ge(f_g, 16 * (half + 1))
                for t in range(2):
                    nc.vector.scalar_tensor_tensor(out=hh[:, t, :], in0=hh[:, t, :], scalar=st[:, 4, t:t + 1], in1=gf,
                                                   op0=ALU.mult, op1=ALU.mult).then_inc(f_sq, 1)

            @block.scalar
            def _(act):
                act.wait_ge(y_read, half + 1)
                for t in range(2):
                    nc.scalar.activation(sq, hh[:, t, :], ACT.Square, accum_out=st[:, 0, t:t + 1]).then_inc(f_ss, 1)
                    act.wait_ge(f_ss, 4 * half + t + 1)
                act.wait_ge(f_ss, 4 * half + 3)
                nc.scalar.activation(st[:, 2, :], st[:, 1, :], ACT.Sqrt).then_inc(f_ss, 1)
        stage.close()
    peer.close()
    top.close()


def _lay_out(a):
    f = {k: np.asarray(v) for k, v in a.items()}
    for k in f:
        if k not in ("x", "mem", "final_norm_g"):
            f[k] = f[k][0]
    w_in = f["w_in"]
    c1 = 2 * GH * GDK + GH * GDV
    c3 = c1 + GH * GDV
    dense = np.concatenate([w_in[:, :c3], w_in[:, c3 + LOWRANK:], f["w_out"], f["w_xkv"], f["w_xq"], f["w_xo"],
                            f["peer_w_q"]], axis=1)
    cols = lambda v: v.reshape(-1, P).T
    conv = f["gla_conv_w"].reshape(CONV, CONV_BLOCKS, P).transpose(2, 1, 0).reshape(P, -1)
    vec = np.concatenate([cols(f["mix_norm_g"]), cols(f["xattn_norm_g"]), cols(f["mem_norm_g"]),
                          cols(f["ffn_norm_g"]), conv, cols(f["gla_gate_b"]), cols(f["gla_out_norm_g"]),
                          cols(f["sb_out_norm_g"])], axis=1)
    r = np.arange(P)
    const = np.zeros((P, NCONST), np.float32)
    const[:, C_ID:C_ID + P] = np.eye(P)
    const[:, C_ONES:C_ONES + P] = 1
    const[:, C_TRI:C_TRI + P] = r[:, None] >= r[None, :]
    const[:, C_IOTA16:C_IOTA16 + TOPK] = np.arange(TOPK)[None, :]
    masks = [np.eye(P, dtype=bool)]
    key, query = r[:, None], r[None, :]
    for b in LEVELS:
        masks.append((key // (2 * b) == query // (2 * b)) & (key % (2 * b) < b) & (query % (2 * b) >= b))
    out = {
        "x": f["x"].reshape(TB, P, D).transpose(1, 0, 2),
        "mem": f["mem"].reshape(MB, P, D).transpose(1, 0, 2),
        "w_tiles": dense.reshape(DC, P, 4 * NQUADS, P).transpose(1, 2, 0, 3),
        "w_low": w_in[:, c3:c3 + LOWRANK].reshape(DC, P, LOWRANK).transpose(1, 0, 2),
        "gate_w": f["gla_gate_w"],
        "vec": vec,
        "const": const,
        "iota": np.broadcast_to(r.astype(np.float32), (P, P)),
        "masks": np.stack(masks, axis=1).astype(np.uint32),
        "keys": f["peer_sub_keys"].reshape(HP, NKEYS, P).transpose(2, 0, 1),
        "u_tiles": f["peer_u"].reshape(NKEYS, NKEYS, DC, P).transpose(1, 3, 2, 0),
        "v": f["peer_v"].reshape(NKEYS, NKEYS, D),
        "final_g": f["final_norm_g"],
    }
    return {k: np.ascontiguousarray(v) for k, v in out.items()}


def kernel(**inputs):
    import concourse.bacc as bacc
    from concourse.bass_utils import run_bass_kernel_spmd

    arrays = _lay_out(inputs)
    nc = bacc.Bacc("TRN2", target_bir_lowering=False, num_devices=1)
    A = {k: nc.dram_tensor("in_" + k, v.shape, mybir.dt.from_np(v.dtype), kind="ExternalInput").ap()
         for k, v in arrays.items()}
    out = nc.dram_tensor("out_0", [P, TB, D], F32, kind="ExternalOutput").ap()
    layer(nc, A, out)
    r = run_bass_kernel_spmd(nc, [{"in_" + k: v for k, v in arrays.items()}], core_ids=[0])
    return r.results[0]["out_0"].transpose(1, 0, 2).reshape(1, T, D)
```

```python
from contextlib import ExitStack

import numpy as np
import concourse.bass as bass
from concourse import mybir

F32 = mybir.dt.float32
F32R = mybir.dt.float32r
U32 = mybir.dt.uint32
ALU = mybir.AluOpType
ACT = mybir.ActivationFunctionType
AX = mybir.AxisListType

P = 128
D = 1024
DC = D // P
T = 512
TB = T // P
M = 256
MB = M // P
EPS = 1e-6

GH, GDK, GDV, LOWRANK = 4, 64, 128, 16
GATE_NORM = 16.0
CONV = 4
CONV_BLOCKS = (2 * GH * GDK + GH * GDV) // P
SH, SD = 8, 64
XH, XD = 4, 256
PH, NKEYS, TOPK = 8, 128, 16
HP = 2 * PH
SLOTS = PH * TOPK
NEG = -3.0e38

LEVELS = [64, 32, 16, 8, 4, 2, 1]

Q_CONV, Q_OG, Q_SBQ, Q_SBK, Q_SBV, Q_OUT, Q_XK, Q_XV, Q_XQ, Q_XO, Q_PQ = 0, 2, 3, 4, 5, 6, 8, 10, 12, 14, 16
NQUADS = 20
NTILES = 4 * NQUADS
AHEAD = 2
RAW, SPLIT = 4, 8

V_MIX, V_XA, V_MEM, V_FFN, V_CONV, V_GATEB, V_GLAG, V_SBG = 0, 8, 16, 24, 32, 64, 66, 67
NVEC = 71

C_ID, C_ONES, C_TRI, C_IOTA16 = 0, 128, 256, 384
NCONST = 400

SOFF = [0, 512, 896, 1152]
SLEN = [512, 384, 256, 128]
STOT = 1280


class Counts:

    def __init__(self):
        self.full = 0
        self.act = 0
        self.dve = 0
        self.chain = {}


class Groups:

    def __init__(self, counts, plan, banks=8):
        self.banks, self.at, self.value, self.who = banks, {}, [], []
        self.base = counts.full
        for n, (name, who) in enumerate(plan):
            assert name not in self.at
            self.at[name] = n
            if who == "act":
                counts.act += 1
                self.value.append(counts.act)
            else:
                counts.dve += 1
                self.value.append(counts.dve)
            self.who.append(who)
        counts.full += len(plan)

    def bank(self, name):
        return self.at[name] % self.banks

    def full(self, name):
        return self.base + self.at[name] + 1

    def read(self, name):
        n = self.at[name]
        return self.who[n], self.value[n]

    def before(self, name):
        n = self.at[name] - self.banks
        return None if n < 0 else (self.who[n], self.value[n])


def layer(nc, A, out):
    top = ExitStack()

    def sem(name):
        return top.enter_context(nc.semaphore(name))

    def sb(stack, name, shape, dt=F32):
        return stack.enter_context(nc.sbuf_tensor(name, shape, dt))

    psum_full = sem("psum_full")
    act_evac = sem("act_evac")
    dve_evac = sem("dve_evac")
    evac = {"act": act_evac, "dve": dve_evac}
    act_chain, dve_chain, pool_chain = sem("act_chain"), sem("dve_chain"), sem("pool_chain")
    tile_loaded = [sem(f"tile_loaded{s}") for s in range(RAW)]
    w_hi_done, w_split = sem("w_tile_hi"), sem("w_tile_split")
    small_loaded = sem("small_loaded")
    stored = sem("stored")
    C = Counts()
    loads = [0]
    steps = {"act": 0, "dve": 0, "pool": 0}
    chains = {"act": act_chain, "dve": dve_chain, "pool": pool_chain}

    def link(eng, who, ins):
        steps[who] += 1
        ins.then_inc(chains[who], 1)
        eng.wait_ge(chains[who], steps[who])

    psum = [top.enter_context(nc.psum_tensor(f"bank{b}", [P, 512], F32)) for b in range(8)]
    iota_t = sb(top, "iota", [P, P])
    slot_t = sb(top, "slot_t", [P, 3, T])
    main = ExitStack()
    const = sb(main, "const", [P, NCONST])
    vec = sb(main, "vec", [P, NVEC])
    act_t = sb(main, "act_t", [P, DC, T])
    ident = const[:, C_ID:C_ID + P]
    ones = const[:, C_ONES:C_ONES + P]
    tri = const[:, C_TRI:C_TRI + P]
    iota = iota_t[:]
    iota16 = const[:, C_IOTA16:C_IOTA16 + TOPK]
    h_scratch = nc.dram_tensor("h_scratch", [P, TB, D], F32, kind="Internal").ap()

    xf_scratch = nc.dram_tensor("xf_scratch", [2, P, DC, T], F32, kind="Internal").ap()
    gate_scratch = nc.dram_tensor("gate_scratch", [TB - 1, P, NKEYS, P], F32, kind="Internal").ap()
    h = sb(main, "h", [P, TB, D])
    w_raw = sb(main, "w_raw", [P, RAW, DC, P])
    tile_last = {}

    def load_tile(sp, n):
        if n >= NTILES:
            return
        if n >= RAW:
            sp.wait_ge(w_split, n - RAW + 1)
        sp.dma_start(w_raw[:, n % RAW], A["w_tiles"][:, n]).then_inc(tile_loaded[n % RAW], 16)

    def load_tiles(sp, a, b):
        for n in range(a, b):
            load_tile(sp, n + RAW)

    def tile_hi(act, w, n, first):
        act.wait_ge(tile_loaded[n % RAW], 16 * (n // RAW + 1))
        if n - SPLIT >= first:
            act.wait_ge(psum_full, tile_last[n - SPLIT])
        nc.scalar.activation(w[0][:, n % SPLIT], w_raw[:, n % RAW], ACT.Identity).then_inc(w_hi_done, 1)

    def tile_lo(queue, w, n, engine=nc.vector):
        queue.wait_ge(w_hi_done, n + 1)
        engine.tensor_tensor(w[1][:, n % SPLIT], w_raw[:, n % RAW], w[0][:, n % SPLIT].bitcast(F32),
                                ALU.subtract).then_inc(w_split, 1)

    def pair(stack, name, shape):
        return sb(stack, name + "_hi", shape, F32R), sb(stack, name + "_lo", shape, F32R)

    def opened(pe, g, name):
        old = g.before(name)
        if old:
            pe.wait_ge(evac[old[0]], old[1])
        return psum[g.bank(name)]

    def wait_read(eng, g, name):
        who, value = g.read(name)
        eng.wait_ge(evac[who], value)

    x_block = [sem(f"x_block{t}") for t in range(TB)]
    ssq = sb(main, "ssq", [P, TB])

    with nc.Block() as block:
        @block.sync
        def _(sp):
            for t in range(TB):
                sp.dma_start(h[:, t], A["x"][:, t]).then_inc(x_block[t], 16)
            sp.dma_start(const[:], A["const"]).then_inc(small_loaded, 16)
            sp.dma_start(iota_t[:], A["iota"]).then_inc(small_loaded, 16)
            sp.dma_start(vec[:], A["vec"]).then_inc(small_loaded, 16)
            for n in range(RAW):
                load_tile(sp, n)
            sp.wait_ge(small_loaded, 48)
    loads[0] = 48

    def norm_transpose(name, src, nt, width, gain_at, dst, chunk0=0, parts=None, summed=None, loaded=None,
                       ahead=None):
        nc_chunks = width // P
        stack = ExitStack()
        stat = sb(stack, name + "_stat", [P, 5, nt])
        xs = sb(stack, name + "_xs", [P, nt, width])
        sq = xs[:, 0, :]
        total = stat[:, 0, :] if summed is None else summed
        a_sum, a_sqrt, d_scaled = sem(name + "_sum"), sem(name + "_sqrt"), sem(name + "_scaled")
        a_hi, d_lo = sem(name + "_hi_done"), sem(name + "_lo_done")
        d_rsqrt, a_scaled = sem(name + "_rsqrt"), sem(name + "_act_scaled")
        plan = [((t, c), "dve") for t in range(nt) for c in range(0, nc_chunks, 4)]
        g = Groups(C, plan)
        sums = nt if summed is None else 0
        with nc.Block() as block:
            @block.scalar
            def _(act):
                if summed is None:
                    for t in range(nt):
                        if loaded:
                            act.wait_ge(loaded[t], 16)
                        if t:
                            act.wait_ge(a_sum, t)
                        nc.scalar.activation(sq, src[:, t, :], ACT.Square,
                                             accum_out=stat[:, 0, t:t + 1]).then_inc(a_sum, 1)
                act.wait_ge(a_sum, sums + 1)
                nc.scalar.activation(stat[:, 2, :], stat[:, 1, :], ACT.Sqrt).then_inc(a_sqrt, 1)
                if ahead:
                    tile_hi(act, ahead[0], ahead[1], ahead[1])
                act.wait_ge(d_rsqrt, 1)
                for t in range(2, nt):
                    nc.scalar.activation(xs[:, t, :], src[:, t, :], ACT.Identity,
                                         scale=stat[:, 4, t:t + 1]).then_inc(a_scaled, 1)
                if ahead:
                    for n in range(1, ahead[2]):
                        tile_hi(act, ahead[0], ahead[1] + n, ahead[1])
                if parts:
                    for t in range(nt):
                        wait_read(act, g, (t, nc_chunks - 4))
                        cols = slice(t * P, (t + 1) * P)
                        nc.scalar.activation(parts[0][:, :, cols], dst[:, :, cols], ACT.Identity).then_inc(a_hi, 1)

            @block.vector
            def _(dve):
                if sums:
                    dve.wait_ge(a_sum, sums)
                nc.vector.tensor_scalar(stat[:, 1, :], total, 1.0 / width, EPS, ALU.mult,
                                        ALU.add).then_inc(a_sum, 1)
                dve.wait_ge(a_sqrt, 1)
                link(dve, "dve", nc.vector.reciprocal(stat[:, 2, :], stat[:, 2, :]))
                link(dve, "dve", nc.vector.tensor_tensor(stat[:, 3, :], stat[:, 2, :], stat[:, 2, :], ALU.mult))
                link(dve, "dve", nc.vector.tensor_tensor(stat[:, 3, :], stat[:, 3, :], stat[:, 1, :], ALU.mult))
                link(dve, "dve", nc.vector.tensor_scalar(stat[:, 3, :], stat[:, 3, :], -0.5, 1.5, ALU.mult, ALU.add))
                nc.vector.tensor_tensor(stat[:, 4, :], stat[:, 3, :], stat[:, 2, :], ALU.mult).then_inc(d_rsqrt, 1)
                dve.wait_ge(d_rsqrt, 1)

                def scale(t):
                    nc.vector.tensor_scalar(xs[:, t, :], src[:, t, :], stat[:, 4, t:t + 1], None,
                                            ALU.mult).then_inc(d_scaled, 1)
                def low_part(t):
                    cols = slice(t * P, (t + 1) * P)
                    dve.wait_ge(a_hi, t + 1)
                    nc.vector.tensor_tensor(parts[1][:, :, cols], dst[:, :, cols], parts[0][:, :, cols].bitcast(F32),
                                            ALU.subtract).then_inc(d_lo, 1)
                scale(0)
                scale(1)
                for t in range(nt):
                    for c in range(0, nc_chunks, 4):
                        dve.wait_ge(psum_full, g.full((t, c)))
                        gain = vec[:, gain_at + c:gain_at + c + 4].unsqueeze(2).to_broadcast([P, 4, P])
                        nc.vector.tensor_tensor(
                            dst[:, chunk0 + c:chunk0 + c + 4, t * P:(t + 1) * P],
                            psum[g.bank((t, c))][:].rearrange("p (c t) -> p c t", c=4), gain,
                            ALU.mult).then_inc(dve_evac, 1)
                    if parts and t >= 1:
                        low_part(t - 1)
                if parts:
                    low_part(nt - 1)

            @block.tensor
            def _(pe):
                for t in range(nt):
                    if t < 2:
                        pe.wait_ge(d_scaled, t + 1)
                    else:
                        pe.wait_ge(a_scaled, t - 1)
                    for c in range(0, nc_chunks, 4):
                        bank = opened(pe, g, (t, c))
                        for k in range(4):
                            last = nc.tensor.transpose(bank[:, k * P:(k + 1) * P],
                                                       xs[:, t, (c + k) * P:(c + k + 1) * P], ident)
                        last.then_inc(psum_full, 1)

            if ahead:
                @block.gpsimd
                def _(pool):
                    for n in range(ahead[2]):
                        tile_lo(pool, ahead[0], ahead[1] + n, nc.gpsimd)
        stack.close()

    def three(bank, lhs, rhs, start, stop):
        nc.tensor.matmul(bank, lhs(1), rhs(0), start=start, stop=False)
        nc.tensor.matmul(bank, lhs(0), rhs(1), start=False, stop=False)
        return nc.tensor.matmul(bank, lhs(0), rhs(0), start=False, stop=stop)

    def projected(pe, g, name, w, tile, x, n):
        bank = opened(pe, g, name)
        pe.wait_ge(w_split, tile + 1)
        for c in range(DC):
            last = three(bank[:, 0:n], lambda s: w[s][:, tile % SPLIT, c, :], lambda s: x[s][:, c, :], c == 0, c == DC - 1)
        last.then_inc(psum_full, 1)

    def projected_natural(pe, g, name, w, q, x, t):
        bank = opened(pe, g, name)
        pe.wait_ge(w_split, 4 * q + 4)
        e = 4 * q % SPLIT
        for c in range(DC):
            last = three(bank[:], lambda s: x[s][:, c, t * P:(t + 1) * P], lambda s: w[s][:, e:e + 4, c, :],
                         c == 0, c == DC - 1)
        last.then_inc(psum_full, 1)

    dense = ExitStack()
    zg = sb(dense, "zg", [P, 2, T])
    og = sb(dense, "og", [P, TB, GH * GDV])
    s_q = sb(dense, "s_q", [P, SH // 2, T])
    s_k = sb(dense, "s_k", [P, SH // 2, T])
    s_v = sb(dense, "s_v", [P, TB, SH * SD])
    mixer = dense
    stage = ExitStack()
    x2 = pair(stage, "xn", [P, DC, T])
    w = pair(stage, "w_in", [P, SPLIT, DC, P])
    norm_transpose("nx", h, TB, D, V_MIX, act_t, parts=x2, loaded=x_block, ahead=(w, 0, AHEAD))

    qkv = act_t
    w_low = sb(stage, "w_low", [P, DC, LOWRANK])
    gate_w = sb(stage, "gate_w", [LOWRANK, 2 * P])
    low = sb(stage, "low", [LOWRANK, T])
    conv = sb(stage, "conv", [P, 2, T])
    conv_done, conv_silu = sem("conv_done"), sem("conv_silu")
    plan = [("low", "act")] + [(("conv", n), "dve") for n in range(4)] + [("gate0", "act"), ("gate1", "act")]
    plan += [(("conv", n), "dve") for n in range(4, CONV_BLOCKS)]
    plan += [(("og", t), "act") for t in range(TB)]
    plan += [(("sq", n), "act") for n in range(4)] + [(("sk", n), "dve") for n in range(4)]
    plan += [(("sv", t), "dve") for t in range(TB)]
    g = Groups(C, plan)
    for n in range(4):
        for q in range(2):
            tile_last[4 * (Q_CONV + q) + n] = g.full(("conv", 4 * q + n))
        for q, name in ((Q_OG, ("og", 3)), (Q_SBQ, ("sq", n)), (Q_SBK, ("sk", n)), (Q_SBV, ("sv", 3))):
            tile_last[4 * q + n] = g.full(name)
    with nc.Block() as block:
        @block.sync
        def _(sp):
            sp.dma_start(w_low[:], A["w_low"]).then_inc(small_loaded, 16)
            sp.dma_start(gate_w[:], A["gate_w"]).then_inc(small_loaded, 16)
            load_tiles(sp, 0, 4 * Q_OUT)

        @block.tensor
        def _(pe):
            pe.wait_ge(small_loaded, loads[0] + 32)
            bank = opened(pe, g, "low")
            for c in range(DC):
                last = nc.tensor.matmul(bank[0:LOWRANK, :], w_low[:, c, :], act_t[:, c, :],
                                        start=(c == 0), stop=(c == DC - 1))
            last.then_inc(psum_full, 1)
            for n in range(4):
                projected(pe, g, ("conv", n), w, n, x2, T)
            wait_read(pe, g, "low")
            for n in range(2):
                bank = opened(pe, g, f"gate{n}")
                nc.tensor.matmul(bank[:], gate_w[:, n * P:(n + 1) * P], low[:], start=True,
                                 stop=True).then_inc(psum_full, 1)
            for n in range(4, CONV_BLOCKS):
                projected(pe, g, ("conv", n), w, n, x2, T)
            for t in range(TB):
                projected_natural(pe, g, ("og", t), w, Q_OG, x2, t)
            for q, name in ((Q_SBQ, "sq"), (Q_SBK, "sk")):
                for n in range(4):
                    projected(pe, g, (name, n), w, 4 * q + n, x2, T)
            for t in range(TB):
                projected_natural(pe, g, ("sv", t), w, Q_SBV, x2, t)

        @block.vector
        def _(dve):
            for n in range(AHEAD, SPLIT):
                tile_lo(dve, w, n)
            for n in range(CONV_BLOCKS):
                tap = lambda k: vec[:, V_CONV + n * CONV + k:V_CONV + n * CONV + k + 1]
                y, x = conv[:, n % 2, :], psum[g.bank(("conv", n))]
                if n >= 2:
                    dve.wait_ge(conv_silu, n - 1)
                dve.wait_ge(psum_full, g.full(("conv", n)))
                link(dve, "dve", nc.vector.tensor_scalar(y, x[:], tap(CONV - 1), None, ALU.mult))
                for back in range(1, CONV - 1):
                    link(dve, "dve", nc.vector.scalar_tensor_tensor(
                        out=y[:, back:], in0=x[:, 0:T - back], scalar=tap(CONV - 1 - back), in1=y[:, back:],
                        op0=ALU.mult, op1=ALU.add))
                back = CONV - 1
                nc.vector.scalar_tensor_tensor(out=y[:, back:], in0=x[:, 0:T - back], scalar=tap(0), in1=y[:, back:],
                                               op0=ALU.mult, op1=ALU.add).then_inc(dve_evac, 1)
                tile_lo(dve, w, n + SPLIT)
            for n in range(4 * Q_SBK, 4 * Q_OUT):
                tile_lo(dve, w, n)
            for n in range(4):
                dve.wait_ge(psum_full, g.full(("sk", n)))
                nc.vector.tensor_copy(s_k[:, n, :], psum[g.bank(("sk", n))][:]).then_inc(dve_evac, 1)
            for t in range(TB):
                dve.wait_ge(psum_full, g.full(("sv", t)))
                nc.vector.tensor_copy(s_v[:, t, :], psum[g.bank(("sv", t))][:]).then_inc(dve_evac, 1)

        @block.scalar
        def _(act):
            for n in range(AHEAD, SPLIT):
                tile_hi(act, w, n, 0)
            act.wait_ge(psum_full, g.full("low"))
            nc.scalar.activation(low[:], psum[g.bank("low")][0:LOWRANK, :], ACT.Identity).then_inc(act_evac, 1)
            for n in range(CONV_BLOCKS):
                if n == 4:
                    for m in range(2):
                        act.wait_ge(psum_full, g.full(f"gate{m}"))
                        nc.scalar.activation(zg[:, m, :], psum[g.bank(f"gate{m}")][:], ACT.Identity,
                                             bias=vec[:, V_GATEB + m:V_GATEB + m + 1]).then_inc(act_evac, 1)
                wait_read(act, g, ("conv", n))
                nc.scalar.activation(qkv[:, n, :], conv[:, n % 2, :], ACT.Silu).then_inc(conv_silu, 1)
                tile_hi(act, w, n + SPLIT, 0)
            for t in range(TB):
                act.wait_ge(psum_full, g.full(("og", t)))
                nc.scalar.activation(og[:, t, :], psum[g.bank(("og", t))][:], ACT.Silu).then_inc(act_evac, 1)
            for n in range(4 * Q_SBK, 4 * Q_SBV):
                tile_hi(act, w, n, 0)
            for n in range(4):
                act.wait_ge(psum_full, g.full(("sq", n)))
                nc.scalar.activation(s_q[:, n, :], psum[g.bank(("sq", n))][:], ACT.Identity,
                                     scale=float(SD) ** -0.5).then_inc(act_evac, 1)
                tile_hi(act, w, 4 * Q_SBV + n, 0)
    loads[0] += 32
    stage.close()

    stage = ExitStack()
    masks = sb(stage, "masks", [P, len(LEVELS) + 1, P], U32)
    cum = sb(stage, "cum", [P, 2, TB, P])
    lv_e = sb(stage, "lv_e", [P, 2, 2 * T])
    lv_q = sb(stage, "lv_q", [P, 2, 2, T])
    lv_k = sb(stage, "lv_k", [P, 2, 2, T])
    q_s = sb(stage, "q_s", [P, 2, T])
    q_in = sb(stage, "q_in", [P, 2, T])
    k_dec = sb(stage, "k_dec", [P, 2, T])
    k_nat = sb(stage, "k_nat", [P, 2, TB, P])
    dec = sb(stage, "dec", [P, 2, TB])
    v_nat = sb(stage, "v_nat", [P, TB, GH * GDV])
    scores = sb(stage, "scores", [P, GH, TB, P])
    state = sb(stage, "state", [P, 2, 2, GDV])
    o_gla = sb(stage, "o_gla", [P, TB, GH * GDV])
    gst = sb(stage, "gst", [P, 5, TB * GH])
    tmp = lv_e[:].rearrange("p a b -> p (a b)")
    NL = len(LEVELS)
    names = ["gl_mask", "gl_abs", "gl_ln", "gl_cum", "gl_diff", "gl_exp", "gl_fac", "gl_qin", "gl_kdiff",
             "gl_kexp", "gl_kdec", "gl_sq", "gl_var", "gl_sqrt", "gl_on", "gl_clear", "gl_qs", "gl_decay", "gl_scored"]
    S = {n: sem(n) for n in names}
    plan = [(("vt", x), "act") for x in range(GH)]
    plan += [(("lv", 0, x), "dve") for x in range(GH)]
    plan += [(("kt", x), "act") for x in range(2)]
    plan += [(("lv", l, x), "dve") for l in range(1, NL + 1) for x in range(GH)]
    for t in range(TB):
        plan += [(("o", t, y), "act") for y in range(2)]
        if t < TB - 1:
            plan += [(("st", t), "dve")]
    plan += [(("gt", x), "act") for x in range(GH)]
    g = Groups(C, plan)
    with nc.Block() as block:
        @block.sync
        def _(sp):
            sp.dma_start(masks[:], A["masks"]).then_inc(small_loaded, 16)

        @block.scalar
        def _(act):
            z = zg[:].rearrange("p a b -> p (a b)")
            z2 = lv_q[:, 0].rearrange("p a b -> p (a b)")
            link(act, "act", nc.scalar.activation(z2, z, ACT.Abs))
            link(act, "act", nc.scalar.activation(z2, z2, ACT.Exp, scale=-1.0))
            nc.scalar.activation(z2, z2, ACT.Ln, bias=1.0).then_inc(S["gl_ln"], 1)
            act.wait_ge(S["gl_cum"], 1)
            cf = cum[:].rearrange("p a b c -> p (a b c)")
            nc.scalar.activation(tmp[:, 0:2 * T], cf, ACT.Exp).then_inc(S["gl_exp"], 1)
            nc.scalar.activation(dec[:], cum[:, :, :, P - 1], ACT.Exp).then_inc(S["gl_decay"], 1)
            act.wait_ge(S["gl_kdiff"], 1)
            nc.scalar.activation(tmp[:, 2 * T:4 * T], tmp[:, 2 * T:4 * T], ACT.Exp, scale=-1.0).then_inc(S["gl_kexp"], 1)
            for x in range(GH):
                act.wait_ge(psum_full, g.full(("vt", x)))
                nc.scalar.activation(v_nat[:, :, x * GDV:(x + 1) * GDV],
                                     psum[g.bank(("vt", x))][:].rearrange("p (t d) -> p t d", t=TB),
                                     ACT.Identity).then_inc(act_evac, 1)
            for x in range(2):
                act.wait_ge(psum_full, g.full(("kt", x)))
                nc.scalar.activation(k_nat[:, x], psum[g.bank(("kt", x))][:].rearrange("p (t d) -> p t d", t=TB),
                                     ACT.Identity).then_inc(act_evac, 1)
            for l in range(NL):
                act.wait_ge(S["gl_diff"], l + 1)
                nc.scalar.activation(lv_e[:, l % 2], lv_e[:, l % 2], ACT.Exp).then_inc(S["gl_exp"], 1)
            for t in range(TB):
                for y in range(2):
                    act.wait_ge(psum_full, g.full(("o", t, y)))
                    nc.scalar.activation(o_gla[:, t, :].rearrange("p (x y d) -> p x y d", y=2, d=GDV)[:, :, y, :],
                                         psum[g.bank(("o", t, y))][:, 0:2 * GDV].rearrange("p (x d) -> p x d", x=2),
                                         ACT.Identity).then_inc(act_evac, 1)
            wait_read(act, g, ("o", TB - 1, 1))
            act.wait_ge(S["gl_fac"], 2 * NL)
            nc.scalar.activation(tmp[:, 0:4 * T], o_gla[:].rearrange("p a b -> p (a b)"),
                                 ACT.Square).then_inc(S["gl_sq"], 1)
            act.wait_ge(S["gl_var"], 1)
            nc.scalar.activation(gst[:, 2, :], gst[:, 1, :], ACT.Sqrt).then_inc(S["gl_sqrt"], 1)
            for x in range(GH):
                act.wait_ge(psum_full, g.full(("gt", x)))
                nc.scalar.activation(act_t[:, x, :], psum[g.bank(("gt", x))][:], ACT.Identity,
                                     scale=vec[:, V_GLAG:V_GLAG + 1]).then_inc(act_evac, 1)

        @block.vector
        def _(dve):
            link(dve, "dve", nc.vector.memset(lv_k[:], 0.0))
            nc.vector.memset(lv_q[:, 1], 0.0)
            nc.vector.memset(scores[:], 0.0).then_inc(S["gl_clear"], 1)
            nc.vector.tensor_scalar(q_s[:], qkv[:, 0:2, :], float(GDK) ** -0.5, None, ALU.mult).then_inc(S["gl_qs"], 1)
            dve.wait_ge(S["gl_ln"], 1)
            zf = zg[:].rearrange("p a b -> p (a b)")
            z2 = lv_q[:, 0].rearrange("p a b -> p (a b)")
            link(dve, "dve", nc.vector.scalar_tensor_tensor(out=zf, in0=zf, scalar=0.0, in1=z2,
                                                            op0=ALU.min, op1=ALU.subtract))
            link(dve, "dve", nc.vector.tensor_scalar(zf, zf, 1.0 / GATE_NORM, None, ALU.mult))
            nc.vector.memset(lv_q[:, 0], 0.0)
            for x in range(2):
                for t in range(TB):
                    last = nc.vector.tensor_tensor_scan(cum[:, x, t, :], ones, zg[:, x, t * P:(t + 1) * P], 0.0,
                                                        ALU.mult, ALU.add)
            last.then_inc(S["gl_cum"], 1)
            dve.wait_ge(S["gl_cum"], 1)
            cb = cum[:].rearrange("p a b c -> p (a b) c")
            nc.vector.tensor_tensor(tmp[:, 2 * T:4 * T].rearrange("p (a c) -> p a c", c=P), cb,
                                    cb[:, :, P - 1:P].to_broadcast([P, 2 * TB, P]),
                                    ALU.subtract).then_inc(S["gl_kdiff"], 1)
            qf = lambda a: a.rearrange("p a b -> p (a b)")
            dve.wait_ge(S["gl_exp"], 1)
            dve.wait_ge(S["gl_qs"], 1)
            nc.vector.tensor_tensor(qf(q_in[:]), qf(q_s[:]), tmp[:, 0:2 * T], ALU.mult).then_inc(S["gl_qin"], 1)
            dve.wait_ge(S["gl_kexp"], 1)
            nc.vector.tensor_tensor(qf(k_dec[:]), qf(qkv[:, 2:4, :]), tmp[:, 2 * T:4 * T],
                                    ALU.mult).then_inc(S["gl_kdec"], 1)
            dve.wait_ge(S["gl_kdec"], 1)
            dve.wait_ge(S["gl_qin"], 1)
            dve.wait_ge(small_loaded, loads[0] + 16)

            def halves(a, half):
                return a.rearrange("p (n b) -> p n b", b=2 * half)

            def diff(l):
                half = LEVELS[l]
                n = 2 * T // (2 * half)
                c = halves(cum[:].rearrange("p a b c -> p (a b c)"), half)
                e = halves(lv_e[:, l % 2], half)
                edge = c[:, :, half - 1:half].to_broadcast([P, n, half])
                nc.vector.tensor_tensor(e[:, :, half:], c[:, :, half:], edge, ALU.subtract)
                nc.vector.tensor_tensor(e[:, :, 0:half], edge, c[:, :, 0:half], ALU.subtract).then_inc(S["gl_diff"], 1)

            def factors(l):
                half = LEVELS[l]
                e = halves(lv_e[:, l % 2], half)
                if l >= 2:
                    dve.wait_ge(psum_full, g.full(("lv", l - 1, GH - 1)))
                dve.wait_ge(S["gl_exp"], l + 2)
                nc.vector.tensor_tensor(halves(qf(lv_q[:, l % 2]), half)[:, :, half:],
                                        halves(qf(q_s[:]), half)[:, :, half:], e[:, :, half:],
                                        ALU.mult).then_inc(S["gl_fac"], 1)
                nc.vector.tensor_tensor(halves(qf(lv_k[:, l % 2]), half)[:, :, 0:half],
                                        halves(qf(qkv[:, 2:4, :]), half)[:, :, 0:half], e[:, :, 0:half],
                                        ALU.mult).then_inc(S["gl_fac"], 1)
                dve.wait_ge(S["gl_fac"], 2 * l + 2)

            def keep(l):
                for x in range(GH):
                    dve.wait_ge(psum_full, g.full(("lv", l, x)))
                    nc.vector.copy_predicated(
                        scores[:, x], masks[:, l, :].unsqueeze(1).to_broadcast([P, TB, P]),
                        psum[g.bank(("lv", l, x))][:].rearrange("p (t c) -> p t c", t=TB)).then_inc(dve_evac, 1)
                dve.wait_ge(dve_evac, g.read(("lv", l, GH - 1))[1])

            diff(0)
            for l in range(NL):
                if l + 1 < NL:
                    diff(l + 1)
                factors(l)
                keep(l)
            keep(NL)
            nc.vector.engine_nop().then_inc(S["gl_scored"], 1)
            dve.wait_ge(S["gl_decay"], 1)
            for t in range(TB - 1):
                dve.wait_ge(psum_full, g.full(("st", t)))
                b = psum[g.bank(("st", t))]
                for x in range(2):
                    for y in range(2):
                        r = slice(GDK * y, GDK * y + GDK)
                        new = state[r, t % 2, x, :]
                        add = b[r, 2 * x * GDV + y * GDV:2 * x * GDV + (y + 1) * GDV]
                        if t == 0:
                            last = nc.vector.tensor_copy(new, add)
                        else:
                            last = nc.vector.scalar_tensor_tensor(out=new, in0=state[r, (t - 1) % 2, x, :],
                                                                  scalar=dec[r, x, t:t + 1], in1=add,
                                                                  op0=ALU.mult, op1=ALU.add)
                last.then_inc(dve_evac, 1)
                dve.wait_ge(dve_evac, g.read(("st", t))[1])
            dve.wait_ge(S["gl_sq"], 1)
            link(dve, "dve", nc.vector.reduce_sum(gst[:, 0, :], tmp[:, 0:4 * T].rearrange("p (n d) -> p n d", d=GDV),
                                                  axis=AX.X))
            nc.vector.tensor_scalar(gst[:, 1, :], gst[:, 0, :], 1.0 / GDV, EPS, ALU.mult, ALU.add).then_inc(S["gl_var"], 1)
            dve.wait_ge(S["gl_sqrt"], 1)
            link(dve, "dve", nc.vector.reciprocal(gst[:, 2, :], gst[:, 2, :]))
            link(dve, "dve", nc.vector.tensor_tensor(gst[:, 3, :], gst[:, 2, :], gst[:, 2, :], ALU.mult))
            link(dve, "dve", nc.vector.tensor_tensor(gst[:, 3, :], gst[:, 3, :], gst[:, 1, :], ALU.mult))
            link(dve, "dve", nc.vector.tensor_scalar(gst[:, 3, :], gst[:, 3, :], -0.5, 1.5, ALU.mult, ALU.add))
            link(dve, "dve", nc.vector.tensor_tensor(gst[:, 4, :], gst[:, 3, :], gst[:, 2, :], ALU.mult))
            of = o_gla[:].rearrange("p t (x d) -> p (t x) d", d=GDV)
            link(dve, "dve", nc.vector.tensor_tensor(of, of, gst[:, 4, :].unsqueeze(2).to_broadcast([P, TB * GH, GDV]),
                                                     ALU.mult))
            nc.vector.tensor_tensor(o_gla[:], o_gla[:], og[:], ALU.mult).then_inc(S["gl_on"], 1)

        @block.tensor
        def _(pe):
            for x in range(GH):
                bank = opened(pe, g, ("vt", x))
                for t in range(TB):
                    last = nc.tensor.transpose(bank[:, t * P:(t + 1) * P], qkv[:, 4 + x, t * P:(t + 1) * P], ident)
                last.then_inc(psum_full, 1)

            def level(l, q, k):
                for x in range(GH):
                    bank = opened(pe, g, ("lv", l, x))
                    r = slice(GDK * (x % 2), GDK * (x % 2) + GDK)
                    for t in range(TB):
                        c = slice(t * P, (t + 1) * P)
                        last = nc.tensor.matmul(bank[:, c], k[r, x // 2, c], q[r, x // 2, c], start=True, stop=True)
                    last.then_inc(psum_full, 1)
            pe.wait_ge(S["gl_qs"], 1)
            level(0, q_s, qkv[:, 2:4, :])
            pe.wait_ge(S["gl_kdec"], 1)
            for x in range(2):
                bank = opened(pe, g, ("kt", x))
                for t in range(TB):
                    last = nc.tensor.transpose(bank[:, t * P:(t + 1) * P], k_dec[:, x, t * P:(t + 1) * P], ident)
                last.then_inc(psum_full, 1)
            pe.wait_ge(S["gl_clear"], 1)
            for l in range(NL):
                pe.wait_ge(S["gl_fac"], 2 * l + 2)
                level(l + 1, lv_q[:, l % 2], lv_k[:, l % 2])
            pe.wait_ge(S["gl_scored"], 1)
            pe.wait_ge(S["gl_qin"], 1)
            wait_read(pe, g, ("kt", 1))
            wait_read(pe, g, ("vt", GH - 1))
            for t in range(TB):
                if t:
                    wait_read(pe, g, ("st", t - 1))
                for y in range(2):
                    bank = opened(pe, g, ("o", t, y))
                    r = slice(GDK * y, GDK * y + GDK)
                    for x in (y, y + 2):
                        o = bank[:, (x // 2) * GDV:(x // 2 + 1) * GDV]
                        last = nc.tensor.matmul(o, scores[:, x, t, :], v_nat[:, t, x * GDV:(x + 1) * GDV],
                                                start=True, stop=(t == 0))
                        if t:
                            last = nc.tensor.matmul(o, q_in[r, x // 2, t * P:(t + 1) * P],
                                                    state[r, (t - 1) % 2, x // 2, :], start=False, stop=True)
                    last.then_inc(psum_full, 1)
                if t < TB - 1:
                    bank = opened(pe, g, ("st", t))
                    for x in range(2):
                        last = nc.tensor.matmul(bank[:, 2 * x * GDV:2 * (x + 1) * GDV], k_nat[:, x, t, :],
                                                v_nat[:, t, 2 * x * GDV:2 * (x + 1) * GDV], start=True, stop=True)
                    last.then_inc(psum_full, 1)
            pe.wait_ge(S["gl_on"], 1)
            for x in range(GH):
                bank = opened(pe, g, ("gt", x))
                for t in range(TB):
                    last = nc.tensor.transpose(bank[:, t * P:(t + 1) * P], o_gla[:, t, x * GDV:(x + 1) * GDV], ident)
                last.then_inc(psum_full, 1)
    loads[0] += 16
    stage.close()

    stage = ExitStack()
    ZR, PR, WR, LC, LP = 4, 3, 2, 2, 3
    zb = sb(stage, "zb", [P, ZR, STOT])
    sp_ = sb(stage, "sp", [P, PR, STOT])
    wb = sb(stage, "wb", [P, WR, STOT])
    o_sb = sb(stage, "o_sb", [P, TB, SH * SD])
    s_names = ["sb_ln", "sb_sp", "sb_spm", "sb_arg", "sb_w", "sb_wm"]
    S = {n: sem(n) for n in s_names}
    plan = []
    for i in range(SH + LP):
        if i < SH:
            plan += [(("z", i, s), "dve") for s in range(TB)]
        if LC <= i < SH + LC:
            plan += [(("c", i - LC, s), "dve") for s in range(TB)]
        if i >= LP:
            plan += [(("pv", i - LP), "act")]
    g = Groups(C, plan)
    with nc.Block() as block:
        @block.tensor
        def _(pe):
            for i in range(SH + LP):
                if i < SH:
                    x, r = i // 2, slice(SD * (i % 2), SD * (i % 2) + SD)
                    for s in range(TB):
                        bank = opened(pe, g, ("z", i, s))
                        nc.tensor.matmul(bank[:, 0:SLEN[s]], s_k[r, x, s * P:(s + 1) * P], s_q[r, x, s * P:T],
                                         start=True, stop=True).then_inc(psum_full, 1)
                if LC <= i < SH + LC:
                    n = i - LC
                    pe.wait_ge(S["sb_spm"], n + 1)
                    for s in range(TB):
                        bank = opened(pe, g, ("c", n, s))
                        for s2 in range(s, TB):
                            last = nc.tensor.matmul(bank[:, (s2 - s) * P:SLEN[s]], tri if s2 == s else ones,
                                                    sp_[:, n % PR, SOFF[s2]:SOFF[s2] + SLEN[s2]],
                                                    start=(s2 == s), stop=(s2 == TB - 1))
                        last.then_inc(psum_full, 1)
                if i >= LP:
                    n = i - LP
                    pe.wait_ge(S["sb_wm"], n + 1)
                    bank = opened(pe, g, ("pv", n))
                    for t in range(TB):
                        for s in range(t + 1):
                            at = SOFF[s] + (t - s) * P
                            last = nc.tensor.matmul(bank[:, t * SD:(t + 1) * SD], wb[:, n % WR, at:at + P],
                                                    s_v[:, s, n * SD:(n + 1) * SD], start=(s == 0), stop=(s == t))
                    last.then_inc(psum_full, 1)

        @block.scalar
        def _(act):
            for i in range(SH + LP):
                if i < SH:
                    wait_read(act, g, ("z", i, TB - 1))
                    if i >= PR:
                        act.wait_ge(psum_full, g.full(("c", i - PR, TB - 1)))
                    t = sp_[:, i % PR, :]
                    link(act, "act", nc.scalar.activation(t, zb[:, i % ZR, :], ACT.Abs))
                    link(act, "act", nc.scalar.activation(t, t, ACT.Exp, scale=-1.0))
                    nc.scalar.activation(t, t, ACT.Ln, bias=1.0).then_inc(S["sb_ln"], 1)
                if LC <= i < SH + LC:
                    n = i - LC
                    act.wait_ge(S["sb_arg"], n + 1)
                    nc.scalar.activation(wb[:, n % WR, :], wb[:, n % WR, :], ACT.Exp).then_inc(S["sb_w"], 1)
                if i >= LP:
                    n = i - LP
                    act.wait_ge(psum_full, g.full(("pv", n)))
                    nc.scalar.activation(o_sb[:, :, n * SD:(n + 1) * SD],
                                         psum[g.bank(("pv", n))][:, 0:TB * SD].rearrange("p (t d) -> p t d", t=TB),
                                         ACT.Identity).then_inc(act_evac, 1)

        @block.vector
        def _(dve):
            for i in range(SH + LC):
                if i < SH:
                    for s in range(TB):
                        dve.wait_ge(psum_full, g.full(("z", i, s)))
                        nc.vector.tensor_copy(zb[:, i % ZR, SOFF[s]:SOFF[s] + SLEN[s]],
                                              psum[g.bank(("z", i, s))][:, 0:SLEN[s]]).then_inc(dve_evac, 1)
                if i >= LC:
                    n = i - LC
                    if n >= WR:
                        dve.wait_ge(psum_full, g.full(("pv", n - WR)))
                    for s in range(TB):
                        o = slice(SOFF[s], SOFF[s] + SLEN[s])
                        dve.wait_ge(psum_full, g.full(("c", n, s)))
                        nc.vector.tensor_tensor(wb[:, n % WR, o], zb[:, n % ZR, o],
                                                psum[g.bank(("c", n, s))][:, 0:SLEN[s]],
                                                ALU.subtract).then_inc(dve_evac, 1)
                    dve.wait_ge(dve_evac, g.read(("c", n, TB - 1))[1])
                    nc.vector.engine_nop().then_inc(S["sb_arg"], 1)
                if i < SH:
                    dve.wait_ge(S["sb_ln"], i + 1)
                    nc.vector.scalar_tensor_tensor(out=sp_[:, i % PR, :], in0=zb[:, i % ZR, :], scalar=0.0,
                                                   in1=sp_[:, i % PR, :], op0=ALU.max,
                                                   op1=ALU.add).then_inc(S["sb_sp"], 1)

        @block.gpsimd
        def _(pool):
            def strict(buf, done):
                for s in range(TB):
                    piece = buf[:, SOFF[s]:SOFF[s] + P]
                    last = nc.gpsimd.affine_select(out=piece, in_=piece, compare_op=ALU.is_gt, fill=0.0, base=0,
                                                   pattern=[[1, P]], channel_multiplier=-1)
                last.then_inc(done, 1)
            for i in range(SH + LC):
                if i >= LC:
                    pool.wait_ge(S["sb_w"], i - LC + 1)
                    strict(wb[:, (i - LC) % WR, :], S["sb_wm"])
                if i < SH:
                    pool.wait_ge(S["sb_sp"], i + 1)
                    strict(sp_[:, i % PR, :], S["sb_spm"])
    norm_transpose("nsb", o_sb, TB, SH * SD, V_SBG, act_t, GH * GDV // P)
    stage.close()
    mixer.close()

    def add_projection(name, q0, w=None):
        stage = ExitStack()
        x = pair(stage, name + "_x", [P, DC, T])
        split = w is not None
        if not split:
            w = pair(stage, name + "_w", [P, SPLIT, DC, P])
        x_hi_done, x_split = sem(name + "_x_hi"), sem(name + "_x_split")
        squares, squared = sb(stage, name + "_sq", [P, D]), sem(name + "_squared")
        g = Groups(C, [((t, half), "dve") for t in range(TB) for half in range(2)])
        for n in range(8):
            tile_last[4 * q0 + n] = g.full((TB - 1, n // 4))
        with nc.Block() as block:
            @block.sync
            def _(sp):
                load_tiles(sp, 4 * q0 + (RAW if split else 0), 4 * q0 + 8)

            @block.tensor
            def _(pe):
                for t in range(TB):
                    pe.wait_ge(x_split, t + 1)
                    for half in range(2):
                        projected_natural(pe, g, (t, half), w, q0 + half, x, t)

            @block.scalar
            def _(act):
                for t in range(TB):
                    cols = slice(t * P, (t + 1) * P)
                    nc.scalar.activation(x[0][:, :, cols], act_t[:, :, cols], ACT.Identity).then_inc(x_hi_done, 1)
                    if t < 2 and not split:
                        for n in range(4 * t, 4 * t + 4):
                            tile_hi(act, w, 4 * q0 + n, 4 * q0)
                for t in range(TB):
                    wait_read(act, g, (t, 1))
                    if t:
                        act.wait_ge(squared, t)
                    nc.scalar.activation(squares[:], h[:, t, :], ACT.Square, accum_out=ssq[:, t:t + 1]).then_inc(squared, 1)

            @block.vector
            def _(dve):
                for t in range(TB):
                    cols = slice(t * P, (t + 1) * P)
                    dve.wait_ge(x_hi_done, t + 1)
                    nc.vector.tensor_tensor(x[1][:, :, cols], act_t[:, :, cols], x[0][:, :, cols].bitcast(F32),
                                            ALU.subtract).then_inc(x_split, 1)
                    if t < 2 and not split:
                        for n in range(4 * t, 4 * t + 4):
                            tile_lo(dve, w, 4 * q0 + n)
                for t in range(TB):
                    for half in range(2):
                        dve.wait_ge(psum_full, g.full((t, half)))
                        o = h[:, t, 512 * half:512 * half + 512]
                        nc.vector.tensor_tensor(o, o, psum[g.bank((t, half))][:], ALU.add).then_inc(dve_evac, 1)
        stage.close()

    add_projection("wout", Q_OUT)

    xa = ExitStack()
    xk = sb(xa, "xk", [P, DC, M])
    xv = sb(xa, "xv", [P, MB, D])
    xq = sb(xa, "xq", [P, DC, T])
    stage = ExitStack()
    mem = sb(stage, "mem", [P, MB, D])
    mem_t = sb(stage, "mem_t", [P, DC, M])
    m2 = pair(stage, "mem", [P, DC, M])
    w = pair(stage, "w_xkv", [P, SPLIT, DC, P])
    with nc.Block() as block:
        @block.sync
        def _(sp):
            sp.dma_start(mem[:], A["mem"]).then_inc(small_loaded, 16)
            sp.wait_ge(small_loaded, loads[0] + 16)
    loads[0] += 16
    norm_transpose("nmem", mem, MB, D, V_MEM, mem_t, parts=m2, ahead=(w, 4 * Q_XK, AHEAD))
    plan = [(("k", n), "dve") for n in range(DC)]
    plan += [(("v", half, t), "dve") for half in range(2) for t in range(MB)]
    g = Groups(C, plan)
    for n in range(8):
        tile_last[4 * Q_XK + n] = g.full(("k", n))
        tile_last[4 * Q_XV + n] = g.full(("v", n // 4, MB - 1))
    with nc.Block() as block:
        @block.sync
        def _(sp):
            load_tiles(sp, 4 * Q_XK, 4 * Q_XQ)

        @block.tensor
        def _(pe):
            for n in range(DC):
                projected(pe, g, ("k", n), w, 4 * Q_XK + n, m2, M)
            for q in range(2):
                for t in range(MB):
                    projected_natural(pe, g, ("v", q, t), w, Q_XV + q, m2, t)

        @block.scalar
        def _(act):
            for n in range(4 * Q_XK + AHEAD, 4 * Q_XQ):
                tile_hi(act, w, n, 4 * Q_XK)

        @block.vector
        def _(dve):
            for n in range(AHEAD, SPLIT):
                tile_lo(dve, w, 4 * Q_XK + n)
            for n in range(DC):
                dve.wait_ge(psum_full, g.full(("k", n)))
                nc.vector.tensor_copy(xk[:, n, :], psum[g.bank(("k", n))][:, 0:M]).then_inc(dve_evac, 1)
                tile_lo(dve, w, 4 * Q_XV + n)
            for half in range(2):
                for t in range(MB):
                    dve.wait_ge(psum_full, g.full(("v", half, t)))
                    nc.vector.tensor_copy(xv[:, t, 512 * half:512 * half + 512],
                                          psum[g.bank(("v", half, t))][:]).then_inc(dve_evac, 1)
    stage.close()
    stage = ExitStack()
    x2 = pair(stage, "xh", [P, DC, T])
    w = pair(stage, "w_xq", [P, SPLIT, DC, P])
    norm_transpose("nxa", h, TB, D, V_XA, act_t, parts=x2, summed=ssq[:], ahead=(w, 4 * Q_XQ, AHEAD))
    g = Groups(C, [(n, "act") for n in range(DC)])
    for n in range(8):
        tile_last[4 * Q_XQ + n] = g.full(n)
    with nc.Block() as block:
        @block.sync
        def _(sp):
            load_tiles(sp, 4 * Q_XQ, 4 * Q_XO)

        @block.tensor
        def _(pe):
            for n in range(DC):
                projected(pe, g, n, w, 4 * Q_XQ + n, x2, T)

        @block.vector
        def _(dve):
            for n in range(4 * Q_XQ + AHEAD, 4 * Q_XO):
                tile_lo(dve, w, n)

        @block.scalar
        def _(act):
            for n in range(4 * Q_XQ + AHEAD, 4 * Q_XO):
                tile_hi(act, w, n, 4 * Q_XQ)
            for n in range(DC):
                act.wait_ge(psum_full, g.full(n))
                nc.scalar.activation(xq[:, n, :], psum[g.bank(n)][:], ACT.Identity).then_inc(act_evac, 1)
    stage.close()
    w_xo = pair(xa, "w_xo", [P, SPLIT, DC, P])
    stage = ExitStack()
    prob = sb(stage, "prob", [P, 2, TB, M])
    prob_t = sb(stage, "prob_t", [P, 2, MB, T])
    xst = sb(stage, "xst", [P, XH, 4, TB])
    x_max, x_exp, x_norm = sem("x_max"), sem("x_exp"), sem("x_norm")
    XSCALE = float(XD) ** -0.5
    plan = []
    for i in range(XH + 1):
        if i < XH:
            plan += [(("s", i, u), "act") for u in range(TB // 2)]
        if i >= 1:
            plan += [(("p", i - 1, m), "act") for m in range(MB)]
            plan += [(("o", i - 1, c), "dve") for c in range(2)]
    g = Groups(C, plan)
    with nc.Block() as block:
        @block.sync
        def _(sp):
            load_tiles(sp, 4 * Q_XO, 4 * Q_XO + SPLIT - RAW)

        @block.gpsimd
        def _(pool):
            for n in range(SPLIT):
                tile_lo(pool, w_xo, 4 * Q_XO + n, nc.gpsimd)

        @block.tensor
        def _(pe):
            for i in range(XH + 1):
                if i < XH:
                    for u in range(TB // 2):
                        bank = opened(pe, g, ("s", i, u))
                        for v in range(2):
                            t = 2 * u + v
                            for c in range(2):
                                last = nc.tensor.matmul(bank[:, v * M:(v + 1) * M],
                                                        xq[:, 2 * i + c, t * P:(t + 1) * P], xk[:, 2 * i + c, :],
                                                        start=(c == 0), stop=(c == 1))
                        last.then_inc(psum_full, 1)
                if i >= 1:
                    n = i - 1
                    pe.wait_ge(x_norm, n + 1)
                    for m in range(MB):
                        bank = opened(pe, g, ("p", n, m))
                        for t in range(TB):
                            last = nc.tensor.transpose(bank[:, t * P:(t + 1) * P],
                                                       prob[:, n % 2, t, m * P:(m + 1) * P], ident)
                        last.then_inc(psum_full, 1)
                    wait_read(pe, g, ("p", n, MB - 1))
                    for c in range(2):
                        bank = opened(pe, g, ("o", n, c))
                        f = (2 * n + c) * P
                        for m in range(MB):
                            last = nc.tensor.matmul(bank[:], xv[:, m, f:f + P], prob_t[:, n % 2, m, :],
                                                    start=(m == 0), stop=(m == MB - 1))
                        last.then_inc(psum_full, 1)

        @block.scalar
        def _(act):
            for i in range(XH + 1):
                if i < XH:
                    if i >= 2:
                        act.wait_ge(psum_full, g.full(("p", i - 2, MB - 1)))
                    act.wait_ge(x_max, i + 1)
                    for t in range(TB):
                        b = psum[g.bank(("s", i, t // 2))]
                        ins = nc.scalar.activation(prob[:, i % 2, t, :], b[:, (t % 2) * M:(t % 2 + 1) * M], ACT.Exp,
                                                   bias=xst[:, i, 1, t:t + 1], scale=XSCALE,
                                                   accum_out=xst[:, i, 2, t:t + 1])
                        if t % 2:
                            ins.then_inc(act_evac, 1)
                if i >= 1:
                    for m in range(MB):
                        act.wait_ge(psum_full, g.full(("p", i - 1, m)))
                        nc.scalar.activation(prob_t[:, (i - 1) % 2, m, :], psum[g.bank(("p", i - 1, m))][:],
                                             ACT.Identity).then_inc(act_evac, 1)
                if i < SPLIT // 2:
                    for n in range(2 * i, 2 * i + 2):
                        tile_hi(act, w_xo, 4 * Q_XO + n, 4 * Q_XO)

        @block.vector
        def _(dve):
            for i in range(XH + 1):
                if i < XH:
                    for u in range(2):
                        dve.wait_ge(psum_full, g.full(("s", i, u)))
                        ins = nc.vector.reduce_max(xst[:, i, 0, 2 * u:2 * u + 2],
                                                   psum[g.bank(("s", i, u))][:].rearrange("p (t m) -> p t m", t=2),
                                                   axis=AX.X)
                    link(dve, "dve", ins)
                    nc.vector.tensor_scalar(xst[:, i, 1, :], xst[:, i, 0, :], -XSCALE, None, ALU.mult).then_inc(x_max, 1)
                    wait_read(dve, g, ("s", i, 1))
                    link(dve, "dve", nc.vector.reciprocal(xst[:, i, 3, :], xst[:, i, 2, :]))
                    nc.vector.tensor_tensor(prob[:, i % 2], prob[:, i % 2],
                                            xst[:, i, 3, :].unsqueeze(2).to_broadcast([P, TB, M]),
                                            ALU.mult).then_inc(x_norm, 1)
                if i >= 1:
                    for c in range(2):
                        dve.wait_ge(psum_full, g.full(("o", i - 1, c)))
                        nc.vector.tensor_copy(act_t[:, 2 * (i - 1) + c, :],
                                              psum[g.bank(("o", i - 1, c))][:]).then_inc(dve_evac, 1)
    stage.close()
    add_projection("xo", Q_XO, w_xo)
    xa.close()

    stage = ExitStack()
    x2 = pair(stage, "xf", [P, DC, T])
    w = pair(stage, "w_pq", [P, SPLIT, DC, P])
    norm_transpose("nffn", h, TB, D, V_FFN, act_t, parts=x2, summed=ssq[:], ahead=(w, 4 * Q_PQ, RAW))
    ROWS, RW = 10, 8
    NC = ROWS * RW
    HS = TB * TOPK
    keys = sb(stage, "keys", [P, HP, NKEYS])
    pq = sb(stage, "pq", [P, 2, T])
    ps = sb(stage, "ps", [P, 4, TB, NKEYS])
    pw = sb(stage, "pw", [P, 2, TB, NKEYS])
    top_v = sb(stage, "top_v", [P, 4, TB, TOPK])
    top_i = sb(stage, "top_i", [P, 4, TB, TOPK], U32)
    cand = sb(stage, "cand", [P, TB, NC])
    cw = sb(stage, "cw", [P, TB, NC])
    best = sb(stage, "best", [P, TB, TOPK])
    pos = sb(stage, "pos", [P, TB, TOPK], U32)
    posx = sb(stage, "posx", [P, 2, HS], U32)
    posf = sb(stage, "posf", [P, 2, HS])
    extra = sb(stage, "extra", [P, 3, HS])
    rank = sb(stage, "rank", [P, 2, HS])
    idxf = sb(stage, "idxf", [P, 2, 2, TB, TOPK])
    picked = sb(stage, "picked", [P, 2, 2, HS, TOPK])
    triple = sb(stage, "triple", [P, TB, 3, SLOTS])
    gs = sb(stage, "gs", [P, 2, TB * PH])
    r_top, r_diff, r_hot, r_index, r_exp, r_triple = (
        sem(x) for x in ("r_top", "r_diff", "r_hot", "r_index", "r_exp", "r_triple"))
    plan = []
    for i in range(HP):
        plan += [(("q", i), "act"), (("s", i), "act")]
    plan += [(("t", t), "act") for t in range(TB)]
    g = Groups(C, plan)
    for n in range(HP):
        tile_last[4 * Q_PQ + n] = g.full(("q", n))
    with nc.Block() as block:
        @block.sync
        def _(sp):
            sp.dma_start(keys[:], A["keys"]).then_inc(small_loaded, 16)
            load_tiles(sp, 4 * Q_PQ, 4 * Q_PQ + 2 * SPLIT)
            sp.dma_start(h_scratch, h[:]).then_inc(stored, 16)
            for s in range(2):
                sp.dma_start(xf_scratch[s], x2[s][:].bitcast(F32)).then_inc(stored, 16)
            load_tiles(sp, 4 * Q_PQ + 2 * SPLIT, NTILES)
            sp.wait_ge(stored, 48)

        @block.tensor
        def _(pe):
            for i in range(HP):
                projected(pe, g, ("q", i), w, 4 * Q_PQ + i, x2, T)
                if i == 0:
                    pe.wait_ge(small_loaded, loads[0] + 16)
                wait_read(pe, g, ("q", i))
                bank = opened(pe, g, ("s", i))
                for t in range(TB):
                    last = nc.tensor.matmul(bank[:, t * P:(t + 1) * P], pq[:, i % 2, t * P:(t + 1) * P],
                                            keys[:, i, :], start=True, stop=True)
                last.then_inc(psum_full, 1)
            pe.wait_ge(r_triple, 1)
            for t in range(TB):
                bank = opened(pe, g, ("t", t))
                for s in range(3):
                    last = nc.tensor.transpose(bank[:, s * P:(s + 1) * P], triple[:, t, s, :], ident)
                last.then_inc(psum_full, 1)

        @block.gpsimd
        def _(pool):
            n = RAW
            for x in range(PH - 1):
                while n < min(HP, 3 * x + 10):
                    tile_lo(pool, w, 4 * Q_PQ + n, nc.gpsimd)
                    n += 1
                pool.wait_ge(r_hot, x + 1)
                pick = picked[:, x % 2].rearrange("p s (t k) a -> p (s t) k a", k=TOPK)
                nc.gpsimd.tensor_tensor(
                    pick, pick, idxf[:, x % 2].rearrange("p s t a -> p (s t) a").unsqueeze(2).to_broadcast(
                        [P, 2 * TB, TOPK, TOPK]), ALU.mult).then_inc(r_index, 1)

        @block.scalar
        def _(act):
            for i in range(HP):
                act.wait_ge(psum_full, g.full(("q", i)))
                if i >= 2:
                    act.wait_ge(psum_full, g.full(("s", i - 2)))
                nc.scalar.activation(pq[:, i % 2, :], psum[g.bank(("q", i))][:], ACT.Identity).then_inc(act_evac, 1)
                act.wait_ge(psum_full, g.full(("s", i)))
                if i >= 4:
                    act.wait_ge(r_top, i - 3)
                nc.scalar.activation(ps[:, i % 4], psum[g.bank(("s", i))][:].rearrange("p (t n) -> p t n", t=TB),
                                     ACT.Identity).then_inc(act_evac, 1)
                if i + RAW < HP:
                    tile_hi(act, w, 4 * Q_PQ + i + RAW, 4 * Q_PQ)
            act.wait_ge(r_diff, PH)
            nc.scalar.activation(triple[:, :, 2, :], triple[:, :, 2, :], ACT.Exp).then_inc(r_exp, 1)
            for t in range(TB):
                act.wait_ge(psum_full, g.full(("t", t)))
                nc.scalar.activation(slot_t[:, :, t * P:(t + 1) * P],
                                     psum[g.bank(("t", t))][:, 0:3 * P].rearrange("p (s t) -> p s t", s=3),
                                     ACT.Identity).then_inc(act_evac, 1)

        @block.vector
        def _(dve):
            def lockstep(*chains):
                chains = list(chains)
                while chains:
                    last = None
                    for chain in list(chains):
                        ins = next(chain, None)
                        if ins is None:
                            chains.remove(chain)
                        else:
                            last = ins
                    if last is not None:
                        link(dve, "dve", last)

            def one_after_another(*chains):
                for chain in chains:
                    yield from chain

            def top(i):
                wait_read(dve, g, ("s", i))
                v, n, p, q = top_v[:, i % 4], top_i[:, i % 4], ps[:, i % 4], pw[:, i % 2]
                for t in range(TB):
                    ins = nc.vector.max(v[:, t, 0:8], p[:, t, :])
                yield ins
                for t in range(TB):
                    nc.vector.max_index(n[:, t, 0:8], v[:, t, 0:8], p[:, t, :])
                    ins = nc.vector.match_replace(q[:, t, :], v[:, t, 0:8], p[:, t, :], NEG)
                yield ins
                for t in range(TB):
                    ins = nc.vector.max(v[:, t, 8:16], q[:, t, :])
                nc.vector.engine_nop().then_inc(r_top, 1)
                yield ins
                for t in range(TB):
                    ins = nc.vector.max_index(n[:, t, 8:16], v[:, t, 8:16], q[:, t, :])
                yield ins

            def combine(x):
                r = 2 * (x % 2)
                va, vb, index = top_v[:, r], top_v[:, r + 1], top_i[:, r:r + 2]
                c4 = cand[:].rearrange("p t (r c) -> p t r c", c=RW)
                nc.vector.tensor_copy(idxf[:, x % 2], index)
                nc.vector.tensor_tensor(cand[:, :, 0:2 * RW], va[:, :, 0:1].to_broadcast([P, TB, 2 * RW]), vb, ALU.add)
                nc.vector.tensor_tensor(c4[:, :, 2:9, :], va[:, :, 1:8].unsqueeze(3).to_broadcast([P, TB, 7, RW]),
                                        vb[:, :, 0:RW].unsqueeze(2).to_broadcast([P, TB, 7, RW]), ALU.add)
                yield nc.vector.tensor_tensor(c4[:, :, 9, :], va[:, :, 8:16],
                                              vb[:, :, 0:1].to_broadcast([P, TB, RW]), ALU.add)
                for t in range(TB):
                    ins = nc.vector.max(best[:, t, 0:8], cand[:, t, :])
                yield ins
                for t in range(TB):
                    nc.vector.max_index(pos[:, t, 0:8], best[:, t, 0:8], cand[:, t, :])
                    ins = nc.vector.match_replace(cw[:, t, :], best[:, t, 0:8], cand[:, t, :], NEG)
                yield ins
                for t in range(TB):
                    ins = nc.vector.max(best[:, t, 8:16], cw[:, t, :])
                yield ins
                for t in range(TB):
                    ins = nc.vector.max_index(pos[:, t, 8:16], best[:, t, 8:16], cw[:, t, :])
                yield ins
                nc.vector.tensor_tensor(triple[:, :, 2, x * TOPK:(x + 1) * TOPK], best[:],
                                        best[:, :, 0:1].to_broadcast([P, TB, TOPK]), ALU.subtract).then_inc(r_diff, 1)
                pf = pos[:].rearrange("p t k -> p (t k)")
                nc.vector.tensor_scalar(posx[:, 0, :], pf, 3, None, ALU.logical_shift_right)
                yield nc.vector.tensor_scalar(posx[:, 1, :], pf, RW - 1, None, ALU.bitwise_and)
                yield nc.vector.tensor_copy(posf[:], posx[:])
                row, col = posf[:, 0, :], posf[:, 1, :]
                end, shift, moved = extra[:, 0, :], extra[:, 1, :], extra[:, 2, :]
                a, b = rank[:, 0, :], rank[:, 1, :]
                nc.vector.tensor_scalar(end, row, float(ROWS - 1), None, ALU.is_equal)
                nc.vector.tensor_scalar(shift, row, 1.0, float(RW), ALU.is_equal, ALU.mult)
                yield nc.vector.tensor_scalar(a, row, -1.0, 0.0, ALU.add, ALU.max)
                yield nc.vector.tensor_tensor(moved, end, col, ALU.mult)
                nc.vector.tensor_tensor(a, a, moved, ALU.add)
                yield nc.vector.tensor_tensor(b, col, moved, ALU.subtract)
                yield nc.vector.tensor_tensor(b, b, shift, ALU.add)
                nc.vector.tensor_tensor(
                    picked[:, x % 2], rank[:].unsqueeze(3).to_broadcast([P, 2, HS, TOPK]),
                    iota16.unsqueeze(1).unsqueeze(1).to_broadcast([P, 2, HS, TOPK]), ALU.is_equal).then_inc(r_hot, 1)

            def finish(x):
                if x < PH - 1:
                    dve.wait_ge(r_index, x + 1)
                else:
                    dve.wait_ge(r_hot, PH)
                    pick = picked[:, x % 2].rearrange("p s (t k) a -> p (s t) k a", k=TOPK)
                    yield nc.vector.tensor_tensor(
                        pick, pick, idxf[:, x % 2].rearrange("p s t a -> p (s t) a").unsqueeze(2).to_broadcast(
                            [P, 2 * TB, TOPK, TOPK]), ALU.mult)
                for s in range(2):
                    ins = nc.vector.reduce_sum(triple[:, :, s, x * TOPK:(x + 1) * TOPK],
                                               picked[:, x % 2, s].rearrange("p (t k) a -> p t k a", k=TOPK), axis=AX.X)
                yield ins

            lockstep(one_after_another(top(0), top(1)))
            for x in range(1, PH):
                finished = [finish(x - 2)] if x >= 2 else []
                lockstep(combine(x - 1), one_after_another(top(2 * x), top(2 * x + 1), *finished))
            lockstep(one_after_another(combine(PH - 1), finish(PH - 2), finish(PH - 1)))
            dve.wait_ge(r_exp, 1)
            gate = triple[:, :, 2, :].rearrange("p t (x k) -> p t x k", k=TOPK)
            gs4 = lambda n: gs[:, n, :].rearrange("p (t x) -> p t x", x=PH)
            link(dve, "dve", nc.vector.reduce_sum(gs4(0), gate, axis=AX.X))
            link(dve, "dve", nc.vector.reciprocal(gs[:, 1, :], gs[:, 0, :]))
            nc.vector.tensor_tensor(gate, gate, gs4(1).unsqueeze(3).to_broadcast([P, TB, PH, TOPK]),
                                    ALU.mult).then_inc(r_triple, 1)
    loads[0] += 16
    stage.close()
    main.close()

    peer = ExitStack()
    NB = 4
    NT, HOT = 4, 4
    NPOOL = 3
    TD = TB - 1
    G = sb(peer, "gates", [P, NKEYS, P])
    xs_hi = sb(peer, "xs_hi", [P, DC, T], F32R)
    xs_lo = sb(peer, "xs_lo", [P, DC, T], F32R)
    raw = sb(peer, "raw", [P, 4, D])
    u_raw = lambda n: raw[:, n % 2].rearrange("p (c i) -> p c i", i=P)
    v_raw = lambda n: raw[:, 2 + n % 2]
    u_loaded = [sem(f"u_loaded{k}") for k in range(2)]
    v_loaded = [sem(f"v_loaded{k}") for k in range(2)]
    g_loaded = [sem(f"g_loaded{k}") for k in range(2)]
    gate_stored = [sem(f"gate_stored{c}") for c in range(TD)]
    hot_ready, hot_used, g_read = sem("hot_ready"), sem("hot_used"), sem("g_read")
    gated_pool, gated_act = sem("gated_pool"), sem("gated_act")
    u_hi_done, u_lo_done, v_hi_done, v_lo_done = (sem(x) for x in ("u_hi_done", "u_lo_done", "v_hi_done", "v_lo_done"))
    u_done, gelu_done, w_mult, w_hi_done, w_ready = (
        sem(x) for x in ("u_done", "gelu_done", "w_mult", "w_hi_done", "w_ready"))
    y_full, y_added, y_loaded = sem("y_full"), sem("y_added"), sem("y_loaded")
    x_loaded = sem("x_loaded")
    f_g, f_ss, f_sq = sem("f_g"), sem("f_ss"), sem("f_sq")
    BODIES = NKEYS // NB
    BATCHES = P // NT
    TBODIES = BATCHES // HOT

    def load_u(sp, i, k):
        sp.dma_start(u_raw(k), A["u_tiles"][bass.ds(i * NB + k, 1)].rearrange("o p c i -> (o p) c i")
                     ).then_inc(u_loaded[k % 2], 16)

    def load_v(sp, i, k):
        sp.dma_start(v_raw(k), A["v"][:, bass.ds(i * NB + k, 1), :].rearrange("i o d -> i (o d)")
                     ).then_inc(v_loaded[k % 2], 16)

    stage = ExitStack()
    G_other = sb(stage, "gates_other", [P, NKEYS, P])
    hot = sb(stage, "hot", [P, HOT, 2, NT, P])
    gates = [G if c % 2 == TD % 2 else G_other for c in range(TB)]
    batch = lambda c, i, b: i * HOT + (c * BATCHES + b)
    token = lambda c, i, b: i * (HOT * NT) + (c * P + b * NT)
    with nc.Block() as block:
        @block.sync
        def _(sp):
            sp.dma_start(xs_hi[:].bitcast(F32), xf_scratch[0]).then_inc(x_loaded, 16)
            sp.dma_start(xs_lo[:].bitcast(F32), xf_scratch[1]).then_inc(x_loaded, 16)
            for k in range(2):
                load_u(sp, 0, k)
                load_v(sp, 0, k)
            for c in range(TD):
                sp.wait_ge(g_read, (c + 1) * BATCHES)
                sp.dma_start(gate_scratch[c], gates[c][:]).then_inc(gate_stored[c], 16)
            for c in range(TD):
                sp.wait_ge(gate_stored[c], 16)
            sp.wait_ge(x_loaded, 32)

        @block.vector
        def _(dve):
            def body(c, i, first=False):
                for b in range(HOT):
                    if not first:
                        dve.wait_ge(hot_used, batch(c, i, b) + (1 - HOT))
                    nc.vector.tensor_tensor(
                        hot[:, b], iota.unsqueeze(1).unsqueeze(1).to_broadcast([P, 2, NT, P]),
                        slot_t[:, 0:2, bass.ds(token(c, i, b), NT)].unsqueeze(3).to_broadcast([P, 2, NT, P]),
                        ALU.is_equal).then_inc(hot_ready, 1)
            for c in range(TB):
                body(c, 0, first=(c == 0))
                with dve.Fori(1, TBODIES) as i:
                    body(c, i)

        @block.gpsimd
        def _(pool):
            for c in range(TB):
                with pool.Fori(0, TBODIES) as i:
                    for b in range(HOT):
                        pool.wait_ge(hot_ready, batch(c, i, b) + 1)
                        o = hot[:, b, 1, 0:NPOOL, :]
                        nc.gpsimd.tensor_tensor(o, o, slot_t[:, 2, bass.ds(token(c, i, b), NPOOL)].unsqueeze(2).
                                                to_broadcast([P, NPOOL, P]), ALU.mult).then_inc(gated_pool, 1)

        @block.tensor
        def _(pe):
            def body(c, i, first=False):
                for b in range(HOT):
                    n = batch(c, i, b)
                    if not first:
                        pe.wait_ge(g_read, n + (1 - HOT))
                    pe.wait_ge(gated_pool, n + 1)
                    pe.wait_ge(gated_act, n + 1)
                    for k in range(NT):
                        last = nc.tensor.matmul(psum[b][:, k * P:(k + 1) * P], hot[:, b, 0, k, :], hot[:, b, 1, k, :],
                                                start=True, stop=True)
                    last.then_inc(hot_used, 1)
            for c in range(TB):
                body(c, 0, first=(c == 0))
                with pe.Fori(1, TBODIES) as i:
                    body(c, i)

        @block.scalar
        def _(act):
            def gate(c, i, b):
                act.wait_ge(hot_ready, batch(c, i, b) + 1)
                for k in range(NPOOL, NT):
                    o = hot[:, b % HOT, 1, k, :]
                    last = nc.scalar.activation(o, o, ACT.Identity, scale=slot_t[:, 2, bass.ds(token(c, i, b) + k, 1)])
                last.then_inc(gated_act, 1)

            def read(c, i, b):
                act.wait_ge(hot_used, batch(c, i, b) + 1)
                nc.scalar.activation(gates[c][:, :, bass.ds(i * (HOT * NT) + b * NT, NT)],
                                     psum[b][:].rearrange("p (t j) -> p j t", t=NT),
                                     ACT.Identity).then_inc(g_read, 1)

            def body(c, i, last=False):
                for b in range(HOT):
                    if not (last and b == HOT - 1):
                        gate(c, i, b + 1)
                    read(c, i, b)
            gate(0, 0, 0)
            for c in range(TB):
                if c >= 2:
                    act.wait_ge(gate_stored[c - 2], 16)
                with act.Fori(0, TBODIES - (c == TB - 1)) as i:
                    body(c, i)
            body(TB - 1, TBODIES - 1, last=True)
    stage.close()

    stage = ExitStack()
    YB = 4
    u_hi = sb(stage, "u_hi", [P, 2, DC, P], F32R)
    u_lo = sb(stage, "u_lo", [P, 2, DC, P], F32R)
    v_hi = sb(stage, "v_hi", [P, 4, D], F32R)
    v_lo = sb(stage, "v_lo", [P, 4, D], F32R)
    g_in = sb(stage, "g_in", [P, 2, TD, P])
    gel = sb(stage, "gel", [P, 2, T])
    w_hi = sb(stage, "w_hi", [P, 4, T], F32R)
    w_lo = sb(stage, "w_lo", [P, 4, T], F32R)
    Y = sb(stage, "y", [P, TB, D])
    gf, sq = raw[:, 0], raw[:, 1]
    st = gel[:, 0, 0:5 * TB].rearrange("p (a b) -> p a b", b=TB)
    with nc.Block() as block:
        @block.sync
        def _(sp):
            def load_g(i, k, first=False):
                if not first:
                    sp.wait_ge(w_ready, i * NB + (k - 1))
                sp.dma_start(g_in[:, k % 2], gate_scratch[:, :, bass.ds(i * NB + k, 1), :].rearrange(
                    "c p o t -> p c (o t)")).then_inc(g_loaded[k % 2], 16)

            def next_u(i, k):
                sp.wait_ge(u_lo_done, i * NB + (k - 1))
                load_u(sp, i, k)

            def next_v(i, k):
                sp.wait_ge(v_lo_done, i * NB + (k - 1))
                load_v(sp, i, k)
            load_g(0, 0, True)
            load_g(0, 1, True)
            sp.dma_start(Y[:], h_scratch).then_inc(y_loaded, 16)
            for k in range(2, NB):
                next_u(0, k)
            for k in range(2):
                next_u(1, k)
                next_v(0, k + 2)
                load_g(0, k + 2)
            for k in range(2, NB):
                next_u(1, k)
                next_v(1, k - 2)
                load_g(1, k - 2)
            with sp.Fori(2, BODIES) as i:
                for k in range(NB):
                    next_u(i, k)
                    next_v(i, k - 2)
                    load_g(i, k - 2)
            for k in range(2, NB):
                next_v(BODIES - 1, k)
                load_g(BODIES - 1, k)
            sp.wait_ge(u_lo_done, NKEYS)
            sp.dma_start(gf, A["final_g"].partition_broadcast(P)).then_inc(f_g, 16)

        @block.tensor
        def _(pe):
            def up(i, k, first=False):
                pe.wait_ge(u_lo_done, i * NB + (k + 1))
                if not first:
                    pe.wait_ge(gelu_done, i * NB + (k - 1))
                bank = psum[k % 2][:]
                for c in range(DC):
                    nc.tensor.matmul(bank, u_lo[:, k % 2, c, :], xs_hi[:, c, :], start=(c == 0), stop=False)
                    nc.tensor.matmul(bank, u_hi[:, k % 2, c, :], xs_lo[:, c, :], start=False, stop=False)
                    last = nc.tensor.matmul(bank, u_hi[:, k % 2, c, :], xs_hi[:, c, :], start=False,
                                            stop=(c == DC - 1))
                last.then_inc(u_done, 1)

            def down(i, k, first=False):
                if k % 2 == 0:
                    pe.wait_ge(v_lo_done, i * NB + (k + 2))
                    pe.wait_ge(w_ready, i * NB + (k + 2))
                for j in range(YB):
                    t, d = 2 * (k % 2) + j // 2, j % 2
                    tk, f = slice(t * P, (t + 1) * P), slice(512 * d, 512 * d + 512)
                    y = psum[YB + j][:]
                    if not first:
                        pe.wait_ge(y_added, i * (NB * YB) + (YB * (k - 1) + j + 1))
                    for e in (k - k % 2, k - k % 2 + 1):
                        nc.tensor.matmul(y, w_lo[:, e, tk], v_hi[:, e, f], start=(e % 2 == 0), stop=False)
                        nc.tensor.matmul(y, w_hi[:, e, tk], v_lo[:, e, f], start=False, stop=False)
                        last = nc.tensor.matmul(y, w_hi[:, e, tk], v_hi[:, e, f], start=False, stop=(e % 2 == 1))
                    last.then_inc(y_full, 1)
            up(0, 0, True)
            up(0, 1, True)
            for k in range(NB):
                up(0, k + 2)
                down(0, k, first=(k == 0))
            with pe.Fori(1, BODIES - 1) as i:
                for k in range(NB):
                    up(i, k + 2)
                    down(i, k)
            for k in range(NB):
                if k + 2 < NB:
                    up(BODIES - 1, k + 2)
                down(BODIES - 1, k)

        @block.scalar
        def _(act):
            def u_part(i, k, first=False):
                act.wait_ge(u_loaded[k % 2], i * (NB // 2 * 16) + 16 * (k // 2 + 1))
                if not first:
                    act.wait_ge(u_done, i * NB + (k - 1))
                nc.scalar.activation(u_hi[:, k % 2], u_raw(k), ACT.Identity).then_inc(u_hi_done, 1)

            def v_part(i, k, first=False):
                act.wait_ge(v_loaded[k % 2], i * (NB // 2 * 16) + 16 * (k // 2 + 1))
                if not first:
                    act.wait_ge(y_full, i * (NB * YB) + YB * (k - k % 2 - 2))
                nc.scalar.activation(v_hi[:, k % 4], v_raw(k), ACT.Identity).then_inc(v_hi_done, 1)

            def gelu(i, k, first=False):
                act.wait_ge(u_done, i * NB + (k + 1))
                if not first:
                    act.wait_ge(w_ready, i * NB + (k - 1))
                nc.scalar.activation(gel[:, k % 2, :], psum[k % 2][:], ACT.Gelu_apprx_tanh).then_inc(gelu_done, 1)
            u_part(0, 0, True)
            u_part(0, 1, True)
            v_part(0, 0, True)
            v_part(0, 1, True)
            for k in range(2):
                gelu(0, k, True)
                u_part(0, k + 2)
            for k in range(NB):
                gelu(0, k + 2)
                u_part(0, k + 4)
                v_part(0, k + 2, first=(k < 2))
            with act.Fori(1, BODIES - 1) as i:
                for k in range(NB):
                    gelu(i, k + 2)
                    u_part(i, k + 4)
                    v_part(i, k + 2)
            for k in range(2):
                gelu(BODIES - 1, k + 2)
                v_part(BODIES - 1, k + 2)
            act.wait_ge(y_added, NKEYS * YB - YB)
            act.wait_ge(w_ready, NKEYS)
            for t in range(2):
                nc.scalar.activation(sq, Y[:, t, :], ACT.Square, accum_out=st[:, 0, t:t + 1]).then_inc(f_ss, 1)
                act.wait_ge(f_ss, t + 1)

        @block.vector
        def _(dve):
            def u_part(i, k):
                dve.wait_ge(u_hi_done, i * NB + (k + 1))
                nc.vector.tensor_tensor(u_lo[:, k % 2], u_raw(k), u_hi[:, k % 2].bitcast(F32),
                                        ALU.subtract).then_inc(u_lo_done, 1)

            def v_part(i, k):
                dve.wait_ge(v_hi_done, i * NB + (k + 1))
                nc.vector.tensor_tensor(v_lo[:, k % 4], v_raw(k), v_hi[:, k % 4].bitcast(F32),
                                        ALU.subtract).then_inc(v_lo_done, 1)

            def weights(i, k, first=False):
                n = lambda d: i * NB + (k + 1 - d)
                wf = gel[:, k % 2, :]
                dve.wait_ge(gelu_done, n(0))
                if not first:
                    dve.wait_ge(y_full, i * (NB * YB) + YB * (k - k % 2 - 2))
                nc.vector.tensor_tensor(wf[:, TD * P:], wf[:, TD * P:], G[:, bass.ds(i * NB + k, 1), :].
                                        rearrange("p o t -> p (o t)"), ALU.mult).then_inc(w_mult, 1)
                dve.wait_ge(g_loaded[k % 2], i * (NB // 2 * 16) + 16 * (k // 2 + 1))
                nc.vector.tensor_tensor(wf[:, 0:TD * P], wf[:, 0:TD * P], g_in[:, k % 2].rearrange(
                    "p c t -> p (c t)"), ALU.mult).then_inc(w_mult, 1)
                dve.wait_ge(w_mult, i * (2 * NB) + 2 * (k + 1))
                nc.vector.tensor_copy(w_hi[:, k % 4, :], wf).then_inc(w_hi_done, 1)
                dve.wait_ge(w_hi_done, n(0))
                nc.vector.tensor_tensor(w_lo[:, k % 4, :], wf, w_hi[:, k % 4, :].bitcast(F32),
                                        ALU.subtract).then_inc(w_ready, 1)

            def add(i, k, j, first=False):
                t, d = 2 * (k % 2) + j // 2, j % 2
                dve.wait_ge(y_full, i * (NB * YB) + (YB * k + j + 1))
                if not first:
                    dve.wait_ge(y_added, i * (NB * YB) + (YB * (k - 2) + j + 1))
                o = Y[:, t, 512 * d:512 * d + 512]
                nc.vector.tensor_tensor(o, o, psum[YB + j][:], ALU.add).then_inc(y_added, 1)
            u_part(0, 0)
            u_part(0, 1)
            v_part(0, 0)
            v_part(0, 1)
            for k in range(2):
                weights(0, k, True)
                u_part(0, k + 2)
            dve.wait_ge(y_loaded, 16)
            for k in range(NB):
                weights(0, k + 2, first=(k < 2))
                add(0, k, 0, first=(k < 2))
                u_part(0, k + 4)
                add(0, k, 1, first=(k < 2))
                v_part(0, k + 2)
                add(0, k, 2, first=(k < 2))
                add(0, k, 3, first=(k < 2))
            with dve.Fori(1, BODIES - 1) as i:
                for k in range(NB):
                    weights(i, k + 2)
                    add(i, k, 0)
                    u_part(i, k + 4)
                    add(i, k, 1)
                    v_part(i, k + 2)
                    add(i, k, 2)
                    add(i, k, 3)
            for k in range(NB):
                if k < 2:
                    weights(BODIES - 1, k + 2)
                    v_part(BODIES - 1, k + 2)
                for j in range(YB):
                    add(BODIES - 1, k, j)
    with nc.Block() as block:
        @block.sync
        def _(sp):
            for t in range(TB):
                sp.wait_ge(f_sq, t + 1)
                sp.dma_start(out[:, t, :], Y[:, t, :]).then_inc(stored, 16)
            sp.wait_ge(stored, 16 * (TB + 3))

        @block.vector
        def _(dve):
            dve.wait_ge(f_ss, TB)
            nc.vector.tensor_scalar(st[:, 1, :], st[:, 0, :], 1.0 / D, EPS, ALU.mult, ALU.add).then_inc(f_ss, 1)
            dve.wait_ge(f_ss, TB + 2)
            link(dve, "dve", nc.vector.reciprocal(st[:, 2, :], st[:, 2, :]))
            link(dve, "dve", nc.vector.tensor_tensor(st[:, 3, :], st[:, 2, :], st[:, 2, :], ALU.mult))
            link(dve, "dve", nc.vector.tensor_tensor(st[:, 3, :], st[:, 3, :], st[:, 1, :], ALU.mult))
            link(dve, "dve", nc.vector.tensor_scalar(st[:, 3, :], st[:, 3, :], -0.5, 1.5, ALU.mult, ALU.add))
            link(dve, "dve", nc.vector.tensor_tensor(st[:, 4, :], st[:, 3, :], st[:, 2, :], ALU.mult))
            dve.wait_ge(f_g, 16)
            for t in range(TB):
                nc.vector.scalar_tensor_tensor(out=Y[:, t, :], in0=Y[:, t, :], scalar=st[:, 4, t:t + 1], in1=gf,
                                               op0=ALU.mult, op1=ALU.mult).then_inc(f_sq, 1)

        @block.scalar
        def _(act):
            for t in range(2, TB):
                nc.scalar.activation(sq, Y[:, t, :], ACT.Square, accum_out=st[:, 0, t:t + 1]).then_inc(f_ss, 1)
                act.wait_ge(f_ss, t + 1)
            act.wait_ge(f_ss, TB + 1)
            nc.scalar.activation(st[:, 2, :], st[:, 1, :], ACT.Sqrt).then_inc(f_ss, 1)
    stage.close()
    peer.close()
    top.close()


def _lay_out(a):
    f = {k: np.asarray(v) for k, v in a.items()}
    for k in f:
        if k not in ("x", "mem", "final_norm_g"):
            f[k] = f[k][0]
    w_in = f["w_in"]
    c1 = 2 * GH * GDK + GH * GDV
    c3 = c1 + GH * GDV
    dense = np.concatenate([w_in[:, :c3], w_in[:, c3 + LOWRANK:], f["w_out"], f["w_xkv"], f["w_xq"], f["w_xo"],
                            f["peer_w_q"]], axis=1)
    cols = lambda v: v.reshape(-1, P).T
    conv = f["gla_conv_w"].reshape(CONV, CONV_BLOCKS, P).transpose(2, 1, 0).reshape(P, -1)
    vec = np.concatenate([cols(f["mix_norm_g"]), cols(f["xattn_norm_g"]), cols(f["mem_norm_g"]),
                          cols(f["ffn_norm_g"]), conv, cols(f["gla_gate_b"]), cols(f["gla_out_norm_g"]),
                          cols(f["sb_out_norm_g"])], axis=1)
    r = np.arange(P)
    const = np.zeros((P, NCONST), np.float32)
    const[:, C_ID:C_ID + P] = np.eye(P)
    const[:, C_ONES:C_ONES + P] = 1
    const[:, C_TRI:C_TRI + P] = r[:, None] >= r[None, :]
    const[:, C_IOTA16:C_IOTA16 + TOPK] = np.arange(TOPK)[None, :]
    masks = [np.eye(P, dtype=bool)]
    key, query = r[:, None], r[None, :]
    for b in LEVELS:
        masks.append((key // (2 * b) == query // (2 * b)) & (key % (2 * b) < b) & (query % (2 * b) >= b))
    out = {
        "x": f["x"].reshape(TB, P, D).transpose(1, 0, 2),
        "mem": f["mem"].reshape(MB, P, D).transpose(1, 0, 2),
        "w_tiles": dense.reshape(DC, P, 4 * NQUADS, P).transpose(1, 2, 0, 3),
        "w_low": w_in[:, c3:c3 + LOWRANK].reshape(DC, P, LOWRANK).transpose(1, 0, 2),
        "gate_w": f["gla_gate_w"],
        "vec": vec,
        "const": const,
        "iota": np.broadcast_to(r.astype(np.float32), (P, P)),
        "masks": np.stack(masks, axis=1).astype(np.uint32),
        "keys": f["peer_sub_keys"].reshape(HP, NKEYS, P).transpose(2, 0, 1),
        "u_tiles": f["peer_u"].reshape(NKEYS, NKEYS, DC, P).transpose(1, 3, 2, 0),
        "v": f["peer_v"].reshape(NKEYS, NKEYS, D),
        "final_g": f["final_norm_g"],
    }
    return {k: np.ascontiguousarray(v) for k, v in out.items()}


def kernel(**inputs):
    import concourse.bacc as bacc
    from concourse.bass_utils import run_bass_kernel_spmd

    arrays = _lay_out(inputs)
    nc = bacc.Bacc("TRN2", target_bir_lowering=False, num_devices=1)
    A = {k: nc.dram_tensor("in_" + k, v.shape, mybir.dt.from_np(v.dtype), kind="ExternalInput").ap()
         for k, v in arrays.items()}
    out = nc.dram_tensor("out_0", [P, TB, D], F32, kind="ExternalOutput").ap()
    layer(nc, A, out)
    r = run_bass_kernel_spmd(nc, [{"in_" + k: v for k, v in arrays.items()}], core_ids=[0])
    return r.results[0]["out_0"].transpose(1, 0, 2).reshape(1, T, D)
```
